# Optimizing a Trainium2 kernel written in Bass

```python
import math
import jax, jax.numpy as jnp
from jax import lax
import numpy as np

D_MODEL = 1024
BATCH = 1
SEQ = 1024
DEPTH = 1

N_META = 16
SSD_HEAD_DIM = 64
SSD_INNER = D_MODEL
SSD_HEADS = SSD_INNER // SSD_HEAD_DIM
SSD_GROUPS = 2
SSD_STATE = 128
SSD_CONV = 4
CHUNK = 128
SB_HEAD_DIM = 64
SB_WIDTH = D_MODEL
SB_HEADS = SB_WIDTH // SB_HEAD_DIM
Q_BLOCK = 128
MIX_WIDTH = SSD_INNER + SB_WIDTH
D_FF = 256 * ((8 * D_MODEL // 3 + 255) // 256)
FFN_CONV = 3
EPS = 1e-6

XBC_WIDTH = SSD_INNER + 2 * SSD_GROUPS * SSD_STATE
OFF_Z = 0
OFF_XBC = OFF_Z + SSD_INNER
OFF_DT = OFF_XBC + XBC_WIDTH
OFF_Q = OFF_DT + SSD_HEADS
OFF_K = OFF_Q + SB_WIDTH
OFF_V = OFF_K + SB_WIDTH
IN_COLS = OFF_V + SB_WIDTH


def rms_norm(x, g):
    x32 = x.astype(jnp.float32)
    y = x32 * lax.rsqrt(jnp.mean(x32 * x32, axis=-1, keepdims=True) + EPS)
    return (y * g.astype(jnp.float32)).astype(x.dtype)

def causal_dwconv(x, w, b):
    K = w.shape[0]
    L = x.shape[1]
    xp = jnp.pad(x, ((0, 0), (K - 1, 0), (0, 0)))
    y = b
    for k in range(K):
        y = y + xp[:, k:k + L] * w[k]
    return y

def ssd_mixer(z, xbc, dt_raw, conv_w, conv_b, dt_bias, a_log, d_skip, norm_g):
    out_dtype = z.dtype
    Bsz, L, _ = xbc.shape
    H, P, G, N = SSD_HEADS, SSD_HEAD_DIM, SSD_GROUPS, SSD_STATE
    J = H // G
    f32 = jnp.float32
    xbc = jax.nn.silu(causal_dwconv(xbc, conv_w, conv_b)).astype(f32)
    xs = xbc[..., :SSD_INNER].reshape(Bsz, L, H, P)
    Bm = xbc[..., SSD_INNER:SSD_INNER + G * N].reshape(Bsz, L, G, N)
    Cm = xbc[..., SSD_INNER + G * N:].reshape(Bsz, L, G, N)
    dt = jax.nn.softplus(dt_raw.astype(f32) + dt_bias.astype(f32))
    A = -jnp.exp(a_log.astype(f32))

    pad = CHUNK - N_META
    Lp = L + pad
    nc = Lp // CHUNK

    def front_pad(t):
        return jnp.pad(t, ((0, 0), (pad, 0)) + ((0, 0),) * (t.ndim - 2))

    Xdt = front_pad(xs * dt[..., None]).reshape(Bsz, nc, CHUNK, G, J, P)
    Adt = front_pad(dt * A).reshape(Bsz, nc, CHUNK, G, J).transpose(0, 3, 4, 1, 2)
    Bc = front_pad(Bm).reshape(Bsz, nc, CHUNK, G, N)
    Cc = front_pad(Cm).reshape(Bsz, nc, CHUNK, G, N)

    Acs = jnp.cumsum(Adt, axis=-1)
    causal = jnp.tril(jnp.ones((CHUNK, CHUNK), dtype=bool))
    seg = Acs[..., :, None] - Acs[..., None, :]
    Ldec = jnp.where(causal, jnp.exp(jnp.where(causal, seg, 0.0)), 0.0)

    CB = jnp.einsum('bclgn,bcsgn->bgcls', Cc, Bc)
    y_diag = jnp.einsum('bgcls,bgjcls,bcsgjp->bclgjp', CB, Ldec, Xdt)

    decay_states = jnp.exp(Acs[..., -1:] - Acs)
    states = jnp.einsum('bclgn,bgjcl,bclgjp->bcgjpn', Bc, decay_states, Xdt)
    chunk_decay = jnp.exp(Acs[..., -1])

    def step(carry, inp):
        st, dec = inp
        return carry * dec[..., None, None] + st, carry

    init = jnp.zeros((Bsz, G, J, P, N), f32)
    _, prev = lax.scan(step, init, (states.transpose(1, 0, 2, 3, 4, 5),
                                    chunk_decay.transpose(3, 0, 1, 2)))
    prev = prev.transpose(1, 0, 2, 3, 4, 5)

    y_off = jnp.einsum('bclgn,bcgjpn,bgjcl->bclgjp', Cc, prev, jnp.exp(Acs))

    y = (y_diag + y_off).reshape(Bsz, Lp, H, P)[:, pad:]
    y = y + xs * d_skip.astype(f32)[:, None]
    y = y.reshape(Bsz, L, SSD_INNER) * jax.nn.silu(z.astype(f32))
    return rms_norm(y, norm_g).astype(out_dtype)

def stick_breaking_attention(q, k, v):
    out_dtype = q.dtype
    Bsz, L, H, D = q.shape
    f32 = jnp.float32
    scale = 1.0 / math.sqrt(D)
    pad = Q_BLOCK - N_META
    Lp = L + pad
    nb = Lp // Q_BLOCK
    padw = ((0, 0), (pad, 0), (0, 0), (0, 0))
    qp = jnp.pad(q.astype(f32), padw)
    kp = jnp.pad(k.astype(f32), padw)
    vp = jnp.pad(v.astype(f32), padw)
    qb = qp.reshape(Bsz, nb, Q_BLOCK, H, D).transpose(1, 0, 2, 3, 4)
    key_pos = jnp.arange(Lp)

    def block(args):
        i, qi = args
        q_pos = i * Q_BLOCK + jnp.arange(Q_BLOCK)
        valid = (key_pos[None, :] < q_pos[:, None]) & (key_pos[None, :] >= pad)
        zlog = jnp.einsum('bqhd,bkhd->bhqk', qi, kp) * scale
        log_beta = jax.nn.log_sigmoid(zlog)
        log_keep = jnp.where(valid, log_beta - zlog, 0.0)
        after = lax.cumsum(log_keep, axis=3, reverse=True) - log_keep
        w = jnp.where(valid, jnp.exp(log_beta + after), 0.0)
        return jnp.einsum('bhqk,bkhd->bqhd', w, vp)

    o = lax.map(block, (jnp.arange(nb), qb))
    o = o.transpose(1, 0, 2, 3, 4).reshape(Bsz, Lp, H, D)[:, pad:]
    return o.astype(out_dtype)

def first_inputs(seed: int = 0) -> dict:
    key = jax.random.key(seed)
    ks = jax.random.split(key, 20)
    f32 = jnp.float32

    def gain(k, n):
        return 1.0 + 0.05 * jax.random.normal(k, (DEPTH, n), f32)

    dt0 = jnp.exp(jax.random.uniform(ks[5], (DEPTH, SSD_HEADS), f32,
                                     math.log(1e-3), math.log(1e-1)))
    dt_bias = dt0 + jnp.log(-jnp.expm1(-dt0))
    return {
        "x": jax.random.normal(ks[0], (BATCH, SEQ, D_MODEL), f32),
        "meta_tokens": jax.random.normal(ks[1], (N_META, D_MODEL), f32),
        "mix_pre_g": gain(ks[2], D_MODEL),
        "w_in": jax.random.normal(ks[3], (DEPTH, D_MODEL, IN_COLS), f32) * D_MODEL ** -0.5,
        "ssd_conv_w": jax.random.normal(ks[4], (DEPTH, SSD_CONV, XBC_WIDTH), f32) * SSD_CONV ** -0.5,
        "ssd_conv_b": 0.01 * jax.random.normal(ks[6], (DEPTH, XBC_WIDTH), f32),
        "ssd_dt_bias": dt_bias,
        "ssd_a_log": jnp.log(jax.random.uniform(ks[7], (DEPTH, SSD_HEADS), f32, 1.0, 16.0)),
        "ssd_d": 1.0 + 0.1 * jax.random.normal(ks[8], (DEPTH, SSD_HEADS), f32),
        "ssd_norm_g": gain(ks[9], SSD_INNER),
        "sb_norm_g": gain(ks[10], SB_WIDTH),
        "w_out": jax.random.normal(ks[11], (DEPTH, MIX_WIDTH, D_MODEL), f32) * MIX_WIDTH ** -0.5,
        "mix_post_g": gain(ks[12], D_MODEL),
        "ffn_pre_g": gain(ks[13], D_MODEL),
        "w_up": jax.random.normal(ks[14], (DEPTH, D_MODEL, 2 * D_FF), f32) * D_MODEL ** -0.5,
        "ffn_conv_w": jax.random.normal(ks[15], (DEPTH, FFN_CONV, D_FF), f32) * FFN_CONV ** -0.5,
        "ffn_conv_b": 0.01 * jax.random.normal(ks[16], (DEPTH, D_FF), f32),
        "w_down": jax.random.normal(ks[17], (DEPTH, D_FF, D_MODEL), f32) * D_FF ** -0.5,
        "ffn_post_g": gain(ks[18], D_MODEL),
    }

def first_block(x, meta_tokens, mix_pre_g, w_in, ssd_conv_w, ssd_conv_b, ssd_dt_bias,
              ssd_a_log, ssd_d, ssd_norm_g, sb_norm_g, w_out, mix_post_g, ffn_pre_g,
              w_up, ffn_conv_w, ffn_conv_b, w_down, ffn_post_g):
    Bsz = x.shape[0]
    meta = jnp.broadcast_to(meta_tokens.astype(x.dtype)[None], (Bsz, N_META, x.shape[-1]))
    h = jnp.concatenate([meta, x], axis=1)
    L = h.shape[1]
    for l in range(DEPTH):
        xn = rms_norm(h, mix_pre_g[l])
        proj = xn @ w_in[l]
        z = proj[..., OFF_Z:OFF_XBC]
        xbc = proj[..., OFF_XBC:OFF_DT]
        dt_raw = proj[..., OFF_DT:OFF_Q]
        q = proj[..., OFF_Q:OFF_K].reshape(Bsz, L, SB_HEADS, SB_HEAD_DIM)
        k = proj[..., OFF_K:OFF_V].reshape(Bsz, L, SB_HEADS, SB_HEAD_DIM)
        v = proj[..., OFF_V:IN_COLS].reshape(Bsz, L, SB_HEADS, SB_HEAD_DIM)
        y_ssd = ssd_mixer(z, xbc, dt_raw, ssd_conv_w[l], ssd_conv_b[l], ssd_dt_bias[l],
                          ssd_a_log[l], ssd_d[l], ssd_norm_g[l])
        y_sb = rms_norm(stick_breaking_attention(q, k, v).reshape(Bsz, L, SB_WIDTH), sb_norm_g[l])
        mix = jnp.concatenate([y_ssd, y_sb], axis=-1) @ w_out[l]
        h = h + rms_norm(mix, mix_post_g[l])
        xn = rms_norm(h, ffn_pre_g[l])
        gu = xn @ w_up[l]
        g = causal_dwconv(gu[..., :D_FF], ffn_conv_w[l], ffn_conv_b[l])
        f = (jax.nn.gelu(g, approximate=True) * gu[..., D_FF:]) @ w_down[l]
        h = h + rms_norm(f, ffn_post_g[l])
    return h[:, N_META:]


D_MIX = D_MODEL
NORM_EPS = 1e-6

GLA_HEADS = 4
GLA_DK = 64
GLA_DV = 128
GLA_KW = GLA_HEADS * GLA_DK
GLA_VW = GLA_HEADS * GLA_DV
GLA_GATE_RANK = 16
GLA_TAU = 16.0
GLA_CHUNK = 64

RWKV_HEAD = 64
RWKV_W = D_MIX - GLA_VW
RWKV_HEADS = RWKV_W // RWKV_HEAD
RWKV_DECAY_RANK = 64
RWKV_A_RANK = 64
RWKV_GN_EPS = 64e-5

GLA_SPLITS = (GLA_KW, GLA_KW, GLA_VW, GLA_GATE_RANK, GLA_VW)
RWKV_SHIFT_SPLITS = (RWKV_W, RWKV_W, RWKV_W, RWKV_DECAY_RANK, RWKV_A_RANK)
GLA_IN = sum(GLA_SPLITS)
RWKV_SHIFT_W = sum(RWKV_SHIFT_SPLITS)
RWKV_IN = RWKV_SHIFT_W + RWKV_W
IN_WIDTH = GLA_IN + RWKV_IN


def _split(t, sizes):
    idx = np.cumsum(np.array(sizes))[:-1].tolist()
    return jnp.split(t, idx, axis=-1)

def _rmsnorm(x, w):
    xf = x.astype(jnp.float32)
    y = xf * lax.rsqrt(jnp.mean(xf * xf, axis=-1, keepdims=True) + NORM_EPS)
    return (y * w.astype(jnp.float32)).astype(x.dtype)

def _gla_chunked(q, k, v, log_a):
    B, T, H, DK = q.shape
    DV = v.shape[-1]
    C = GLA_CHUNK
    N = T // C

    def to_chunks(t):
        return t.reshape(B, N, C, H, t.shape[-1]).transpose(1, 0, 3, 2, 4)

    qc, kc, vc, gc = to_chunks(q), to_chunks(k), to_chunks(v), to_chunks(log_a)
    b = jnp.cumsum(gc, axis=3)
    b_last = b[:, :, :, -1:, :]
    q_in = qc * jnp.exp(b)
    k_in = kc * jnp.exp(-b)
    k_st = kc * jnp.exp(b_last - b)
    causal = jnp.tril(jnp.ones((C, C), dtype=bool))
    scores = jnp.einsum('nbhid,nbhjd->nbhij', q_in, k_in)
    scores = jnp.where(causal, scores, 0.0)
    o_intra = jnp.einsum('nbhij,nbhjv->nbhiv', scores, vc)
    d_state = jnp.einsum('nbhjd,nbhjv->nbhdv', k_st, vc)
    chunk_decay = jnp.exp(b_last[:, :, :, 0, :])

    def step(S, inp):
        dS, dec = inp
        return S * dec[..., None] + dS, S

    S0 = jnp.zeros((B, H, DK, DV), jnp.float32)
    _, S_prev = lax.scan(step, S0, (d_state, chunk_decay))
    o_inter = jnp.einsum('nbhid,nbhdv->nbhiv', q_in, S_prev)
    o = o_intra + o_inter
    return o.transpose(1, 0, 3, 2, 4).reshape(B, T, H, DV)

def _rwkv7_scan(r, decay, k, v, kk, a):
    B, T, H, N = r.shape

    def step(S, inp):
        r_t, w_t, k_t, v_t, kk_t, a_t = inp
        sa = jnp.einsum('bhvk,bhk->bhv', S, -kk_t)
        S = (S * w_t[:, :, None, :]
             + sa[..., None] * (kk_t * a_t)[:, :, None, :]
             + v_t[..., None] * k_t[:, :, None, :])
        y = jnp.einsum('bhvk,bhk->bhv', S, r_t)
        return S, y

    xs = tuple(t.transpose(1, 0, 2, 3) for t in (r, decay, k, v, kk, a))
    S0 = jnp.zeros((B, H, N, N), jnp.float32)
    _, y = lax.scan(step, S0, xs)
    return y.transpose(1, 0, 2, 3)

def _hybrid_layer(x, norm_w, w_in, gla_gate_up, gla_gate_bias, gla_norm_w,
                  rwkv_mu, rwkv_w0, rwkv_w_up, rwkv_a0, rwkv_a_up, rwkv_k_k,
                  rwkv_k_a, rwkv_r_k, rwkv_ln_w, rwkv_ln_b, w_out):
    B, T, _ = x.shape
    f32 = jnp.float32
    h = _rmsnorm(x, norm_w)
    u = (h @ w_in).astype(f32)
    gla_u, rwkv_u = u[..., :GLA_IN], u[..., GLA_IN:]

    gq, gk, gv, glr, gg = _split(gla_u, GLA_SPLITS)
    log_a = jax.nn.log_sigmoid(glr @ gla_gate_up.astype(f32) + gla_gate_bias.astype(f32)) / GLA_TAU
    q = gq.reshape(B, T, GLA_HEADS, GLA_DK) * (GLA_DK ** -0.5)
    k = gk.reshape(B, T, GLA_HEADS, GLA_DK)
    v = gv.reshape(B, T, GLA_HEADS, GLA_DV)
    o = _gla_chunked(q, k, v, log_a.reshape(B, T, GLA_HEADS, GLA_DK))
    o = o * lax.rsqrt(jnp.mean(o * o, axis=-1, keepdims=True) + NORM_EPS) * gla_norm_w.astype(f32)
    gla_out = o.reshape(B, T, GLA_VW) * jax.nn.silu(gg)

    shifted_cols = rwkv_u[..., :RWKV_SHIFT_W]
    rg = rwkv_u[..., RWKV_SHIFT_W:]
    prev = jnp.pad(shifted_cols, ((0, 0), (1, 0), (0, 0)))[:, :-1]
    mixed = shifted_cols + (prev - shifted_cols) * rwkv_mu.astype(f32)
    r, rk, rv, wl, al = _split(mixed, RWKV_SHIFT_SPLITS)
    w = -jax.nn.softplus(-(rwkv_w0.astype(f32) + jnp.tanh(wl) @ rwkv_w_up.astype(f32))) - 0.5
    decay = jnp.exp(-jnp.exp(w))
    a = jax.nn.sigmoid(rwkv_a0.astype(f32) + al @ rwkv_a_up.astype(f32))
    kk = (rk * rwkv_k_k.astype(f32)).reshape(B, T, RWKV_HEADS, RWKV_HEAD)
    kk = kk / jnp.maximum(jnp.linalg.norm(kk, axis=-1, keepdims=True), 1e-12)
    rk = rk * (1.0 + (a - 1.0) * rwkv_k_a.astype(f32))
    hs = (B, T, RWKV_HEADS, RWKV_HEAD)
    r_h, k_h, v_h = r.reshape(hs), rk.reshape(hs), rv.reshape(hs)
    y = _rwkv7_scan(r_h, decay.reshape(hs), k_h, v_h, kk, a.reshape(hs))
    mu = jnp.mean(y, axis=-1, keepdims=True)
    var = jnp.mean(jnp.square(y - mu), axis=-1, keepdims=True)
    y = ((y - mu) * lax.rsqrt(var + RWKV_GN_EPS)).reshape(B, T, RWKV_W)
    y = y * rwkv_ln_w.astype(f32) + rwkv_ln_b.astype(f32)
    bonus = jnp.sum(r_h * k_h * rwkv_r_k.astype(f32), axis=-1, keepdims=True) * v_h
    rwkv_out = (y + bonus.reshape(B, T, RWKV_W)) * jax.nn.silu(rg)

    merged = jnp.concatenate([gla_out, rwkv_out], axis=-1).astype(x.dtype)
    return x + merged @ w_out

def second_inputs(seed: int = 0) -> dict:
    key = jax.random.key(seed)
    ks = jax.random.split(key, 20)
    n = jax.random.normal
    L = DEPTH
    return {
        "x": n(ks[0], (BATCH, SEQ, D_MODEL), jnp.float32),
        "norm_w": 1.0 + 0.05 * n(ks[1], (L, D_MODEL), jnp.float32),
        "w_in": n(ks[2], (L, D_MODEL, IN_WIDTH), jnp.float32) * D_MODEL ** -0.5,
        "gla_gate_up": n(ks[3], (L, GLA_GATE_RANK, GLA_KW), jnp.float32) * GLA_GATE_RANK ** -0.5,
        "gla_gate_bias": 0.1 * n(ks[4], (L, GLA_KW), jnp.float32),
        "gla_norm_w": 1.0 + 0.05 * n(ks[5], (L, GLA_DV), jnp.float32),
        "rwkv_mu": jax.random.uniform(ks[6], (L, RWKV_SHIFT_W), jnp.float32),
        "rwkv_w0": jax.random.uniform(ks[7], (L, RWKV_W), jnp.float32, -6.0, -1.0),
        "rwkv_w_up": 0.1 * n(ks[8], (L, RWKV_DECAY_RANK, RWKV_W), jnp.float32),
        "rwkv_a0": 0.1 * n(ks[9], (L, RWKV_W), jnp.float32),
        "rwkv_a_up": 0.1 * n(ks[10], (L, RWKV_A_RANK, RWKV_W), jnp.float32),
        "rwkv_k_k": 0.85 + 0.05 * n(ks[11], (L, RWKV_W), jnp.float32),
        "rwkv_k_a": 1.0 + 0.05 * n(ks[12], (L, RWKV_W), jnp.float32),
        "rwkv_r_k": 0.1 * n(ks[13], (L, RWKV_HEADS, RWKV_HEAD), jnp.float32),
        "rwkv_ln_w": 1.0 + 0.05 * n(ks[14], (L, RWKV_W), jnp.float32),
        "rwkv_ln_b": 0.02 * n(ks[15], (L, RWKV_W), jnp.float32),
        "w_out": n(ks[16], (L, D_MIX, D_MODEL), jnp.float32) * D_MIX ** -0.5,
        "final_norm_w": 1.0 + 0.05 * n(ks[17], (D_MODEL,), jnp.float32),
    }

def second_block(x, norm_w, w_in, gla_gate_up, gla_gate_bias, gla_norm_w, rwkv_mu,
              rwkv_w0, rwkv_w_up, rwkv_a0, rwkv_a_up, rwkv_k_k, rwkv_k_a,
              rwkv_r_k, rwkv_ln_w, rwkv_ln_b, w_out, final_norm_w):
    for l in range(DEPTH):
        x = _hybrid_layer(x, norm_w[l], w_in[l], gla_gate_up[l], gla_gate_bias[l],
                          gla_norm_w[l], rwkv_mu[l], rwkv_w0[l], rwkv_w_up[l],
                          rwkv_a0[l], rwkv_a_up[l], rwkv_k_k[l], rwkv_k_a[l],
                          rwkv_r_k[l], rwkv_ln_w[l], rwkv_ln_b[l], w_out[l])
    return _rmsnorm(x, final_norm_w)


def setup_inputs(seed=0):
    out = dict(first_inputs(seed))
    for name, value in second_inputs(seed + 1).items():
        if name != "x":
            out[name + "_2"] = value
    return out


def reference(
    x, meta_tokens, mix_pre_g, w_in, ssd_conv_w, ssd_conv_b, ssd_dt_bias, ssd_a_log, ssd_d,
    ssd_norm_g, sb_norm_g, w_out, mix_post_g, ffn_pre_g, w_up, ffn_conv_w, ffn_conv_b, w_down,
    ffn_post_g, norm_w_2, w_in_2, gla_gate_up_2, gla_gate_bias_2, gla_norm_w_2, rwkv_mu_2,
    rwkv_w0_2, rwkv_w_up_2, rwkv_a0_2, rwkv_a_up_2, rwkv_k_k_2, rwkv_k_a_2, rwkv_r_k_2,
    rwkv_ln_w_2, rwkv_ln_b_2, w_out_2, final_norm_w_2,
):
    x = first_block(
        x, meta_tokens, mix_pre_g, w_in, ssd_conv_w, ssd_conv_b, ssd_dt_bias, ssd_a_log, ssd_d,
        ssd_norm_g, sb_norm_g, w_out, mix_post_g, ffn_pre_g, w_up, ffn_conv_w, ffn_conv_b,
        w_down, ffn_post_g,
    )
    return second_block(
        x, norm_w_2, w_in_2, gla_gate_up_2, gla_gate_bias_2, gla_norm_w_2, rwkv_mu_2, rwkv_w0_2,
        rwkv_w_up_2, rwkv_a0_2, rwkv_a_up_2, rwkv_k_k_2, rwkv_k_a_2, rwkv_r_k_2, rwkv_ln_w_2,
        rwkv_ln_b_2, w_out_2, final_norm_w_2,
    )


_drawn_inputs = setup_inputs


def setup_inputs(seed=0):
    import zlib

    import numpy as np

    out = dict(_drawn_inputs(seed))
    spreads = {}
    factors = {'ssd_conv_b': 5.757,
     'ffn_conv_b': 8.0,
     'gla_gate_bias_2': 5.15,
     'gla_norm_w_2': 4.399,
     'rwkv_w_up_2': 5.16,
     'rwkv_a0_2': 6.796,
     'rwkv_k_k_2': 15.944,
     'rwkv_k_a_2': 3.761,
     'rwkv_ln_w_2': 4.801,
     'rwkv_ln_b_2': 22.3}
    for name, (base, spread) in spreads.items():
        noise = np.random.default_rng([zlib.crc32(name.encode()), seed]).standard_normal(out[name].shape)
        drawn = base * np.exp(spread * noise) if base else spread * noise
        out[name] = __import__('jax').numpy.asarray(drawn.astype(out[name].dtype))
    for name, factor in factors.items():
        out[name] = (out[name] * factor).astype(out[name].dtype)
    return out
```

```python
from contextlib import ExitStack
import math

import concourse.bass as bass
from concourse import mybir

F32 = mybir.dt.float32
F16 = mybir.dt.float16
U32 = mybir.dt.uint32
ALU = mybir.AluOpType
ACT = mybir.ActivationFunctionType

P = 128
D = 1024
DB = D // P
SEQ, META = 1024, 16
T = META + SEQ
BANK = 512
NT = 3
TB = 348
TW = NT * TB
NCH = 9
TP = NCH * P
HD = 64
HEADS = 16
PAIRS = HEADS // 2
XBC_B = 12
CONV = 4
FFB = 22
EPS = 1e-6
RWKV_GN_EPS = 64e-5
WSCALE = 64.0
SLOTS = 2

_COLS = {}


def _col(name, n):
    _COLS[name] = (sum(v[1] for v in _COLS.values()), n)


for _name, _n in (("mix_pre_g", 8), ("ssd_norm_g", 8), ("sb_norm_g", 8), ("mix_post_g", 8), ("ffn_pre_g", 8),
                  ("ffn_post_g", 8), ("norm_w_2", 8), ("final_norm_w_2", 8), ("ssd_conv_w", XBC_B * CONV),
                  ("ssd_conv_b", XBC_B), ("ssd_d", PAIRS), ("ssd_dt_bias", 1), ("ssd_a_log", 1),
                  ("ffn_conv_w", FFB * 3), ("ffn_conv_b", FFB), ("gla_gate_bias_2", 2), ("gla_norm_w_2", 1),
                  ("rwkv_mu_2", 13), ("rwkv_w0_2", 4), ("rwkv_a0_2", 4), ("rwkv_k_k_2", 4), ("rwkv_k_a_2", 4),
                  ("rwkv_r_k_2", 4), ("rwkv_ln_w_2", 4), ("rwkv_ln_b_2", 4)):
    _col(_name, _n)
NCOL = sum(v[1] for v in _COLS.values())


class Names:
    pass


class Phase(ExitStack):

    cleared = []

    def __init__(self, nc):
        super().__init__()
        self.nc, self.used = nc, []
        self.callback(self.clear)

    def semaphore(self, name):
        self.used.append(self.nc.alloc_semaphore(name=name))
        return self.used[-1]

    def clear(self):
        for sem in Phase.cleared:
            self.nc.release_semaphore(sem)
        for sem in self.used:
            self.nc.gpsimd.sem_clear(sem)
        Phase.cleared[:] = self.used


class Chain:

    def __init__(self, eng, sem, base=0, alone=None):
        self.eng, self.sem, self.base, self.n, self.alone = eng, sem, base, 0, alone

    def __call__(self, ins):
        self.n += 1
        ins.then_inc(self.sem, 1)
        if self.alone:
            lone_wait(self.alone, self.eng, self.sem, self.base + self.n)
        else:
            self.eng.wait_ge(self.sem, self.base + self.n)


def lone_wait(S, pool, sem, value):
    pool.wait_ge(sem, value)
    pool.sem_inc(S.waited, 1)


def col(S, name, i=0, n=1):
    at, _ = _COLS[name]
    return S.cols[:, at + i:at + i + n]


def dcol(S, name, b, per=1, j=0):
    at, _ = _COLS[name]
    return S.cols[:, bass.ds(b * per + (at + j), 1)]


def blk(t, b):
    return t[:, bass.ds(b, 1), :].rearrange("p a n -> p (a n)")



def linear_buffers(nc, ctx, S, kb, tag):
    L = Names()
    L.kb = kb
    L.raw = ctx.enter_context(nc.sbuf_tensor(f"wraw_{tag}", [P, SLOTS, kb * P], F32))
    L.hi = ctx.enter_context(nc.sbuf_tensor(f"whi_{tag}", [P, SLOTS, kb * P], F16))
    L.lo = ctx.enter_context(nc.sbuf_tensor(f"wlo_{tag}", [P, SLOTS, kb * P], F16))
    L.landed = [ctx.semaphore(f"w_landed{s}_{tag}") for s in range(SLOTS)]
    L.cut = ctx.semaphore(f"w_cut_{tag}")
    L.step = ctx.semaphore(f"w_cut_step_{tag}")
    L.products = ctx.semaphore(f"products_{tag}")
    L.emptied = ctx.semaphore(f"psum_emptied_{tag}")
    return L


def stream_weights(sp, L, w, first, nb):
    for s in range(SLOTS):
        sp.dma_start(L.raw[:, s, :], w[first + s]).then_inc(L.landed[s], 16)
    if nb > SLOTS:
        with sp.Fori(0, nb // SLOTS - 1) as i:
            for s in range(SLOTS):
                sp.wait_ge(L.cut, i * SLOTS + (s + 1))
                sp.dma_start(L.raw[:, s, :], w[bass.ds(i * SLOTS + (first + SLOTS + s), 1)]
                             .rearrange("a p n -> p (a n)")).then_inc(L.landed[s], 16)


def cut_weights(nc, S, pool, L, nb):
    with pool.Fori(0, nb // SLOTS) as i:
        for s in range(SLOTS):
            step = Chain(pool, L.step, i * (2 * SLOTS) + 2 * s, alone=S)
            lone_wait(S, pool, L.landed[s], i * 16 + 16)
            step(nc.gpsimd.tensor_scalar(L.raw[:, s, :], L.raw[:, s, :], WSCALE, 1.0, ALU.mult, ALU.mult))
            lone_wait(S, pool, L.products, i * SLOTS + (s + 1))
            step(nc.gpsimd.tensor_copy(L.hi[:, s, :], L.raw[:, s, :]))
            nc.gpsimd.tensor_tensor(L.lo[:, s, :], L.raw[:, s, :], L.hi[:, s, :], ALU.subtract).then_inc(L.cut, 1)


def products(nc, pe, L, xs, banks, first, nb, nt=NT, tb=TB, t0=0, after=None):
    if first == 0:
        nc.tensor.sem_inc(L.products, SLOTS)
    with pe.Fori(first // SLOTS, nb // SLOTS) as i:
        for s in range(SLOTS):
            pe.wait_ge(L.cut, i * SLOTS + (s + 1))
            pe.wait_ge(L.emptied, i * SLOTS + (s + 1))
            for n in range(nt):
                for k in range(L.kb):
                    hi, lo = (w[:, s, k * P:(k + 1) * P] for w in (L.hi, L.lo))
                    xhi, xlo = (x[:, t0 + n * tb:t0 + (n + 1) * tb] for x in xs(k))
                    out = banks(s)[:, n, 0:tb]
                    nc.tensor.matmul(out, hi, xhi, start=(k == 0), stop=False)
                    nc.tensor.matmul(out, hi, xlo, start=False, stop=False)
                    last = nc.tensor.matmul(out, lo, xhi, start=False, stop=(k == L.kb - 1))
            last.then_inc(L.products, 1)
            if after:
                after(i, s)


def done(L, b):
    return b + (SLOTS + 1)


def normed(S):
    return lambda k: (S.xhi[:, k, :], S.xlo[:, k, :])


def psum_tn(S, s):
    return S.ps[:, NT * s:NT * s + NT, :]


def fm(ap, nt=NT):
    return ap.rearrange("p (n t) -> p n t", n=nt)



def norm_phase(nc, S, tag, src, g, kb, width, out, nt=NT, tb=TB):
    kind = out[0]
    with Phase(nc) as ctx:
        sq = ctx.enter_context(nc.sbuf_tensor(f"sq_{tag}", [P, 2, width], F32))
        rs = ctx.enter_context(nc.sbuf_tensor(f"rs_{tag}", [P, width], F32))
        y = ctx.enter_context(nc.sbuf_tensor(f"y_{tag}", [P, 2, width], F32))
        sem = lambda n: ctx.semaphore(f"{n}_{tag}")
        squared, summed, root, rsd, ysd, used, cut = (sem(n) for n in ("squared", "summed", "root", "rs_done", "ys", "y_used", "y_cut"))
        ps = S.ps[:, 0:nt, 0:tb]
        with nc.Block() as block:
            @block.scalar
            def _(act):
                for k in range(kb):
                    if k >= 2:
                        act.wait_ge(summed, k - 1)
                    nc.scalar.activation(sq[:, k % 2, :], src[:, k, 0:width], ACT.Square).then_inc(squared, 1)
                act.wait_ge(summed, kb)
                nc.scalar.activation(fm(rs[:, :], nt), ps, ACT.Sqrt, scale=1.0 / (kb * P),
                                     bias=S.eps[:, 0:1]).then_inc(root, 1)
                if kind == "cut":
                    for k in range(kb):
                        act.wait_ge(ysd, k + 1)
                        nc.scalar.activation(out[1][:, k, 0:width], y[:, k % 2, :], ACT.Copy).then_inc(used, 1)

            @block.tensor
            def _(pe):
                for k in range(kb):
                    pe.wait_ge(squared, k + 1)
                    for n in range(nt):
                        last = nc.tensor.matmul(S.ps[:, n, 0:tb], S.ones[:, :], sq[:, k % 2, n * tb:(n + 1) * tb],
                                                start=(k == 0), stop=(k == kb - 1))
                    last.then_inc(summed, 1)

            @block.vector
            def _(dve):
                dve.wait_ge(root, 1)
                nc.vector.reciprocal(rs[:, :], rs[:, :]).then_inc(rsd, 1)
                dve.wait_ge(rsd, 1)
                for k in range(kb):
                    if kind == "to":
                        nc.vector.scalar_tensor_tensor(out[1][:, k, 0:width], src[:, k, 0:width], col(S, g, k), rs[:, :],
                                                       ALU.mult, ALU.mult).then_inc(ysd, 1)
                        continue
                    if kind == "cut" and k >= 2:
                        dve.wait_ge(cut, k - 1)
                    nc.vector.scalar_tensor_tensor(y[:, k % 2, :], src[:, k, 0:width], col(S, g, k), rs[:, :],
                                                   ALU.mult, ALU.mult).then_inc(ysd, 1)
                    if kind == "add":
                        dve.wait_ge(ysd, k + 1)
                        nc.vector.tensor_tensor(out[1][:, k, 0:width], out[1][:, k, 0:width], y[:, k % 2, :], ALU.add).then_inc(used, 1)
                        dve.wait_ge(used, k + 1)

            if kind == "cut":
                @block.gpsimd
                def _(pool):
                    for k in range(kb):
                        pool.wait_ge(used, k + 1)
                        nc.gpsimd.tensor_tensor(out[2][:, k, 0:width], y[:, k % 2, :], out[1][:, k, 0:width],
                                                ALU.subtract).then_inc(cut, 1)



def constants_phase(nc, S, A):
    with Phase(nc) as ctx:
        sem = lambda n: ctx.semaphore(n)
        loaded, filled = sem("params_loaded"), sem("masks_filled")
        with nc.Block() as block:
            @block.sync
            def _(sp):
                sp.dma_start(S.cols[:, :], A["cols"]).then_inc(loaded, 16)
                sp.wait_ge(loaded, 16)

            @block.vector
            def _(dve):
                nc.vector.memset(S.ones[:, :], 1.0)
                nc.vector.memset(S.eps[:, :], EPS)
                nc.vector.memset(S.gn_eps[:, :], RWKV_GN_EPS)

            @block.gpsimd
            def _(pool):
                nc.gpsimd.memset(S.ident[:, :], 0.0).then_inc(filled, 1)
                nc.gpsimd.memset(S.upper[:, :], 1.0).then_inc(filled, 1)
                pool.wait_ge(filled, 2)
                nc.gpsimd.memset(S.strict[:, :], 1.0).then_inc(filled, 1)
                nc.gpsimd.memset(S.tri8[:, :], -8.0).then_inc(filled, 1)
                nc.gpsimd.memset(S.ones8[:, :], -8.0)
                pool.wait_ge(filled, 4)
                nc.gpsimd.affine_select(out=S.ident[:, :], in_=S.ident[:, :], compare_op=ALU.not_equal, fill=1.0,
                                        base=0, pattern=[[-1, P]], channel_multiplier=1)
                nc.gpsimd.affine_select(out=S.upper[:, :], in_=S.upper[:, :], compare_op=ALU.is_ge, fill=0.0,
                                        base=0, pattern=[[1, P]], channel_multiplier=-1)
                nc.gpsimd.affine_select(out=S.strict[:, :], in_=S.strict[:, :], compare_op=ALU.is_gt, fill=0.0,
                                        base=0, pattern=[[1, P]], channel_multiplier=-1)
                nc.gpsimd.affine_select(out=S.tri8[:, :], in_=S.tri8[:, :], compare_op=ALU.is_ge, fill=0.0,
                                        base=0, pattern=[[-1, P]], channel_multiplier=1)



def load_h_phase(nc, S, A, tag):
    with Phase(nc) as ctx:
        loaded = ctx.semaphore("h_loaded_" + tag)
        with nc.Block() as block:
            @block.vector
            def _(dve):
                nc.vector.memset(S.h[:, :, T:TW], 0.0)

            @block.sync
            def _(sp):
                sp.dma_start(S.h[:, :, 0:T], A["hT"]).then_inc(loaded, 16)
                sp.wait_ge(loaded, 16)


def xbc_phase(nc, S, A):
    with Phase(nc) as ctx:
        L = linear_buffers(nc, ctx, S, DB, "xbc")
        raw = ctx.enter_context(nc.sbuf_tensor("xbc_raw", [P, SLOTS, CONV - 1 + TW], F32))
        acc = ctx.enter_context(nc.sbuf_tensor("xbc_acc", [P, SLOTS, TW], F32))
        sem = lambda n: ctx.semaphore(n)
        zeroed, copied, conv, conv_step, silu = (sem(n) for n in ("conv_zeroed", "raw_copied", "conv_done", "conv_step", "silu_done"))
        with nc.Block() as block:
            @block.sync
            def _(sp):
                stream_weights(sp, L, A["w_in"], 8, XBC_B)

            @block.gpsimd
            def _(pool):
                cut_weights(nc, S, pool, L, XBC_B)
                nc.gpsimd.memset(S.xbc[:, :, TW:TP], 0.0)

            @block.tensor
            def _(pe):
                products(nc, pe, L, normed(S), lambda s: psum_tn(S, s), 0, XBC_B)

            @block.scalar
            def _(act):
                nc.scalar.sem_inc(L.emptied, SLOTS)
                nc.scalar.preload_act_table(ACT.Silu)
                act.wait_ge(zeroed, 1)
                with act.Fori(0, XBC_B // SLOTS) as i:
                    for s in range(SLOTS):
                        act.wait_ge(L.products, done(L, i * SLOTS + s))
                        act.wait_ge(conv, i * SLOTS + (s + 1))
                        nc.scalar.activation(fm(raw[:, s, CONV - 1:]), psum_tn(S, s)[:, :, 0:TB], ACT.Copy,
                                             scale=1.0 / WSCALE).then_inc(copied, 1)
                        act.wait_ge(copied, i * SLOTS + (s + 1))
                        nc.scalar.sem_inc(L.emptied, 1)
                        act.wait_ge(conv, i * SLOTS + (s + 1 + SLOTS))
                        nc.scalar.activation(S.xbc[:, bass.ds(i * SLOTS + s, 1), 0:TW].rearrange("p a n -> p (a n)"), acc[:, s, :],
                                             ACT.Silu).then_inc(silu, 1)

            @block.vector
            def _(dve):
                nc.vector.memset(raw[:, :, 0:CONV - 1], 0.0).then_inc(zeroed, 1)
                nc.vector.sem_inc(conv, SLOTS)
                nc.vector.sem_inc(silu, SLOTS)
                with dve.Fori(0, XBC_B // SLOTS) as i:
                    for s in range(SLOTS):
                        b = i * SLOTS + s
                        step = Chain(dve, conv_step, b * (CONV - 1))
                        dve.wait_ge(copied, i * SLOTS + (s + 1))
                        dve.wait_ge(silu, i * SLOTS + (s + 1))
                        step(nc.vector.tensor_scalar(acc[:, s, :], raw[:, s, 0:TW], dcol(S, "ssd_conv_w", b, CONV, 0),
                                                     dcol(S, "ssd_conv_b", b), ALU.mult, ALU.add))
                        for j in range(1, CONV):
                            ins = nc.vector.scalar_tensor_tensor(acc[:, s, :], raw[:, s, j:j + TW], dcol(S, "ssd_conv_w", b, CONV, j),
                                                                 acc[:, s, :], ALU.mult, ALU.add)
                            if j < CONV - 1:
                                step(ins)
                            else:
                                ins.then_inc(conv, 1)


def z_dt_phase(nc, S, A):
    with Phase(nc) as ctx:
        L = linear_buffers(nc, ctx, S, DB, "z")
        NB = 10
        sem = lambda n: ctx.semaphore(n)
        stored, dts, acts, padded = sem("z_stored"), sem("dt_steps"), sem("dt_acts"), sem("dt_padded")
        raw = ctx.enter_context(nc.sbuf_tensor("dt_raw", [HEADS, TW], F32))
        low = ctx.enter_context(nc.sbuf_tensor("dt_low", [HEADS, TW], F32))
        arate = ctx.enter_context(nc.sbuf_tensor("a_rate", [HEADS, 1], F32))
        with nc.Block() as block:
            @block.sync
            def _(sp):
                stream_weights(sp, L, A["w_z"], 0, NB)

            @block.gpsimd
            def _(pool):
                cut_weights(nc, S, pool, L, NB)
                nc.gpsimd.memset(S.z[:, :, TW:TP], 0.0)

            @block.tensor
            def _(pe):
                products(nc, pe, L, normed(S), lambda s: psum_tn(S, s), 0, NB)

            @block.scalar
            def _(act):
                nc.scalar.sem_inc(L.emptied, SLOTS)
                nc.scalar.preload_act_table(ACT.Silu)
                with act.Fori(0, 4) as i:
                    for s in range(SLOTS):
                        act.wait_ge(L.products, done(L, i * SLOTS + s))
                        nc.scalar.activation(fm(blk(S.z[:, :, 0:TW], i * SLOTS + s)), psum_tn(S, s)[:, :, 0:TB], ACT.Silu,
                                             scale=1.0 / WSCALE).then_inc(L.emptied, 1)
                act.wait_ge(dts, 2)
                nc.scalar.activation(low[:, :], low[:, :], ACT.Exp).then_inc(acts, 1)
                act.wait_ge(acts, 1)
                nc.scalar.activation(low[:, :], low[:, :], ACT.Ln, bias=1.0).then_inc(acts, 1)
                nc.scalar.activation(arate[:, :], col(S, "ssd_a_log")[0:HEADS], ACT.Exp).then_inc(acts, 1)

            @block.vector
            def _(dve):
                step = Chain(dve, dts)
                nc.vector.memset(S.dt[:, :, T:TP], 0.0).then_inc(padded, 1)
                dve.wait_ge(L.products, done(L, 8))
                step(nc.vector.tensor_scalar(fm(raw[:, :]), psum_tn(S, 0)[0:HEADS, :, 0:TB], 1.0 / WSCALE,
                                             col(S, "ssd_dt_bias")[0:HEADS], ALU.mult, ALU.add))
                step(nc.vector.scalar_tensor_tensor(low[:, :], raw[:, :], -1.0, raw[:, :], ALU.mult, ALU.min))
                dve.wait_ge(acts, 3)
                step(nc.vector.scalar_tensor_tensor(S.dt[:, 0, 0:T], raw[:, 0:T], 0.0, low[:, 0:T], ALU.max, ALU.add))
                step(nc.vector.tensor_scalar(S.dt[:, 1, 0:T], S.dt[:, 0, 0:T], arate[:, 0:1], -1.0, ALU.mult, ALU.mult))
                dve.wait_ge(L.products, done(L, NB - 1))



def ssd_phase(nc, S):
    QUADS, QH = 4, 4
    with Phase(nc) as ctx:
        sb = lambda n, shape: ctx.enter_context(nc.sbuf_tensor(n, shape, F32))
        sem = lambda n: ctx.semaphore(n)
        ch = sb("chunk", [P, XBC_B, P])
        dtc = sb("chunk_dt", [HEADS, 2, P])
        bt = sb("b_tokens", [P, 2, P])
        da = sb("dt_tokens", [P, 2 * HEADS])
        sums = sb("dt_a_sums", [P, 2 * HEADS])
        gap = sb("to_end", [P, HEADS])
        decs = sb("decay_to_end", [P, HEADS])
        ctot = sb("chunk_decay", [P, HEADS])
        xdt = sb("x_dt", [P, HEADS, HD])
        xdec = sb("x_decayed", [P, HEADS, HD])
        cbm = sb("cb_masked", [P, 2, P])
        seg = sb("seg", [P, HEADS, P])
        ea = sb("decay_in", [P, PAIRS, P])
        xd = sb("x_skip", [P, PAIRS, P])
        yt = sb("y_terms", [P, PAIRS, P])
        state = sb("state", [P, HEADS, HD])
        (s_copied, s_xt, s_da, s_bt, s_cum, s_gap, s_dec, s_xdt, s_xdec, s_cb, s_cbm, s_row, s_ea, s_seg, s_m,
         s_off, s_diag, s_t, s_yd, s_step, s_y, s_st, s_decd, s_state, s_skip, s_exp) = (sem("ssd_" + n) for n in (
            "copied", "xt", "da", "bt", "cum", "gap", "dec", "xdt", "xdec", "cb", "cbm", "row", "ea", "seg", "m",
            "off", "diag", "t", "yd", "step", "y", "st", "decd", "state", "skip", "exp"))
        ps = S.ps
        xt_ps = ps[:, 0:2, :]
        st_ps = [ps[:, 0, :], ps[:, 1, :]]
        b_ps, cb_ps = ps[:, 2, 0:2 * P], ps[:, 2, 2 * P:4 * P]
        da_ps, sum_ps = ps[:, 3, 0:2 * HEADS], ps[:, 3, 2 * HEADS:4 * HEADS]
        row_ps = [ps[:, 4, :], ps[:, 5, :]]
        off_ps, diag_ps = ps[:, 6, :], ps[:, 7, :]
        with nc.Block() as block:
            @block.gpsimd
            def _(pool):
                nc.gpsimd.memset(state[:, :, :], 0.0).then_inc(s_state, 2)
                with pool.Fori(0, NCH) as c:
                    lone_wait(S, pool, s_yd, c * 2 + 1)
                    lone_wait(S, pool, s_st, c * 2 + 1)
                    nc.gpsimd.tensor_copy(ch[:, :, :], S.xbc[:, :, bass.ds(c * P, P)])
                    nc.gpsimd.tensor_copy(dtc[:, :, :], S.dt[:, :, bass.ds(c * P, P)]).then_inc(s_copied, 1)
                    lone_wait(S, pool, s_copied, c + 1)
                    for p in range(PAIRS):
                        last = nc.gpsimd.tensor_scalar(xd[:, p, :], ch[:, p, :], col(S, "ssd_d", p), 1.0, ALU.mult, ALU.mult)
                    last.then_inc(s_skip, 1)
                    lone_wait(S, pool, s_xdt, c + 1)
                    lone_wait(S, pool, s_dec, c * 2 + 1)
                    nc.gpsimd.tensor_tensor(xdec[:, :, :], xdt[:, :, :], decs[:, :].unsqueeze(2).to_broadcast([P, HEADS, HD]),
                                            ALU.mult).then_inc(s_xdec, 1)

            @block.tensor
            def _(pe):
                nc.tensor.sem_inc(s_st, 1)
                with pe.Fori(0, NCH) as c:
                    pe.wait_ge(s_copied, c + 1)
                    pe.wait_ge(s_state, c * 2 + 2)
                    for j in range(DB):
                        nc.tensor.transpose(xt_ps.rearrange("p a n -> p (a n)")[:, j * P:(j + 1) * P], ch[:, j, :], S.ident[:, :])
                    for j in range(2):
                        last = nc.tensor.transpose(da_ps[:, j * HEADS:(j + 1) * HEADS], dtc[:, j, :], S.ident[0:HEADS, 0:HEADS])
                    last.then_inc(s_xt, 1)
                    pe.wait_ge(s_cbm, c + 1)
                    for g in range(2):
                        nc.tensor.transpose(b_ps[:, g * P:(g + 1) * P], ch[:, DB + g, :], S.ident[:, :])
                    for g in range(2):
                        last = nc.tensor.matmul(cb_ps[:, g * P:(g + 1) * P], ch[:, DB + g, :], ch[:, DB + 2 + g, :], start=True, stop=True)
                    last.then_inc(s_cb, 1)
                    pe.wait_ge(s_da, c + 1)
                    nc.tensor.matmul(sum_ps[:, 0:HEADS], S.upper[:, :], da[:, HEADS:], start=True, stop=True)
                    nc.tensor.matmul(sum_ps[:, HEADS:], S.ones[:, :], da[:, HEADS:], start=True, stop=True).then_inc(s_cum, 1)
                    for q in range(QUADS):
                        pe.wait_ge(s_seg, c * 4 + (q + 1))
                        for j in range(QH):
                            a = HEADS + q * QH + j
                            last = nc.tensor.matmul(row_ps[q % 2][:, j * P:(j + 1) * P], da[:, a:a + 1].to_broadcast([P, P]),
                                                    S.upper[:, :], start=True, stop=True)
                        last.then_inc(s_row, 1)
                    for g in range(2):
                        pe.wait_ge(s_t, c * 2 + (g + 1))
                        for p in range(4):
                            last = nc.tensor.matmul(off_ps[:, p * P:(p + 1) * P],
                                                    state[:, g * 8 + 2 * p:g * 8 + 2 * p + 2, :].rearrange("p a n -> p (a n)"),
                                                    ch[:, DB + 2 + g, :], start=True, stop=True)
                        last.then_inc(s_off, 1)
                        pe.wait_ge(s_m, c * 4 + 2 * g + 2)
                        pe.wait_ge(s_yd, c * 2 + (g + 1))
                        for p in range(4):
                            for a in range(2):
                                h = g * 8 + 2 * p + a
                                last = nc.tensor.matmul(diag_ps[a * HD:(a + 1) * HD, p * P:(p + 1) * P], xdt[:, h, :], seg[:, h, :],
                                                        start=True, stop=True)
                        last.then_inc(s_diag, 1)
                    pe.wait_ge(s_xdec, c + 1)
                    pe.wait_ge(s_bt, c + 1)
                    for g in range(2):
                        nc.tensor.matmul(st_ps[g], bt[:, g, :], xdec[:, g * 8:g * 8 + 8, :].rearrange("p a n -> p (a n)"),
                                         start=True, stop=True).then_inc(s_st, 1)

            @block.scalar
            def _(act):
                nc.scalar.sem_inc(s_seg, 2)
                nc.scalar.preload_act_table(ACT.Exp)
                with act.Fori(0, NCH) as c:
                    act.wait_ge(s_gap, c + 1)
                    act.wait_ge(s_xdec, c)
                    nc.scalar.activation(decs[:, :], gap[:, :], ACT.Exp).then_inc(s_dec, 1)
                    nc.scalar.activation(ctot[:, :], sums[:, HEADS:], ACT.Exp).then_inc(s_dec, 1)
                    for q in range(QUADS):
                        act.wait_ge(s_row, c * 4 + (q + 1))
                        if q == 0:
                            act.wait_ge(s_t, c * 2 + 1)
                            act.wait_ge(s_diag, c * 2)
                        rows = row_ps[q % 2].rearrange("p (a b n) -> p a b n", a=2, b=2)
                        for a in range(2):
                            nc.scalar.activation(ea[a * HD:(a + 1) * HD, 2 * q:2 * q + 2, :], rows[a * HD:(a + 1) * HD, :, a, :],
                                                 ACT.Exp).then_inc(s_ea, 1)
                        for j in range(QH):
                            h = q * QH + j
                            last = nc.scalar.activation(seg[:, h, :], row_ps[q % 2][:, j * P:(j + 1) * P], ACT.Relu, scale=-1.0,
                                                        bias=sums[:, h:h + 1])
                        last.then_inc(s_seg, 1)
                        act.wait_ge(s_seg, c * 4 + (q + 3))
                        four = seg[:, q * QH:(q + 1) * QH, :]
                        nc.scalar.activation(four, four, ACT.Exp, scale=-1.0).then_inc(s_exp, 1)

            @block.vector
            def _(dve):
                nc.vector.sem_inc(s_cbm, 1)
                nc.vector.sem_inc(s_t, 1)
                nc.vector.sem_inc(s_yd, 1)
                with dve.Fori(0, NCH) as c:
                    dve.wait_ge(s_xt, c + 1)
                    nc.vector.tensor_copy(da[:, :], da_ps).then_inc(s_da, 1)
                    dve.wait_ge(s_da, c + 1)
                    dve.wait_ge(s_st, c * 2 + 1)
                    nc.vector.tensor_tensor(xdt[:, :, :], xt_ps.rearrange("p a (b n) -> p (a b) n", n=HD),
                                            da[:, 0:HEADS].unsqueeze(2).to_broadcast([P, HEADS, HD]), ALU.mult).then_inc(s_xdt, 1)
                    dve.wait_ge(s_cum, c + 1)
                    dve.wait_ge(s_seg, c * 4 + 2)
                    nc.vector.tensor_copy(sums[:, :], sum_ps).then_inc(s_step, 1)
                    dve.wait_ge(s_step, c + 1)
                    nc.vector.tensor_tensor(gap[:, :], sums[:, HEADS:], sums[:, 0:HEADS], ALU.subtract).then_inc(s_gap, 1)
                    dve.wait_ge(s_cb, c + 1)
                    nc.vector.tensor_copy(bt[:, :, :].rearrange("p a n -> p (a n)"), b_ps).then_inc(s_bt, 1)
                    nc.vector.tensor_tensor(cbm[:, :, :], cb_ps.rearrange("p (a n) -> p a n", a=2),
                                            S.upper[:, :].unsqueeze(1).to_broadcast([P, 2, P]), ALU.mult).then_inc(s_cbm, 1)
                    dve.wait_ge(s_cbm, c + 2)
                    for q in range(QUADS):
                        dve.wait_ge(s_exp, c * 4 + (q + 1))
                        four = seg[:, q * QH:(q + 1) * QH, :]
                        nc.vector.tensor_tensor(four, four, cbm[:, q // 2, :].unsqueeze(1).to_broadcast([P, QH, P]),
                                                ALU.mult).then_inc(s_m, 1)
                    dve.wait_ge(s_skip, c + 1)
                    for g in range(2):
                        mine = slice(4 * g, 4 * g + 4)
                        dve.wait_ge(s_off, c * 2 + (g + 1))
                        dve.wait_ge(s_ea, c * 8 + 4 * g + 4)
                        nc.vector.tensor_tensor(yt[:, mine, :], off_ps.rearrange("p (a n) -> p a n", a=4), ea[:, mine, :], ALU.mult).then_inc(s_t, 1)
                        dve.wait_ge(s_t, c * 2 + (g + 2))
                        nc.vector.tensor_tensor(yt[:, mine, :], yt[:, mine, :], xd[:, mine, :], ALU.add).then_inc(s_y, 1)
                        dve.wait_ge(s_y, c * 4 + 2 * g + 1)
                        dve.wait_ge(s_diag, c * 2 + (g + 1))
                        nc.vector.tensor_tensor(yt[:, mine, :], yt[:, mine, :], diag_ps.rearrange("p (a n) -> p a n", a=4), ALU.add).then_inc(s_yd, 1)
                        dve.wait_ge(s_yd, c * 2 + (g + 2))
                        zs = S.z[:, mine, bass.ds(c * P, P)]
                        nc.vector.tensor_tensor(zs, yt[:, mine, :], zs, ALU.mult).then_inc(s_y, 1)
                    for g in range(2):
                        mine = slice(8 * g, 8 * g + 8)
                        if g == 0:
                            dve.wait_ge(s_dec, c * 2 + 2)
                        nc.vector.tensor_tensor(state[:, mine, :], state[:, mine, :], ctot[:, mine].unsqueeze(2).to_broadcast([P, 8, HD]),
                                                ALU.mult).then_inc(s_decd, 1)
                        dve.wait_ge(s_decd, c * 2 + (g + 1))
                        dve.wait_ge(s_st, c * 2 + (g + 2))
                        nc.vector.tensor_tensor(state[:, mine, :], state[:, mine, :], st_ps[g].rearrange("p (a n) -> p a n", n=HD),
                                                ALU.add).then_inc(s_state, 1)



HALF = HEADS // 2
QKV_B = 12


def qkv_phase(nc, S, A, half):
    tag = f"qkv{half}"
    with Phase(nc) as ctx:
        L = linear_buffers(nc, ctx, S, DB, tag)
        sem = lambda n: ctx.semaphore(f"{n}_{tag}")
        sb = lambda n, shape, dt: ctx.enter_context(nc.sbuf_tensor(f"{n}_{tag}", shape, dt))
        full = sb("full", [P, SLOTS, TP], F32)
        hi, lo = sb("hi", [P, SLOTS, TW], F16), sb("lo", [P, SLOTS, TW], F16)
        s_full, s_hi, s_lo, s_placed, s_zero, s_turned, s_vhi, s_vlo = (
            sem(n) for n in ("full", "hi", "lo", "placed", "zero", "turned", "vhi", "vlo"))
        QK_B = 8
        tiles = lambda s, n: psum_tn(S, s)[:, n, 0:3 * P].rearrange("p (t h d) -> p t h d", t=3, d=HD)
        def v2(b, n, part):
            return S.v2[:, 3 * n:3 * n + 3, bass.ds((b - QK_B) * 2, 2), part * HD:(part + 1) * HD]
        with nc.Block() as block:
            @block.sync
            def _(sp):
                stream_weights(sp, L, A["w_qkv"], half * QKV_B, QKV_B)

            @block.gpsimd
            def _(pool):
                cut_weights(nc, S, pool, L, QKV_B)

            @block.tensor
            def _(pe):
                banks = lambda s: psum_tn(S, s)

                def turn(i, s):
                    pe.wait_ge(s_full, i * SLOTS + (s + 1))
                    for t in range(NCH):
                        last = nc.tensor.transpose(psum_tn(S, s)[:, t // 3, (t % 3) * P:(t % 3 + 1) * P],
                                                   full[:, s, t * P:(t + 1) * P], S.ident[:, :])
                    last.then_inc(s_turned, 1)

                products(nc, pe, L, normed(S), banks, 0, QK_B)
                products(nc, pe, L, normed(S), banks, QK_B, QKV_B, after=turn)

            @block.scalar
            def _(act):
                nc.scalar.sem_inc(L.emptied, SLOTS)
                act.wait_ge(s_zero, 1)
                with act.Fori(0, QK_B // SLOTS) as i:
                    for s in range(SLOTS):
                        act.wait_ge(L.products, done(L, i * SLOTS + s))
                        act.wait_ge(s_placed, i * SLOTS + (s + 1))
                        nc.scalar.activation(fm(hi[:, s, :]), psum_tn(S, s)[:, :, 0:TB], ACT.Copy, scale=1.0 / WSCALE).then_inc(s_hi, 1)
                        nc.scalar.activation(fm(full[:, s, 0:TW]), psum_tn(S, s)[:, :, 0:TB], ACT.Copy, scale=1.0 / WSCALE).then_inc(s_full, 1)
                        act.wait_ge(s_full, i * SLOTS + (s + 1))
                        nc.scalar.sem_inc(L.emptied, 1)
                with act.Fori(QK_B // SLOTS, QKV_B // SLOTS) as i:
                    for s in range(SLOTS):
                        b = i * SLOTS + s
                        act.wait_ge(L.products, done(L, b))
                        act.wait_ge(s_placed, QK_B + SLOTS)
                        nc.scalar.activation(fm(full[:, s, 0:TW]), psum_tn(S, s)[:, :, 0:TB], ACT.Copy, scale=1.0 / WSCALE).then_inc(s_full, 1)
                        act.wait_ge(s_turned, b - (QK_B - 1))
                        for n in range(NT):
                            last = nc.scalar.activation(v2(b, n, 0), tiles(s, n), ACT.Copy)
                        last.then_inc(s_vhi, 1)
                        act.wait_ge(s_vlo, b - (QK_B - 1))
                        nc.scalar.sem_inc(L.emptied, 1)

            @block.vector
            def _(dve):
                nc.vector.memset(full[:, :, TW:TP], 0.0).then_inc(s_zero, 1)
                nc.vector.sem_inc(s_placed, SLOTS)
                with dve.Fori(0, QK_B // SLOTS) as i:
                    for s in range(SLOTS):
                        b = i * SLOTS + s
                        dve.wait_ge(s_full, i * SLOTS + (s + 1))
                        nc.vector.tensor_tensor(lo[:, s, :], full[:, s, 0:TW], hi[:, s, :], ALU.subtract).then_inc(s_lo, 1)
                        dve.wait_ge(s_lo, i * SLOTS + (s + 1))
                        for a in range(2):
                            mine = slice(a * HD, (a + 1) * HD)
                            dst = S.qk[:, bass.ds(b * 2 + a, 1), :].rearrange("p a n -> p (a n)")
                            nc.vector.tensor_copy(dst[0:HD], hi[mine, s, :])
                            last = nc.vector.tensor_copy(dst[HD:P], lo[mine, s, :])
                        last.then_inc(s_placed, 1)
                with dve.Fori(QK_B // SLOTS, QKV_B // SLOTS) as i:
                    for s in range(SLOTS):
                        b = i * SLOTS + s
                        dve.wait_ge(s_vhi, b - (QK_B - 1))
                        for n in range(NT):
                            last = nc.vector.tensor_tensor(v2(b, n, 1), tiles(s, n), v2(b, n, 0), ALU.subtract)
                        last.then_inc(s_vlo, 1)


class Tile:

    def __init__(self, i):
        self.i = i
        self.first_queries = i == NCH
        self.sb = 0 if self.first_queries else NCH - 1 - i
        self.s0 = self.sb * P
        self.rows = META if self.first_queries or self.sb == NCH - 1 else P
        self.t0 = 0 if self.first_queries else max(self.s0, META)
        self.w = (META if self.first_queries else T) - self.t0
        self.slot = i % 3
        self.dw = min(self.s0 + P, self.t0 + self.w) - self.t0
        self.d0 = self.t0 - self.s0

    def cuts(self, at=0):
        out = []
        while at < self.w:
            end = min(self.w, (at // BANK + 1) * BANK)
            out.append((at, end))
            at = end
        return out


TILES = [Tile(i) for i in range(NCH + 1)]
NTILE = len(TILES)
NLATER = NCH - 1


def attention_phase(nc, S, half):
    tag = f"att{half}"
    CAP = 40.0
    with Phase(nc) as ctx:
        sem = lambda n: ctx.semaphore(f"{n}_{tag}")
        sb = lambda n, shape, dt=F32: ctx.enter_context(nc.sbuf_tensor(f"{n}_{tag}", shape, dt))
        kf, ks = sb("k_head", [P, TW], F16), sb("k_swapped", [P, TW], F16)
        vf = sb("v_head", [P, NCH, P], F16)
        e = sb("e", [P, 2, SEQ])
        sp_ = sb("softplus", [P, 2, SEQ])
        later = sb("later", [P, 2, T])
        w = sb("w", [P, 2, SEQ])
        whi, wlo = sb("w_hi", [P, 2, SEQ], F16), sb("w_lo", [P, 2, SEQ], F16)
        half_o = sb("o_low", [HD, T])
        (s_head, s_z, s_zm, s_e, s_l, s_raw, s_sp, s_lat, s_b, s_w, s_wm, s_whi, s_cut, s_c, s_oc, s_oe, s_clear) = (sem(n) for n in (
            "head", "z", "zm", "e", "l", "raw", "sp", "lat", "b", "w", "wm", "whi", "cut", "c", "oc", "oe", "clear"))
        flat = S.ps[:, :, :].rearrange("p a n -> p (a n)")
        zps = lambda t: flat[:, 2 * t.slot * BANK:2 * t.slot * BANK + 2 * BANK]
        ops = flat[:, 6 * BANK:8 * BANK]
        first_o = zps(TILES[NCH])[:, BANK:BANK + META]

        def index(it, a, i):
            return it * (2 * NTILE) + (a * NTILE + i)

        with nc.Block() as block:
            @block.tensor
            def _(pe):
                nc.tensor.sem_inc(s_b, 2)
                nc.tensor.sem_inc(s_c, 2)

                def scores(it, a, t):
                    if t.i < 3:
                        pe.wait_ge(s_w, index(it, a, 0))
                        pe.wait_ge(s_oe, it * 2 + a)
                    else:
                        pe.wait_ge(s_w, index(it, a, t.i - 2))
                    q = S.qk[:, bass.ds(it * 2 + a, 1), :].rearrange("p a n -> p (a n)")
                    for lo_, hi_ in t.cuts():
                        for k in (kf, ks):
                            last = nc.tensor.matmul(zps(t)[0:t.rows, lo_:hi_], k[:, t.s0:t.s0 + t.rows], q[:, t.t0 + lo_:t.t0 + hi_],
                                                    start=(k is kf), stop=(k is ks), skip_group_check=True)
                    last.then_inc(s_z, 1)

                def sums(it, a, t):
                    lone_wait(S, pe, s_sp, index(it, a, t.i + 1))
                    for lo_, hi_ in t.cuts():
                        last = nc.tensor.matmul(zps(t)[0:t.rows, lo_:hi_], S.tri8[0:t.rows, 0:t.rows], sp_[0:t.rows, t.i % 2, lo_:hi_],
                                                start=False, stop=True, skip_group_check=True)
                    if 1 <= t.i < NCH:
                        pe.wait_ge(s_lat, it * (2 * NLATER) + (a * NLATER + t.i))
                        for lo_, hi_ in t.cuts(TILES[t.i - 1].t0 - t.t0):
                            last = nc.tensor.matmul(zps(t)[:, lo_:hi_], S.ones8[:, :], later[:, t.i % 2, t.t0 + lo_:t.t0 + hi_],
                                                    start=False, stop=True, skip_group_check=True)
                    last.then_inc(s_b, 1)

                def values(it, a, t):
                    pe.wait_ge(s_cut, index(it, a, t.i + 3))
                    v = vf[0:t.rows, t.sb, :]
                    parts = (whi, wlo)
                    if t.first_queries:
                        for j, x in enumerate(parts):
                            last = nc.tensor.matmul(first_o, v, x[0:t.rows, t.i % 2, 0:t.w], start=(j == 0), stop=(j == 1), skip_group_check=True)
                    else:
                        c0 = t.t0 - META
                        for bank in range(2):
                            lo_, hi_ = max(c0, bank * BANK), (bank + 1) * BANK
                            if lo_ >= hi_:
                                continue
                            opens = t.i == 0 or (bank == 0 and TILES[t.i - 1].t0 - META >= BANK)
                            for j, x in enumerate(parts):
                                last = nc.tensor.matmul(ops[:, lo_:hi_], v, x[0:t.rows, t.i % 2, lo_ - c0:hi_ - c0],
                                                        start=(opens and j == 0), stop=True, skip_group_check=True)
                    last.then_inc(s_c, 1)

                with pe.Fori(0, HALF // 2) as it:
                    for a in range(2):
                        pe.wait_ge(s_head, it * 2 + (a + 1))
                        scores(it, a, TILES[0])
                        scores(it, a, TILES[1])
                        for t in TILES:
                            sums(it, a, t)
                            if t.i + 2 < NTILE:
                                scores(it, a, TILES[t.i + 2])
                            if t.i >= 1:
                                values(it, a, TILES[t.i - 1])
                        values(it, a, TILES[-1])

            @block.scalar
            def _(act):
                nc.scalar.sem_inc(s_l, 2)
                nc.scalar.preload_act_table_set("natural_log_exp_and_others")

                def log1p(it, a, t):
                    n = index(it, a, t.i + 1)
                    x = e[0:t.rows, t.i % 2, 0:t.w]
                    act.wait_ge(s_zm, n)
                    nc.scalar.activation(x, x, ACT.Exp).then_inc(s_e, 1)
                    act.wait_ge(s_e, n)
                    nc.scalar.activation(x, x, ACT.Ln, bias=1.0).then_inc(s_l, 1)

                def weights(it, a, t):
                    act.wait_ge(s_b, index(it, a, t.i + 3))
                    act.wait_ge(s_cut, index(it, a, t.i + 1))
                    nc.scalar.activation(w[0:t.rows, t.i % 2, 0:t.w], zps(t)[0:t.rows, 0:t.w], ACT.Exp, scale=0.125).then_inc(s_w, 1)

                with act.Fori(0, HALF // 2) as it:
                    for a in range(2):
                        log1p(it, a, TILES[0])
                        log1p(it, a, TILES[1])
                        for t in TILES:
                            weights(it, a, t)
                            if t.i + 2 < NTILE:
                                log1p(it, a, TILES[t.i + 2])
                        act.wait_ge(s_c, index(it, a, NTILE + 2))
                        act.wait_ge(s_oe, it * 2 + a)
                        nc.scalar.activation(half_o[:, META:T], ops[HD:P, :], ACT.Copy)
                        nc.scalar.activation(half_o[:, 0:META], first_o[HD:P, :], ACT.Copy).then_inc(s_oc, 1)

            @block.vector
            def _(dve):
                def capped(it, a, t):
                    dve.wait_ge(s_z, index(it, a, t.i + 1))
                    dve.wait_ge(s_l, index(it, a, t.i + 1))
                    nc.vector.tensor_scalar(e[0:t.rows, t.i % 2, 0:t.w], zps(t)[0:t.rows, 0:t.w], 0.125, CAP, ALU.mult, ALU.min).then_inc(s_zm, 1)

                def softplus(it, a, t):
                    n = index(it, a, t.i + 1)
                    dve.wait_ge(s_l, n + 2)
                    dve.wait_ge(s_b, n)
                    x = sp_[0:t.rows, t.i % 2, 0:t.w]
                    nc.vector.scalar_tensor_tensor(x, zps(t)[0:t.rows, 0:t.w], 0.125, e[0:t.rows, t.i % 2, 0:t.w],
                                                   ALU.mult, ALU.max).then_inc(s_raw, 1)
                    dve.wait_ge(s_raw, n)
                    d = sp_[0:t.rows, t.i % 2, 0:t.dw]
                    nc.vector.tensor_tensor(d, d, S.strict[0:t.rows, t.d0:t.d0 + t.dw], ALU.mult).then_inc(s_sp, 1)

                def add_later(it, a, t):
                    dve.wait_ge(s_sp, index(it, a, t.i + 1))
                    new, old = later[:, (t.i + 1) % 2, :], later[:, t.i % 2, :]
                    if t.i == 0:
                        dve.wait_ge(s_b, index(it, a, 2))
                        nc.vector.memset(new[:, t.t0:T], 0.0).then_inc(s_clear, 1)
                        dve.wait_ge(s_clear, it * 2 + (a + 1))
                        nc.vector.tensor_copy(new[0:t.rows, t.t0:T], sp_[0:t.rows, 0, 0:t.w]).then_inc(s_lat, 1)
                        return
                    dve.wait_ge(s_b, index(it, a, t.i + 2))
                    seam = TILES[t.i - 1].t0
                    nc.vector.tensor_copy(new[:, t.t0:seam], sp_[:, t.i % 2, 0:seam - t.t0])
                    nc.vector.tensor_tensor(new[:, seam:T], old[:, seam:T], sp_[:, t.i % 2, seam - t.t0:t.w], ALU.add).then_inc(s_lat, 1)

                def mask_weights(it, a, t):
                    dve.wait_ge(s_w, index(it, a, t.i + 1))
                    d = w[0:t.rows, t.i % 2, 0:t.dw]
                    nc.vector.scalar_tensor_tensor(d, d, 1.0, S.strict[0:t.rows, t.d0:t.d0 + t.dw], ALU.min, ALU.mult).then_inc(s_wm, 1)

                with dve.Fori(0, HALF // 2) as it:
                    for a in range(2):
                        dve.wait_ge(s_c, index(it, a, 2))
                        h = it * 2 + a
                        k = S.qk[:, bass.ds(h + HALF, 1), :].rearrange("p a n -> p (a n)")
                        nc.vector.tensor_copy(kf[:, :], k)
                        nc.vector.tensor_copy(ks[0:HD, :], k[HD:P])
                        nc.vector.tensor_copy(ks[HD:P, :], k[0:HD])
                        nc.vector.tensor_copy(vf[:, :, :], S.v2[:, :, bass.ds(h, 1), :].rearrange("p t a n -> p t (a n)")).then_inc(s_head, 1)
                        capped(it, a, TILES[0])
                        capped(it, a, TILES[1])
                        for t in TILES:
                            softplus(it, a, t)
                            if t.i >= 1:
                                mask_weights(it, a, TILES[t.i - 1])
                            if t.i < NLATER:
                                add_later(it, a, t)
                            if t.i + 2 < NTILE:
                                capped(it, a, TILES[t.i + 2])
                        mask_weights(it, a, TILES[-1])
                        dve.wait_ge(s_oc, it * 2 + (a + 1))
                        o = S.z[a * HD:(a + 1) * HD, bass.ds(it + half * (HALF // 2), 1), 0:T].rearrange("p a n -> p (a n)")
                        nc.vector.tensor_tensor(o[:, META:T], ops[0:HD, :], half_o[:, META:T], ALU.add)
                        nc.vector.tensor_tensor(o[:, 0:META], first_o[0:HD, :], half_o[:, 0:META], ALU.add).then_inc(s_oe, 1)

            @block.gpsimd
            def _(pool):
                nc.gpsimd.sem_inc(s_cut, 2)
                with pool.Fori(0, HALF // 2) as it:
                    for a in range(2):
                        for t in TILES:
                            n = index(it, a, t.i + 1)
                            x = w[0:t.rows, t.i % 2, 0:t.w]
                            hi, lo = whi[0:t.rows, t.i % 2, 0:t.w], wlo[0:t.rows, t.i % 2, 0:t.w]
                            lone_wait(S, pool, s_wm, n)
                            lone_wait(S, pool, s_c, n)
                            nc.gpsimd.tensor_copy(hi, x).then_inc(s_whi, 1)
                            lone_wait(S, pool, s_whi, n)
                            nc.gpsimd.tensor_tensor(lo, x, hi, ALU.subtract).then_inc(s_cut, 1)



def linear_phase(nc, S, w, kb, xs, nb, out, tag, nt=NT, tb=TB, t0=0, plus=None):
    with Phase(nc) as ctx:
        L = linear_buffers(nc, ctx, S, kb, tag)
        banks = lambda s: S.ps[:, nt * s:nt * s + nt, :]
        with nc.Block() as block:
            @block.sync
            def _(sp):
                stream_weights(sp, L, w, 0, nb)

            @block.gpsimd
            def _(pool):
                cut_weights(nc, S, pool, L, nb)

            @block.tensor
            def _(pe):
                products(nc, pe, L, xs, banks, 0, nb, nt, tb, t0)

            if plus is None:
                @block.scalar
                def _(act):
                    nc.scalar.sem_inc(L.emptied, SLOTS)
                    with act.Fori(0, nb // SLOTS) as i:
                        for s in range(SLOTS):
                            act.wait_ge(L.products, done(L, i * SLOTS + s))
                            nc.scalar.activation(fm(blk(out, i * SLOTS + s), nt), banks(s)[:, :, 0:tb], ACT.Copy,
                                                 scale=1.0 / WSCALE).then_inc(L.emptied, 1)
            else:
                @block.vector
                def _(dve):
                    nc.vector.sem_inc(L.emptied, SLOTS)
                    with dve.Fori(0, nb // SLOTS) as i:
                        for s in range(SLOTS):
                            dve.wait_ge(L.products, done(L, i * SLOTS + s))
                            nc.vector.scalar_tensor_tensor(fm(blk(out, i * SLOTS + s), nt), banks(s)[:, :, 0:tb], 1.0 / WSCALE,
                                                           fm(blk(plus, i * SLOTS + s), nt), ALU.mult, ALU.add).then_inc(L.emptied, 1)


FTAPS = 3


def ffn_up_phase(nc, S, A):
    with Phase(nc) as ctx:
        L = linear_buffers(nc, ctx, S, DB, "up")
        sb = lambda n: ctx.enter_context(nc.sbuf_tensor(n, [P, TW], F32))
        sem = lambda n: ctx.semaphore("ffn_" + n)
        raw = ctx.enter_context(nc.sbuf_tensor("gate_raw", [P, FTAPS - 1 + TW], F32))
        acc, f = sb("gate_conv"), sb("f_full")
        s_zero, s_raw, s_step, s_conv, s_gelu, s_f, s_hi, s_lo = (sem(n) for n in ("zero", "raw", "step", "conv", "gelu", "f", "hi", "lo"))
        with nc.Block() as block:
            @block.sync
            def _(sp):
                stream_weights(sp, L, A["w_up"], 0, 2 * FFB)

            @block.gpsimd
            def _(pool):
                cut_weights(nc, S, pool, L, 2 * FFB)

            @block.tensor
            def _(pe):
                products(nc, pe, L, normed(S), lambda s: psum_tn(S, s), 0, 2 * FFB)

            @block.scalar
            def _(act):
                nc.scalar.sem_inc(L.emptied, SLOTS)
                nc.scalar.preload_act_table(ACT.Gelu_apprx_tanh)
                act.wait_ge(s_zero, 1)
                with act.Fori(0, FFB) as i:
                    act.wait_ge(L.products, done(L, i * 2))
                    act.wait_ge(s_conv, i)
                    nc.scalar.activation(fm(raw[:, FTAPS - 1:]), psum_tn(S, 0)[:, :, 0:TB], ACT.Copy, scale=1.0 / WSCALE).then_inc(s_raw, 1)
                    act.wait_ge(s_raw, i + 1)
                    nc.scalar.sem_inc(L.emptied, 1)
                    act.wait_ge(s_conv, i + 1)
                    nc.scalar.activation(acc[:, :], acc[:, :], ACT.Gelu_apprx_tanh).then_inc(s_gelu, 1)
                    act.wait_ge(s_f, i + 1)
                    nc.scalar.activation(blk(S.fhi, i), f[:, :], ACT.Copy).then_inc(s_hi, 1)
                    nc.scalar.sem_inc(L.emptied, 1)

            @block.vector
            def _(dve):
                nc.vector.memset(raw[:, 0:FTAPS - 1], 0.0).then_inc(s_zero, 1)
                with dve.Fori(0, FFB) as i:
                    step = Chain(dve, s_step, i * (FTAPS - 1))
                    dve.wait_ge(s_raw, i + 1)
                    step(nc.vector.tensor_scalar(acc[:, :], raw[:, 0:TW], dcol(S, "ffn_conv_w", i, FTAPS, 0),
                                                 dcol(S, "ffn_conv_b", i), ALU.mult, ALU.add))
                    step(nc.vector.scalar_tensor_tensor(acc[:, :], raw[:, 1:1 + TW], dcol(S, "ffn_conv_w", i, FTAPS, 1), acc[:, :], ALU.mult, ALU.add))
                    nc.vector.scalar_tensor_tensor(acc[:, :], raw[:, 2:2 + TW], dcol(S, "ffn_conv_w", i, FTAPS, 2), acc[:, :],
                                                   ALU.mult, ALU.add).then_inc(s_conv, 1)
                    dve.wait_ge(L.products, done(L, i * 2 + 1))
                    dve.wait_ge(s_gelu, i + 1)
                    nc.vector.scalar_tensor_tensor(fm(f[:, :]), psum_tn(S, 1)[:, :, 0:TB], 1.0 / WSCALE, fm(acc[:, :]),
                                                   ALU.mult, ALU.mult).then_inc(s_f, 1)
                    dve.wait_ge(s_hi, i + 1)
                    nc.vector.tensor_tensor(blk(S.flo, i), f[:, :], blk(S.fhi, i), ALU.subtract).then_inc(s_lo, 1)
                    dve.wait_ge(s_lo, i + 1)


def ffn(nc, S, A):
    with ExitStack() as ctx:
        sb = lambda n, shape, dt: ctx.enter_context(nc.sbuf_tensor(n, shape, dt))
        S.fhi, S.flo = sb("f_hi", [P, FFB, TW], F16), sb("f_lo", [P, FFB, TW], F16)
        with ExitStack() as inp:
            S.xhi, S.xlo = (inp.enter_context(nc.sbuf_tensor(n, [P, DB, TW], F16)) for n in ("ffn_x_hi", "ffn_x_lo"))
            norm_phase(nc, S, "ffn_pre", S.h, "ffn_pre_g", DB, TW, ("cut", S.xhi, S.xlo))
            ffn_up_phase(nc, S, A)
        with nc.sbuf_tensor("ffn_out", [P, DB, SEQ], F32) as down:
            linear_phase(nc, S, A["w_down"], FFB, lambda k: (S.fhi[:, k, :], S.flo[:, k, :]), DB, down, "down", 2, BANK, META)
            norm_phase(nc, S, "ffn_post", down, "ffn_post_g", DB, SEQ, ("add", S.h[:, :, META:T]), 2, BANK)



SUB = 64
NSUB = SEQ // SUB
NUNIT = SEQ // P
NLEVEL = 6
GQ, GK, GV, GG, GLR, GLA_B = 0, 2, 4, 8, 12, 14
GLA_HEADS = 4
GLA_TAU = 16.0


def masks_phase(nc, S):
    with Phase(nc) as ctx:
        s_set, s_sel = (ctx.semaphore(n) for n in ("mask2_set", "mask2_sel"))
        with nc.Block() as block:
            @block.gpsimd
            def _(pool):
                step = Chain(pool, s_set)
                nc.gpsimd.memset(S.scan[:, :], 1.0)
                nc.gpsimd.memset(S.levels[:, :, :], 1.0)
                step(nc.gpsimd.memset(S.same[:, :], 0.0))
                for a in range(2):
                    last = nc.gpsimd.memset(S.same[a * SUB:(a + 1) * SUB, a * SUB:(a + 1) * SUB], 1.0)
                step(last)
                nc.gpsimd.memset(S.scan[:, :].rearrange("p (c t) -> p c t", t=SUB)[:, :, 0:1], 0.0)
                nc.gpsimd.tensor_tensor(S.incl[:, :], S.same[:, :], S.upper[:, :], ALU.mult)
                nc.gpsimd.tensor_tensor(S.excl[:, :], S.same[:, :], S.strict[:, :], ALU.mult).then_inc(s_sel, 1)
                for l in range(NLEVEL):
                    m = 1 << l
                    v = S.levels[:, l, :].rearrange("p (b c t) -> p b c t", c=2, t=m)
                    step(nc.gpsimd.affine_select(out=v, in_=v, compare_op=ALU.is_ge, fill=0.0, base=0,
                                                 pattern=[[-2 * m, P // (2 * m)], [0, 2], [0, m]], channel_multiplier=1))
                    step(nc.gpsimd.affine_select(out=v, in_=v, compare_op=ALU.is_ge, fill=0.0, base=m - 1,
                                                 pattern=[[2 * m, P // (2 * m)], [0, 2], [0, m]], channel_multiplier=-1))
                    step(nc.gpsimd.memset(v[:, :, 0, :], 0.0))


def store_phase(nc, dst, src, tag):
    with Phase(nc) as ctx:
        s = ctx.semaphore("moved_" + tag)
        with nc.Block() as block:
            @block.sync
            def _(sp):
                sp.dma_start(dst, src).then_inc(s, 16)
                sp.wait_ge(s, 16)


def gla_prepare_phase(nc, S, A, u, qi, ki, kst, dec):
    with Phase(nc) as ctx:
        sb = lambda n, shape: ctx.enter_context(nc.sbuf_tensor("gla_" + n, shape, F32))
        sem = lambda n: ctx.semaphore("gla_" + n)
        up = sb("gate_up", [16, 2 * P])
        x, low, b = sb("gate", [P, 2, SEQ]), sb("low", [P, 2, SEQ]), sb("cum", [P, 2, SEQ])
        s_up, s_g, s_v, s_a, s_p = (sem(n) for n in ("up", "g", "v", "a", "p"))
        with nc.Block() as block:
            @block.sync
            def _(sp):
                sp.dma_start(up[:, :], A["gate_up"]).then_inc(s_up, 16)
                sp.wait_ge(s_up, 16)

            @block.tensor
            def _(pe):
                pe.wait_ge(s_up, 16)
                for c in range(2):
                    for n in range(2):
                        last = nc.tensor.matmul(S.ps[:, 2 * c + n, :], up[:, c * P:(c + 1) * P], u[0:16, GLR, n * BANK:(n + 1) * BANK],
                                                start=True, stop=True)
                last.then_inc(s_g, 1)

            @block.vector
            def _(dve):
                step = Chain(dve, s_v)
                dve.wait_ge(s_g, 1)
                for c in range(2):
                    last = nc.vector.tensor_scalar(fm(x[:, c, :], 2), S.ps[:, 2 * c:2 * c + 2, :], col(S, "gla_gate_bias_2", c), None, ALU.add)
                step(last)
                step(nc.vector.scalar_tensor_tensor(low[:, :, :], x[:, :, :], -1.0, x[:, :, :], ALU.mult, ALU.min))
                dve.wait_ge(s_a, 1)
                step(nc.vector.scalar_tensor_tensor(x[:, :, :], x[:, :, :], 0.0, low[:, :, :], ALU.min, ALU.subtract))
                step(nc.vector.tensor_scalar(x[:, :, :], x[:, :, :], 1.0 / GLA_TAU, None, ALU.mult))
                for c in range(2):
                    last = nc.vector.tensor_tensor_scan(b[:, c, :], S.scan[:, :], x[:, c, :], 0.0, ALU.mult, ALU.add)
                step(last)
                dve.wait_ge(s_a, 2)
                nc.vector.scalar_tensor_tensor(qi[:, :, :], u[:, GQ:GQ + 2, :], GLA_DK_SCALE, low[:, :, :], ALU.mult, ALU.mult)
                step(nc.vector.tensor_copy(dec[:, :, :], low[:, :, SUB - 1::SUB]))
                dve.wait_ge(s_a, 3)
                nc.vector.tensor_tensor(ki[:, :, :], u[:, GK:GK + 2, :], x[:, :, :], ALU.mult)
                for c in range(2):
                    bc = b[:, c, :].rearrange("p (n t) -> p n t", t=SUB)
                    last = nc.vector.tensor_tensor(low[:, c, :].rearrange("p (n t) -> p n t", t=SUB),
                                                   bc[:, :, SUB - 1:SUB].to_broadcast([P, NSUB, SUB]), bc, ALU.subtract)
                step(last)
                dve.wait_ge(s_a, 4)
                step(nc.vector.tensor_tensor(kst[:, :, :], u[:, GK:GK + 2, :], low[:, :, :], ALU.mult))

            @block.scalar
            def _(act):
                nc.scalar.preload_act_table_set("natural_log_exp_and_others")
                act.wait_ge(s_v, 2)
                nc.scalar.activation(low[:, :, :], low[:, :, :], ACT.Exp).then_inc(s_p, 1)
                act.wait_ge(s_p, 1)
                nc.scalar.activation(low[:, :, :], low[:, :, :], ACT.Ln, bias=1.0).then_inc(s_a, 1)
                act.wait_ge(s_v, 5)
                nc.scalar.activation(low[:, :, :], b[:, :, :], ACT.Exp).then_inc(s_a, 1)
                nc.scalar.activation(x[:, :, :], b[:, :, :], ACT.Exp, scale=-1.0).then_inc(s_a, 1)
                act.wait_ge(s_v, 7)
                nc.scalar.activation(low[:, :, :], low[:, :, :], ACT.Exp).then_inc(s_a, 1)


GLA_DK_SCALE = 64 ** -0.5


def gla_units_phase(nc, S, u, qi, ki, kst, dec):
    H = GLA_HEADS
    with Phase(nc) as ctx:
        sb = lambda n, shape: ctx.enter_context(nc.sbuf_tensor("gu_" + n, shape, F32))
        sem = lambda n: ctx.semaphore("gu_" + n)
        fmaj = sb("fm", [P, 6 + H, P])
        decs = sb("dec", [P, 2, 2])
        tok = sb("tok", [P, 2 + H, P])
        am = sb("scores", [P, H, P])
        st = sb("state", [P, 2, P])
        s_in, s_tp, s_tok, s_a, s_am, s_o, s_out, s_ds, s_st = (sem(n) for n in ("in", "tp", "tok", "a", "am", "o", "out", "ds", "st"))
        tp = S.ps[:, 0:2, :].rearrange("p a n -> p (a n)")
        aps, ops2 = [S.ps[:, b, 0:2 * P] for b in (2, 7)], [S.ps[:, b, 0:2 * P] for b in (4, 7)]
        ops = S.ps[:, 3, :]
        dps = [S.ps[:, 5 + c, 0:2 * P] for c in range(2)]
        with nc.Block() as block:
            @block.gpsimd
            def _(pool):
                nc.gpsimd.memset(st[:, :, :], 0.0).then_inc(s_in, 1)
                with pool.Fori(0, NUNIT) as c:
                    lone_wait(S, pool, s_out, c * 2 + 2)
                    at = bass.ds(c * P, P)
                    for j, src in enumerate((qi, ki, kst)):
                        nc.gpsimd.tensor_copy(fmaj[:, 2 * j:2 * j + 2, :], src[:, :, at])
                    nc.gpsimd.tensor_copy(fmaj[:, 6:6 + H, :], u[:, GV:GV + H, at])
                    nc.gpsimd.tensor_copy(decs[:, :, :], dec[:, :, bass.ds(c * 2, 2)]).then_inc(s_in, 1)

            @block.tensor
            def _(pe):
                with pe.Fori(0, NUNIT) as c:
                    pe.wait_ge(s_in, c + 2)
                    pe.wait_ge(s_st, c * 2)
                    for j in range(2 + H):
                        last = nc.tensor.transpose(tp[:, j * P:(j + 1) * P], fmaj[:, 4 + j, :], S.ident[:, :])
                    last.then_inc(s_tp, 1)
                    for h in range(H):
                        a = slice((h % 2) * HD, (h % 2 + 1) * HD)
                        last = nc.tensor.matmul(aps[h % 2][:, (h // 2) * P:(h // 2 + 1) * P], fmaj[a, 2 + h // 2, :], fmaj[a, h // 2, :], start=True, stop=True)
                    last.then_inc(s_a, 1)
                    pe.wait_ge(s_tok, c + 1)
                    pe.wait_ge(s_am, c + 1)
                    for h in range(H):
                        last = nc.tensor.matmul(ops[:, h * P:(h + 1) * P], tok[:, 2 + h, :], am[:, h, :], start=True, stop=True)
                    last.then_inc(s_o, 1)
                    for k in range(2):
                        t = slice(k * SUB, (k + 1) * SUB)
                        for h in range(H):
                            a = slice((h % 2) * HD, (h % 2 + 1) * HD)
                            last = nc.tensor.matmul(dps[k][a, (h // 2) * P:(h // 2 + 1) * P], tok[t, h // 2, a], tok[t, 2 + h, :],
                                                    start=True, stop=True)
                        last.then_inc(s_ds, 1)
                    for k in range(2):
                        lone_wait(S, pe, s_st, c * 2 + k)
                        t = slice(k * SUB, (k + 1) * SUB)
                        for h in range(H):
                            a = slice((h % 2) * HD, (h % 2 + 1) * HD)
                            last = nc.tensor.matmul(ops2[h % 2][:, (h // 2) * P + k * SUB:(h // 2) * P + (k + 1) * SUB], st[a, h // 2, :], fmaj[a, h // 2, t],
                                                    start=True, stop=True)
                        last.then_inc(s_o, 1)

            @block.vector
            def _(dve):
                nc.vector.sem_inc(s_out, 2)
                with dve.Fori(0, NUNIT) as c:
                    dve.wait_ge(s_tp, c + 1)
                    nc.vector.tensor_copy(tok[:, :, :].rearrange("p a n -> p (a n)"), tp[:, 0:(2 + H) * P]).then_inc(s_tok, 1)
                    dve.wait_ge(s_a, c + 1)
                    for a in range(2):
                        last = nc.vector.tensor_tensor(am[:, a::2, :], aps[a].rearrange("p (a n) -> p a n", a=2),
                                                       S.incl[:, :].unsqueeze(1).to_broadcast([P, 2, P]), ALU.mult)
                    last.then_inc(s_am, 1)
                    for k in range(2):
                        dve.wait_ge(s_ds, c * 2 + (k + 1))
                        dve.wait_ge(s_o, c * 3 + (k + 2))
                        for j in range(2):
                            last = nc.vector.scalar_tensor_tensor(st[:, j, :], st[:, j, :], decs[:, j, k:k + 1], dps[k][:, j * P:(j + 1) * P],
                                                                  ALU.mult, ALU.add)
                        last.then_inc(s_st, 1)
                    o = u[:, GV:GV + H, bass.ds(c * P, P)]
                    dve.wait_ge(s_o, c * 3 + 3)
                    nc.vector.tensor_copy(o, ops.rearrange("p (a n) -> p a n", a=H)).then_inc(s_out, 1)
                    dve.wait_ge(s_out, c * 2 + 3)
                    for a in range(2):
                        oa = u[:, GV + a:GV + H:2, bass.ds(c * P, P)]
                        last = nc.vector.tensor_tensor(oa, oa, ops2[a].rearrange("p (a n) -> p a n", a=2), ALU.add)
                    last.then_inc(s_out, 1)


def gla_finish_phase(nc, S, u, mhi, mlo):
    H = GLA_HEADS
    with Phase(nc) as ctx:
        sb = lambda n: ctx.enter_context(nc.sbuf_tensor("gf_" + n, [P, 2, SEQ], F32))
        sem = lambda n: ctx.semaphore("gf_" + n)
        sq, rs, gate = sb("sq"), sb("rs"), ctx.enter_context(nc.sbuf_tensor("gf_gate", [P, H, SEQ], F32))
        s_sq, s_sum, s_rt, s_rs, s_gt, s_y, s_hi, s_lo = (sem(n) for n in ("sq", "sum", "rt", "rs", "gt", "y", "hi", "lo"))
        with nc.Block() as block:
            @block.scalar
            def _(act):
                nc.scalar.activation(gate[:, :, :], u[:, GG:GG + H, :], ACT.Silu).then_inc(s_gt, 1)
                for h in range(H):
                    if h >= 2:
                        act.wait_ge(s_sum, h - 1)
                    nc.scalar.activation(sq[:, h % 2, :], u[:, GV + h, :], ACT.Square).then_inc(s_sq, 1)
                for h in range(H):
                    act.wait_ge(s_sum, h + 1)
                    if h >= 2:
                        act.wait_ge(s_y, 2 * (h - 1))
                    nc.scalar.activation(fm(rs[:, h % 2, :], 2), S.ps[:, 2 * h:2 * h + 2, :], ACT.Sqrt, scale=1.0 / P,
                                         bias=S.eps[:, 0:1]).then_inc(s_rt, 1)
                for h in range(H):
                    act.wait_ge(s_y, 2 * h + 2)
                    nc.scalar.activation(mhi[:, h, :], u[:, GV + h, :], ACT.Copy).then_inc(s_hi, 1)

            @block.tensor
            def _(pe):
                for h in range(H):
                    pe.wait_ge(s_sq, h + 1)
                    for n in range(2):
                        last = nc.tensor.matmul(S.ps[:, 2 * h + n, :], S.ones[:, :], sq[:, h % 2, n * BANK:(n + 1) * BANK], start=True, stop=True)
                    last.then_inc(s_sum, 1)

            @block.vector
            def _(dve):
                dve.wait_ge(s_gt, 1)
                for h in range(H):
                    dve.wait_ge(s_rt, h + 1)
                    nc.vector.reciprocal(rs[:, h % 2, :], rs[:, h % 2, :]).then_inc(s_rs, 1)
                    dve.wait_ge(s_rs, h + 1)
                    o = u[:, GV + h, :]
                    nc.vector.scalar_tensor_tensor(o, o, col(S, "gla_norm_w_2"), rs[:, h % 2, :], ALU.mult, ALU.mult).then_inc(s_y, 1)
                    dve.wait_ge(s_y, 2 * h + 1)
                    nc.vector.tensor_tensor(o, o, gate[:, h, :], ALU.mult).then_inc(s_y, 1)

            @block.gpsimd
            def _(pool):
                for h in range(H):
                    pool.wait_ge(s_hi, h + 1)
                    nc.gpsimd.tensor_tensor(mlo[:, h, :], u[:, GV + h, :], mhi[:, h, :], ALU.subtract).then_inc(s_lo, 1)



RR, RK, RV, RWA, RG, RWKV_B = 0, 4, 8, 12, 13, 18
RWKV_P = 4
RWKV_H = 2 * RWKV_P
MIXED = 13
DECAY = math.exp(-0.5)
LEVELS = range(1, NLEVEL)
VSTEPS = 12


def rwkv_prepare_phase(nc, S, A, u, kap, bt, bonus, plast):
    with Phase(nc) as ctx:
        sb = lambda n, shape=(P, SEQ): ctx.enter_context(nc.sbuf_tensor("rp_" + n, list(shape), F32))
        sem = lambda n: ctx.semaphore("rp_" + n)
        up, upb = sb("up", [P, RWKV_P * P]), sb("up_block", [P, P])
        d = sb("shift", [P, 2, SEQ])
        sg, a, cum, ep, en, em, kk, sq, t = (sb(n) for n in ("sg", "a", "cum", "ep", "en", "em", "kk", "sq", "t"))
        (s_up, s_mix, s_step, s_tanh, s_upb, s_x, s_sg, s_v, s_sq, s_sum, s_exp, s_fin, s_pool, s_bon, s_norm) = (
            sem(n) for n in ("up_landed", "mix", "step", "tanh", "upb", "x", "sg", "v", "sq", "sum", "exp", "fin", "pool", "bon", "norm"))
        xw, xa, sums, bsum = (S.ps[:, 2 * j:2 * j + 2, :] for j in range(4))
        with nc.Block() as block:
            @block.sync
            def _(sp):
                sp.dma_start(up[:, :], A["decay_a_up"]).then_inc(s_up, 16)
                sp.wait_ge(s_up, 16)

            @block.vector
            def _(dve):
                with dve.Fori(0, MIXED) as i:
                    step = Chain(dve, s_mix, i * 2)
                    ub = blk(u, i)
                    nc.vector.tensor_scalar(d[:, 0, 0:1], ub[:, 0:1], -1.0, None, ALU.mult)
                    step(nc.vector.tensor_tensor(d[:, 0, 1:SEQ], ub[:, 0:SEQ - 1], ub[:, 1:SEQ], ALU.subtract))
                    step(nc.vector.scalar_tensor_tensor(ub, d[:, 0, :], dcol(S, "rwkv_mu_2", i), ub, ALU.mult, ALU.add))
                nc.vector.sem_inc(s_step, 1)
                with dve.Fori(0, RWKV_P) as b:
                    step = Chain(dve, s_v, b * VSTEPS)
                    r, rk = blk(u, b + RR), blk(u, b + RK)
                    dve.wait_ge(s_fin, b)
                    step(nc.vector.tensor_scalar(kk[:, :], rk, dcol(S, "rwkv_k_k_2", b), None, ALU.mult))
                    dve.wait_ge(s_sg, b * 2 + 1)
                    step(nc.vector.tensor_tensor_scan(cum[:, :], S.scan[:, :], sg[:, :], 0.0, ALU.mult, ALU.add))
                    step(nc.vector.tensor_tensor(em[:, :], cum[:, :], sg[:, :], ALU.subtract))
                    dve.wait_ge(s_norm, b + 1)
                    step(nc.vector.tensor_scalar(sq[:, :], sq[:, :], 1e-12, None, ALU.max))
                    step(nc.vector.reciprocal(sq[:, :], sq[:, :]))
                    step(nc.vector.tensor_tensor(kk[:, :], kk[:, :], sq[:, :], ALU.mult))
                    dve.wait_ge(s_sg, b * 2 + 2)
                    step(nc.vector.tensor_scalar(t[:, :], a[:, :], -1.0, dcol(S, "rwkv_k_a_2", b), ALU.add, ALU.mult))
                    step(nc.vector.scalar_tensor_tensor(t[:, :], t[:, :], 1.0, rk, ALU.add, ALU.mult))
                    step(nc.vector.scalar_tensor_tensor(sq[:, :], r, dcol(S, "rwkv_r_k_2", b), t[:, :], ALU.mult, ALU.mult))
                    dve.wait_ge(s_exp, b * 3 + 3)
                    nc.vector.tensor_copy(blk(plast, b), ep[:, SUB - 1::SUB])
                    step(nc.vector.tensor_tensor(r, r, ep[:, :], ALU.mult))
                    step(nc.vector.tensor_tensor(rk, t[:, :], en[:, :], ALU.mult))
                    dve.wait_ge(s_bon, b + 1)
                    step(nc.vector.tensor_tensor(fm(blk(bonus, b), 2), bsum, fm(blk(u, b + RV), 2), ALU.mult))

            @block.gpsimd
            def _(pool):
                with pool.Fori(0, RWKV_P) as b:
                    lone_wait(S, pool, s_v, b * VSTEPS + 6)
                    lone_wait(S, pool, s_exp, b * 3 + 3)
                    nc.gpsimd.tensor_tensor(blk(kap, b), kk[:, :], em[:, :], ALU.mult)
                    nc.gpsimd.tensor_tensor(kk[:, :], kk[:, :], a[:, :], ALU.mult).then_inc(s_pool, 1)
                    lone_wait(S, pool, s_pool, b + 1)
                    nc.gpsimd.tensor_tensor(blk(bt, b), kk[:, :], en[:, :], ALU.mult).then_inc(s_fin, 1)

            @block.tensor
            def _(pe):
                with pe.Fori(0, RWKV_P) as b:
                    pe.wait_ge(s_upb, b + 1)
                    for n in range(2):
                        cols = slice(n * BANK, (n + 1) * BANK)
                        nc.tensor.matmul(xw[:, n, :], upb[0:HD, :], u[0:HD, RWA, cols], start=True, stop=True)
                        last = nc.tensor.matmul(xa[:, n, :], upb[HD:P, :], u[HD:P, RWA, cols], start=True, stop=True)
                    last.then_inc(s_x, 1)
                    pe.wait_ge(s_sq, b + 1)
                    for n in range(2):
                        last = nc.tensor.matmul(sums[:, n, :], S.same[:, :], sq[:, n * BANK:(n + 1) * BANK], start=True, stop=True)
                    last.then_inc(s_sum, 1)
                    pe.wait_ge(s_v, b * VSTEPS + 9)
                    for n in range(2):
                        last = nc.tensor.matmul(bsum[:, n, :], S.same[:, :], sq[:, n * BANK:(n + 1) * BANK], start=True, stop=True)
                    last.then_inc(s_bon, 1)

            @block.scalar
            def _(act):
                act.wait_ge(s_up, 16)
                act.wait_ge(s_step, 1)
                nc.scalar.activation(u[0:HD, RWA, :], u[0:HD, RWA, :], ACT.Tanh).then_inc(s_tanh, 1)
                act.wait_ge(s_tanh, 1)
                with act.Fori(0, RWKV_P) as b:
                    act.wait_ge(s_x, b)
                    nc.scalar.activation(upb[:, :], up[:, bass.ds(b * P, P)], ACT.Copy).then_inc(s_upb, 1)
                    act.wait_ge(s_v, b * VSTEPS + 1)
                    nc.scalar.activation(sq[:, :], kk[:, :], ACT.Square).then_inc(s_sq, 1)
                    act.wait_ge(s_sum, b + 1)
                    nc.scalar.activation(fm(sq[:, :], 2), sums, ACT.Sqrt).then_inc(s_norm, 1)
                    act.wait_ge(s_x, b + 1)
                    act.wait_ge(s_fin, b)
                    nc.scalar.activation(fm(sg[:, :], 2), xw, ACT.Sigmoid, bias=dcol(S, "rwkv_w0_2", b)).then_inc(s_sg, 1)
                    nc.scalar.activation(fm(a[:, :], 2), xa, ACT.Sigmoid, bias=dcol(S, "rwkv_a0_2", b)).then_inc(s_sg, 1)
                    act.wait_ge(s_v, b * VSTEPS + 3)
                    nc.scalar.activation(ep[:, :], cum[:, :], ACT.Exp, scale=-DECAY).then_inc(s_exp, 1)
                    nc.scalar.activation(en[:, :], cum[:, :], ACT.Exp, scale=DECAY).then_inc(s_exp, 1)
                    nc.scalar.activation(em[:, :], em[:, :], ACT.Exp, scale=-DECAY).then_inc(s_exp, 1)


def rwkv_units_phase(nc, S, u, kap, bt, plast):
    H = RWKV_H
    KAP, RT, BT, KT, VV = range(5)
    with Phase(nc) as ctx:
        sb = lambda n, shape: ctx.enter_context(nc.sbuf_tensor("ru_" + n, shape, F32))
        sem = lambda n: ctx.semaphore("ru_" + n)
        fx = sb("fm", [P, 5, RWKV_P, P])
        tok = sb("tok", [P, 3, RWKV_P, 2, HD])
        z = sb("kk_akv", [P, H, 2, HD])
        ab, rb, ak, rkm = (sb(n, [P, H, P]) for n in ("ab", "rb", "ak", "rk"))
        am = sb("a_level", [P, 2, H, P])
        x, xt, t1, first = (sb(n, [P, H, P]) for n in ("x", "xt", "t1", "a_first"))
        nw = sb("removed", [P, H, 2, HD])
        g = sb("g", [P, 2, RWKV_P, HD])
        rr = sb("rr", [P, RWKV_P, P])
        st = sb("state", [P, RWKV_P, HD])
        eye2 = sb("eye2", [P, HD])
        (s_in, s_am, s_tr, s_ab, s_ak, s_l0, s_akv, s_t1, s_dx, s_w, s_g, s_rr, s_gs, s_zero,
         s_tokb, s_abm, s_first, s_rbm, s_akm, s_rkm, s_x, s_z, s_gc, s_rrc, s_state, s_tokv, s_t1c, s_nw, s_y) = (sem(n) for n in (
            "in", "am", "tr", "ab", "ak", "l0", "akv", "t1", "dx", "w", "g", "rr", "gs", "zero",
            "tokb", "abm", "first", "rbm", "akm", "rkm", "x", "z", "gc", "rrc", "state", "tokv", "t1c", "nw", "y"))
        two = [S.ps[:, 2 * j:2 * j + 2, :].rearrange("p a n -> p (a n)") for j in range(4)]
        heads = lambda ap: ap.rearrange("p (h n) -> p h n", h=H)
        mask = lambda m: m.unsqueeze(1).to_broadcast([P, H, P])
        akv_ps, rr_ps, y_ps = (S.ps[:, b, :] for b in (6, 4, 5))
        g_ps, h_ps = [S.ps[:, k, 0:4 * HD] for k in range(2)], [S.ps[:, 2 + k, 0:4 * HD] for k in range(2)]
        HEADS_BY_BLOCK = [a * RWKV_P + q for q in range(RWKV_P) for a in range(2)]
        half = lambda h: slice((h // RWKV_P) * HD, (h // RWKV_P + 1) * HD)
        first_in_bank, last_in_bank = (lambda h: h % RWKV_P == 0), (lambda h: h % RWKV_P == RWKV_P - 1)
        by_half = lambda ap: ap.rearrange("p (q a n) -> p a q n", q=RWKV_P, a=2)
        NL = len(LEVELS)
        with nc.Block() as block:
            @block.gpsimd
            def _(pool):
                nc.gpsimd.memset(st[:, :, :], 0.0).then_inc(s_zero, 1)
                nc.gpsimd.tensor_tensor(eye2[:, :], S.ident[:, 0:HD], S.ident[:, HD:P], ALU.add).then_inc(s_zero, 1)
                with pool.Fori(0, NUNIT) as c:
                    lone_wait(S, pool, s_y, c)
                    at = bass.ds(c * P, P)
                    for j, src in ((KAP, kap[:, :, at]), (RT, u[:, RR:RR + RWKV_P, at]), (BT, bt[:, :, at]),
                                   (KT, u[:, RK:RK + RWKV_P, at]), (VV, u[:, RV:RV + RWKV_P, at])):
                        last = nc.gpsimd.tensor_copy(fx[:, j, :, :], src)
                    last.then_inc(s_in, 1)
                    lone_wait(S, pool, s_abm, c + 1)
                    for l in LEVELS:
                        if l > 2:
                            lone_wait(S, pool, s_t1, c * NL + (l - 2))
                        nc.gpsimd.tensor_tensor(am[:, l % 2, :, :], ab[:, :, :], mask(S.levels[:, l, :]), ALU.mult).then_inc(s_am, 1)

            @block.tensor
            def _(pe):
                with pe.Fori(0, NUNIT) as c:
                    pe.wait_ge(s_in, c + 1)
                    pe.wait_ge(s_state, c * 2)
                    for j, (kind, out) in enumerate(((KAP, two[0][:, 0:BANK]), (BT, two[0][:, BANK:]), (KT, two[1][:, 0:BANK]), (VV, two[1][:, BANK:]))):
                        for p in range(RWKV_P):
                            last = nc.tensor.transpose(out[:, p * P:(p + 1) * P], fx[:, kind, p, :], S.ident[:, :])
                    last.then_inc(s_tr, 1)
                    for kind, out in ((KAP, two[2]), (RT, two[3])):
                        for h in HEADS_BY_BLOCK:
                            last = nc.tensor.matmul(out[:, h * P:(h + 1) * P], fx[half(h), BT, h % RWKV_P, :], fx[half(h), kind, h % RWKV_P, :],
                                                    start=True, stop=True)
                    last.then_inc(s_ab, 1)
                    lone_wait(S, pe, s_tokb, c + 1)
                    lone_wait(S, pe, s_tokv, c + 1)
                    for kind, out in ((KAP, two[0]), (RT, two[1])):
                        for h in HEADS_BY_BLOCK:
                            last = nc.tensor.matmul(out[:, h * P:(h + 1) * P], fx[half(h), KT, h % RWKV_P, :], fx[half(h), kind, h % RWKV_P, :],
                                                    start=True, stop=True)
                    last.then_inc(s_ak, 1)
                    pe.wait_ge(s_first, c + 1)
                    for h in HEADS_BY_BLOCK:
                        last = nc.tensor.transpose(two[2][:, h * P:(h + 1) * P], first[:, h, :], S.ident[:, :])
                    last.then_inc(s_l0, 1)
                    lone_wait(S, pe, s_akm, c + 1)
                    lone_wait(S, pe, s_rbm, c + 1)
                    for h in HEADS_BY_BLOCK:
                        last = nc.tensor.matmul(akv_ps[:, h * HD:(h + 1) * HD], ak[:, h, :], tok[:, 2, h % RWKV_P, h // RWKV_P, :], start=True, stop=True)
                    last.then_inc(s_akv, 1)
                    for l in LEVELS:
                        pe.wait_ge(s_am, c * NL + l)
                        pe.wait_ge(s_x, c * (NL + 1) + l)
                        for h in HEADS_BY_BLOCK:
                            last = nc.tensor.matmul(two[0][:, h * P:(h + 1) * P], am[:, l % 2, h, :], x[:, h, :], start=True, stop=True)
                        last.then_inc(s_t1, 1)
                        pe.wait_ge(s_t1c, c * NL + l)
                        if l == LEVELS[0]:
                            pe.wait_ge(s_z, c + 1)
                        if l != LEVELS[-1]:
                            for h in HEADS_BY_BLOCK:
                                nc.tensor.matmul(two[2][:, h * P:(h + 1) * P], xt[:, h, :], t1[:, h, :], start=True, stop=True)
                        for h in HEADS_BY_BLOCK:
                            last = nc.tensor.matmul(two[3][:, h * P:(h + 1) * P], t1[:, h, :], xt[:, h, :], start=True, stop=True)
                        last.then_inc(s_dx, 1)
                    pe.wait_ge(s_x, (c + 1) * (NL + 1))
                    for h in HEADS_BY_BLOCK:
                        last = nc.tensor.matmul(two[0][:, h * P:(h + 1) * P], xt[:, h, :], z[:, h, :, :].rearrange("p a n -> p (a n)"),
                                                start=True, stop=True)
                    last.then_inc(s_w, 1)
                    lone_wait(S, pe, s_nw, c + 1)
                    lone_wait(S, pe, s_rkm, c + 1)
                    for k in range(2):
                        i = slice(k * SUB, (k + 1) * SUB)
                        for h in HEADS_BY_BLOCK:
                            o = slice((h % RWKV_P) * HD, (h % RWKV_P + 1) * HD)
                            last = nc.tensor.matmul(g_ps[k][half(h), o], nw[i, h, 0, :], tok[i, 0, h % RWKV_P, h // RWKV_P, :], start=True, stop=True)
                    last.then_inc(s_g, 1)
                    for k in range(2):
                        i = slice(k * SUB, (k + 1) * SUB)
                        for h in HEADS_BY_BLOCK:
                            o = slice((h % RWKV_P) * HD, (h % RWKV_P + 1) * HD)
                            nc.tensor.matmul(h_ps[k][half(h), o], tok[i, 1, h % RWKV_P, h // RWKV_P, :], tok[i, 2, h % RWKV_P, h // RWKV_P, :], start=first_in_bank(h), stop=False)
                            nc.tensor.matmul(h_ps[k][half(h), o], tok[i, 0, h % RWKV_P, h // RWKV_P, :], nw[i, h, 1, :], start=False, stop=False)
                    for h in HEADS_BY_BLOCK:
                        o = slice((h % RWKV_P) * P, (h % RWKV_P + 1) * P)
                        nc.tensor.matmul(y_ps[half(h), o], tok[:, 2, h % RWKV_P, h // RWKV_P, :], rkm[:, h, :], start=first_in_bank(h), stop=False)
                        nc.tensor.matmul(y_ps[half(h), o], nw[:, h, 1, :], rb[:, h, :], start=False, stop=False)
                    for h in HEADS_BY_BLOCK:
                        last = nc.tensor.matmul(rr_ps[half(h), (h % RWKV_P) * P:(h % RWKV_P + 1) * P], nw[:, h, 0, :], rb[:, h, :], start=True, stop=True)
                    last.then_inc(s_rr, 1)
                    lone_wait(S, pe, s_gc, c + 1)
                    lone_wait(S, pe, s_rrc, c + 1)
                    for k in range(2):
                        lone_wait(S, pe, s_state, c * 2 + k)
                        for h in HEADS_BY_BLOCK:
                            o = slice((h % RWKV_P) * P + k * SUB, (h % RWKV_P) * P + (k + 1) * SUB)
                            nc.tensor.matmul(y_ps[half(h), o], st[half(h), h % RWKV_P, :], rr[half(h), h % RWKV_P, k * SUB:(k + 1) * SUB],
                                             start=False, stop=(k == 1 and last_in_bank(h)))
                        for h in HEADS_BY_BLOCK:
                            o = slice((h % RWKV_P) * HD, (h % RWKV_P + 1) * HD)
                            last = nc.tensor.matmul(h_ps[k][half(h), o], g[half(h), k, h % RWKV_P, :], st[half(h), h % RWKV_P, :], start=False, stop=last_in_bank(h))
                        last.then_inc(s_gs, 1)

            @block.vector
            def _(dve):
                dve.wait_ge(s_zero, 2)
                with dve.Fori(0, NUNIT) as c:
                    dve.wait_ge(s_tr, c + 1)
                    nc.vector.tensor_copy(z[:, :, 0, :].rearrange("p (a q) n -> p a q n", a=2), by_half(two[0][:, 0:BANK]))
                    nc.vector.tensor_copy(tok[:, 0, :, :, :].rearrange("p q a n -> p (q a n)"), two[0][:, BANK:]).then_inc(s_tokb, 1)
                    dve.wait_ge(s_ab, c + 1)
                    nc.vector.tensor_tensor(ab[:, :, :], heads(two[2]), mask(S.excl[:, :]), ALU.mult).then_inc(s_abm, 1)
                    nc.vector.tensor_tensor(rb[:, :, :], heads(two[3]), mask(S.incl[:, :]), ALU.mult).then_inc(s_rbm, 1)
                    dve.wait_ge(s_abm, c + 1)
                    nc.vector.tensor_tensor(first[:, :, :], ab[:, :, :], mask(S.levels[:, 0, :]), ALU.mult).then_inc(s_first, 1)
                    dve.wait_ge(s_ak, c + 1)
                    nc.vector.tensor_tensor(ak[:, :, :], heads(two[0]), mask(S.excl[:, :]), ALU.mult).then_inc(s_akm, 1)
                    nc.vector.tensor_tensor(rkm[:, :, :], heads(two[1]), mask(S.incl[:, :]), ALU.mult).then_inc(s_rkm, 1)
                    dve.wait_ge(s_first, c + 1)
                    nc.vector.scalar_tensor_tensor(xt[:, :, :], first[:, :, :], -1.0, mask(S.ident[:, :]), ALU.mult, ALU.add)
                    dve.wait_ge(s_l0, c + 1)
                    nc.vector.scalar_tensor_tensor(x[:, :, :], heads(two[2]), -1.0, mask(S.ident[:, :]), ALU.mult, ALU.add).then_inc(s_x, 1)
                    dve.wait_ge(s_akv, c + 1)
                    nc.vector.tensor_copy(z[:, :, 1, :], akv_ps.rearrange("p (h n) -> p h n", h=H)).then_inc(s_z, 1)
                    for l in LEVELS:
                        dve.wait_ge(s_x, c * (NL + 1) + l)
                        dve.wait_ge(s_dx, c * NL + l)
                        if l != LEVELS[-1]:
                            nc.vector.tensor_tensor(x[:, :, :], x[:, :, :], heads(two[2]), ALU.subtract)
                        nc.vector.tensor_tensor(xt[:, :, :], xt[:, :, :], heads(two[3]), ALU.subtract).then_inc(s_x, 1)
                    dve.wait_ge(s_g, c + 1)
                    for k in range(2):
                        last = nc.vector.tensor_tensor(g[:, k, :, :], g_ps[k].rearrange("p (q n) -> p q n", q=RWKV_P),
                                                       eye2[:, :].unsqueeze(1).to_broadcast([P, RWKV_P, HD]), ALU.add)
                    last.then_inc(s_gc, 1)
                    dve.wait_ge(s_rr, c + 1)
                    nc.vector.tensor_tensor(rr[:, :, :], rr_ps.rearrange("p (q n) -> p q n", q=RWKV_P), fx[:, RT, :, :], ALU.add).then_inc(s_rrc, 1)
                    for k in range(2):
                        dve.wait_ge(s_gs, c * 2 + (k + 1))
                        nc.vector.tensor_tensor(st[:, :, :], h_ps[k].rearrange("p (q n) -> p q n", q=RWKV_P),
                                                plast[:, :, bass.ds(c * 2 + k, 1)].to_broadcast([P, RWKV_P, HD]), ALU.mult).then_inc(s_state, 1)

            @block.scalar
            def _(act):
                with act.Fori(0, NUNIT) as c:
                    act.wait_ge(s_tr, c + 1)
                    act.wait_ge(s_state, c * 2)
                    nc.scalar.activation(tok[:, 1:3, :, :, :].rearrange("p j q a n -> p (j q a n)"), two[1], ACT.Copy).then_inc(s_tokv, 1)
                    for l in LEVELS:
                        act.wait_ge(s_t1, c * NL + l)
                        nc.scalar.activation(t1[:, :, :], heads(two[0]), ACT.Copy).then_inc(s_t1c, 1)
                    act.wait_ge(s_w, c + 1)
                    nc.scalar.activation(nw[:, :, :, :].rearrange("p h a n -> p (h a n)"), two[0], ACT.Copy, scale=-1.0).then_inc(s_nw, 1)
                    act.wait_ge(s_gs, c * 2 + 2)
                    nc.scalar.activation(u[:, RR:RR + RWKV_P, bass.ds(c * P, P)], y_ps.rearrange("p (q n) -> p q n", q=RWKV_P),
                                         ACT.Copy).then_inc(s_y, 1)


def rwkv_finish_phase(nc, S, u, bonus, mhi, mlo):
    with Phase(nc) as ctx:
        sb = lambda n: ctx.enter_context(nc.sbuf_tensor("rf_" + n, [P, SEQ], F32))
        sem = lambda n: ctx.semaphore("rf_" + n)
        dev, sq, rs = sb("dev"), sb("sq"), sb("rs")
        s_gate, s_mean, s_v, s_sq, s_var, s_rt, s_hi, s_lo = (sem(n) for n in ("gate", "mean", "v", "sq", "var", "rt", "hi", "lo"))
        mean, var = S.ps[:, 0:2, :], S.ps[:, 2:4, :]
        V = 5
        with nc.Block() as block:
            @block.scalar
            def _(act):
                nc.scalar.activation(u[:, RG:RG + RWKV_P, :], u[:, RG:RG + RWKV_P, :], ACT.Silu).then_inc(s_gate, 1)
                with act.Fori(0, RWKV_P) as b:
                    act.wait_ge(s_v, b * V + 1)
                    nc.scalar.activation(sq[:, :], dev[:, :], ACT.Square).then_inc(s_sq, 1)
                    act.wait_ge(s_var, b + 1)
                    nc.scalar.activation(fm(rs[:, :], 2), var, ACT.Sqrt, scale=1.0 / HD, bias=S.gn_eps[:, 0:1]).then_inc(s_rt, 1)
                    act.wait_ge(s_v, b * V + 5)
                    nc.scalar.activation(blk(mhi, b + RWKV_P), dev[:, :], ACT.Copy).then_inc(s_hi, 1)

            @block.tensor
            def _(pe):
                with pe.Fori(0, RWKV_P) as b:
                    pe.wait_ge(s_v, b * V)
                    for n in range(2):
                        last = nc.tensor.matmul(mean[:, n, :], S.same[:, :], blk(u, b + RR)[:, n * BANK:(n + 1) * BANK], start=True, stop=True)
                    last.then_inc(s_mean, 1)
                    pe.wait_ge(s_sq, b + 1)
                    for n in range(2):
                        last = nc.tensor.matmul(var[:, n, :], S.same[:, :], sq[:, n * BANK:(n + 1) * BANK], start=True, stop=True)
                    last.then_inc(s_var, 1)

            @block.vector
            def _(dve):
                dve.wait_ge(s_gate, 1)
                with dve.Fori(0, RWKV_P) as b:
                    step = Chain(dve, s_v, b * V)
                    dve.wait_ge(s_mean, b + 1)
                    dve.wait_ge(s_lo, b)
                    step(nc.vector.scalar_tensor_tensor(fm(dev[:, :], 2), mean, -1.0 / HD, fm(blk(u, b + RR), 2), ALU.mult, ALU.add))
                    dve.wait_ge(s_rt, b + 1)
                    step(nc.vector.reciprocal(rs[:, :], rs[:, :]))
                    step(nc.vector.scalar_tensor_tensor(dev[:, :], dev[:, :], dcol(S, "rwkv_ln_w_2", b), rs[:, :], ALU.mult, ALU.mult))
                    step(nc.vector.scalar_tensor_tensor(dev[:, :], dev[:, :], dcol(S, "rwkv_ln_b_2", b), blk(bonus, b), ALU.add, ALU.add))
                    step(nc.vector.tensor_tensor(dev[:, :], dev[:, :], blk(u, b + RG), ALU.mult))

            @block.gpsimd
            def _(pool):
                with pool.Fori(0, RWKV_P) as b:
                    lone_wait(S, pool, s_hi, b + 1)
                    nc.gpsimd.tensor_tensor(blk(mlo, b + RWKV_P), dev[:, :], blk(mhi, b + RWKV_P), ALU.subtract).then_inc(s_lo, 1)



def scratch(nc, name, shape, dt=F32):
    return nc.dram_tensor(name, shape, dt, kind="Internal").ap()


def second_layer(nc, S, A, out):
    h = S.h[:, :, META:T]
    parked_h = scratch(nc, "parked_h", (P, DB, SEQ))
    parked_gla = [scratch(nc, n, (P, GLA_HEADS, SEQ), F16) for n in ("parked_gla_hi", "parked_gla_lo")]
    with ExitStack() as ctx:
        sb = lambda e, n, shape, dt=F32, **kw: e.enter_context(nc.sbuf_tensor(n, shape, dt, **kw))
        S.same, S.incl, S.excl = (sb(ctx, n, [P, P]) for n in ("same_chunk", "incl", "excl"))
        S.scan, S.levels = sb(ctx, "scan_starts", [P, SEQ]), sb(ctx, "levels", [P, NLEVEL, P])
        masks_phase(nc, S)
        store_phase(nc, parked_h, h, "h_out")
        inp = ExitStack()
        S.xhi, S.xlo = (sb(inp, n, [P, DB, SEQ], F16, side="right") for n in ("second_x_hi", "second_x_lo"))
        norm_phase(nc, S, "second", h, "norm_w_2", DB, SEQ, ("cut", S.xhi, S.xlo), 2, BANK)
        with ExitStack() as gla:
            m1 = [sb(gla, n, [P, GLA_HEADS, SEQ], F16) for n in ("gla_hi", "gla_lo")]
            u = sb(gla, "gla_u", [P, GLA_B, SEQ])
            linear_phase(nc, S, A["w_gla"], DB, normed(S), GLA_B, u, "gla", 2, BANK)
            with ExitStack() as e:
                qi, ki, kst = (sb(e, n, [P, 2, SEQ]) for n in ("gla_qi", "gla_ki", "gla_kst"))
                dec = sb(e, "gla_dec", [P, 2, NSUB])
                gla_prepare_phase(nc, S, A, u, qi, ki, kst, dec)
                gla_units_phase(nc, S, u, qi, ki, kst, dec)
            gla_finish_phase(nc, S, u, *m1)
            for n in range(2):
                store_phase(nc, parked_gla[n], m1[n][:, :, :], f"gla_out{n}")
        with ExitStack() as rwkv:
            u = sb(rwkv, "rwkv_u", [P, RWKV_B, SEQ])
            linear_phase(nc, S, A["w_rwkv"], DB, normed(S), RWKV_B, u, "rwkv", 2, BANK)
            inp.close()
            S.free_h()
            plast = sb(rwkv, "rwkv_last", [P, RWKV_P, NSUB])
            bonus = sb(rwkv, "rwkv_bonus", [P, RWKV_P, SEQ])
            with ExitStack() as e:
                kap, bt = (sb(e, n, [P, RWKV_P, SEQ]) for n in ("rwkv_kap", "rwkv_bt"))
                rwkv_prepare_phase(nc, S, A, u, kap, bt, bonus, plast)
                rwkv_units_phase(nc, S, u, kap, bt, plast)
            m = [sb(ctx, n, [P, 2 * RWKV_P, SEQ], F16, side="right") for n in ("merged_hi", "merged_lo")]
            rwkv_finish_phase(nc, S, u, bonus, *m)
        for n in range(2):
            store_phase(nc, m[n][:, 0:GLA_HEADS, :], parked_gla[n], f"gla_back{n}")
        back = sb(ctx, "h_back", [P, DB, SEQ])
        store_phase(nc, back[:, :, :], parked_h, "h_back")
        linear_phase(nc, S, A["w_out_2"], DB, lambda k: (m[0][:, k, :], m[1][:, k, :]), DB, back, "out2", 2, BANK, plus=back)
        res = sb(ctx, "result_fm", [P, DB, SEQ])
        norm_phase(nc, S, "final", back, "final_norm_w_2", DB, SEQ, ("to", res), 2, BANK)
        store_phase(nc, out, res[:, :, :], "result")



def persistent(nc, ctx, S):
    sb = lambda n, shape, dt=F32: ctx.enter_context(nc.sbuf_tensor(n, shape, dt))
    S.cols = sb("params", [P, NCOL])
    S.ones = sb("ones", [P, P])
    S.ident = sb("ident", [P, P])
    S.upper = sb("upper", [P, P])
    S.strict = sb("strict", [P, P])
    S.tri8 = sb("tri8", [P, P])
    S.ones8 = sb("ones8", [P, P])
    S.eps = sb("eps", [P, 1])
    S.gn_eps = sb("gn_eps", [P, 1])
    S.waited = ctx.enter_context(nc.semaphore("waited"))
    S.ps = ctx.enter_context(nc.psum_tensor("ps", [P, 8, BANK], F32))


def program(nc, A, out):
    with ExitStack() as ctx:
        S = Names()
        Phase.cleared.clear()
        persistent(nc, ctx, S)
        constants_phase(nc, S, A)
        with ExitStack() as mix:
            sb = lambda n, shape, dt=F32: mix.enter_context(nc.sbuf_tensor(n, shape, dt))
            S.z = sb("z", [P, DB, TP])
            with ExitStack() as inp:
                S.xhi, S.xlo = (inp.enter_context(nc.sbuf_tensor(n, [P, DB, TW], F16)) for n in ("x_hi", "x_lo"))
                with nc.sbuf_tensor("h_in", [P, DB, TW], F32) as h:
                    S.h = h
                    load_h_phase(nc, S, A, "in")
                    norm_phase(nc, S, "mix_pre", S.h, "mix_pre_g", DB, TW, ("cut", S.xhi, S.xlo))
                with ExitStack() as ssd:
                    S.xbc = ssd.enter_context(nc.sbuf_tensor("xbc", [P, XBC_B, TP], F32))
                    S.dt = ssd.enter_context(nc.sbuf_tensor("dt", [HEADS, 2, TP], F32))
                    xbc_phase(nc, S, A)
                    z_dt_phase(nc, S, A)
                    ssd_phase(nc, S)
                y1_scope = ExitStack()
                y1 = [y1_scope.enter_context(nc.sbuf_tensor(n, [P, DB, TW], F16, side="right")) for n in ("y_ssd_hi", "y_ssd_lo")]
                norm_phase(nc, S, "ssd", S.z, "ssd_norm_g", DB, TW, ("cut", *y1))
                with ExitStack() as att:
                    S.qk = att.enter_context(nc.sbuf_tensor("qk", [P, 2 * HALF, TW], F16))
                    S.v2 = att.enter_context(nc.sbuf_tensor("v2", [P, NCH, HALF, P], F16))
                    for half in range(2):
                        qkv_phase(nc, S, A, half)
                        attention_phase(nc, S, half)
            y2 = [sb(n, [P, DB, TW], F16) for n in ("y_sb_hi", "y_sb_lo")]
            norm_phase(nc, S, "sb", S.z, "sb_norm_g", DB, TW, ("cut", *y2))
            mixed = S.z[:, :, 0:TW]
            linear_phase(nc, S, A["w_out"], 2 * DB, lambda k: tuple(y[:, k % DB, :] for y in ((y1, y2)[k // DB])), DB, mixed, "out")
            y1_scope.close()
            h_scope = ExitStack()
            S.h = h_scope.enter_context(nc.sbuf_tensor("h", [P, DB, TW], F32, side="right"))
            S.free_h = h_scope.close
            load_h_phase(nc, S, A, "again")
            norm_phase(nc, S, "mix_post", mixed, "mix_post_g", DB, TW, ("add", S.h))
        ffn(nc, S, A)
        second_layer(nc, S, A, out)



def lay_out(inputs):
    import numpy as np
    get = lambda n: np.ascontiguousarray(np.asarray(inputs[n]))
    cols = np.zeros((P, NCOL), np.float32)

    def put(name, a, per=1):
        at, n = _COLS[name]
        cols[:a.shape[0], at:at + n] = a

    feature = lambda a: np.ascontiguousarray(a.reshape(-1, P).T)
    taps = lambda a: np.ascontiguousarray(a.reshape(a.shape[0], -1, P).transpose(2, 1, 0).reshape(P, -1))
    for name in _COLS:
        a = get(name)
        if name in ("ssd_conv_w", "ffn_conv_w"):
            put(name, taps(a[0]))
        elif name == "ssd_d":
            put(name, np.repeat(a[0].reshape(PAIRS, 2).T, HD, axis=0))
        elif name in ("ssd_dt_bias", "ssd_a_log"):
            put(name, a.reshape(-1, 1))
        else:
            put(name, feature(a.reshape(-1)))

    def blocks(w):
        k, n = w.shape
        return np.ascontiguousarray(w.reshape(k // P, P, n // P, P).transpose(2, 1, 0, 3)).reshape(n // P, P, k)

    w_in = get("w_in")[0]
    z0, x0, d0, q0, k0, v0, end = 0, 1024, 2560, 2576, 3600, 4624, 5648
    zw = np.concatenate([w_in[:, z0:x0], w_in[:, d0:d0 + P], w_in[:, d0:d0 + P]], axis=1)
    halves = [w_in[:, o + 512 * g:o + 512 * (g + 1)] for g in range(2) for o in (q0, k0, v0)]
    w_up = get("w_up")[0].reshape(D, 2, FFB, P)
    w2 = get("w_in_2")[0]
    h = np.concatenate([get("meta_tokens"), get("x")[0]], axis=0)
    return {
        "hT": np.ascontiguousarray(h.T.reshape(DB, P, T).transpose(1, 0, 2)),
        "cols": cols,
        "w_in": blocks(w_in[:, 0:d0]),
        "w_z": blocks(zw),
        "w_qkv": blocks(np.concatenate(halves, axis=1)),
        "w_out": blocks(get("w_out")[0]),
        "w_up": blocks(np.ascontiguousarray(w_up.transpose(0, 2, 1, 3)).reshape(D, -1)),
        "w_down": blocks(get("w_down")[0]),
        "w_gla": blocks(np.concatenate([w2[:, 0:1024], w2[:, 1040:1552], w2[:, 1024:1152], w2[:, 1024:1152]], axis=1)),
        "w_rwkv": blocks(np.concatenate([w2[:, 1552:3728], w2[:, 3600:3728]], axis=1)),
        "w_out_2": blocks(get("w_out_2")[0]),
        "gate_up": get("gla_gate_up_2")[0],
        "decay_a_up": np.concatenate([get("rwkv_w_up_2")[0], get("rwkv_a_up_2")[0]], axis=0),
    }


def kernel(**inputs):
    import numpy as np
    import concourse.bacc as bacc
    from concourse.bass_utils import run_bass_kernel_spmd

    arrays = lay_out(inputs)
    nc = bacc.Bacc("TRN2", target_bir_lowering=False, num_devices=1)
    A = {n: nc.dram_tensor("in_" + n, a.shape, F32, kind="ExternalInput").ap() for n, a in arrays.items()}
    out = nc.dram_tensor("result", (P, DB, SEQ), F32, kind="ExternalOutput").ap()
    program(nc, A, out)
    r = run_bass_kernel_spmd(nc, [{"in_" + n: a for n, a in arrays.items()}], core_ids=[0])
    got = r.results[0]["result"]
    return np.ascontiguousarray(got.transpose(2, 1, 0)).reshape(1, SEQ, D)
```

```python
from contextlib import ExitStack
import math

import concourse.bass as bass
from concourse import mybir

F32 = mybir.dt.float32
F16 = mybir.dt.float16
U32 = mybir.dt.uint32
ALU = mybir.AluOpType
ACT = mybir.ActivationFunctionType

P = 128
D = 1024
DB = D // P
SEQ, META = 1024, 16
T = META + SEQ
BANK = 512
NT = 3
TB = 348
TW = NT * TB
NCH = 9
TP = NCH * P
HD = 64
HEADS = 16
PAIRS = HEADS // 2
XBC_B = 12
CONV = 4
FFB = 22
EPS = 1e-6
RWKV_GN_EPS = 64e-5
WSCALE = 64.0
SLOTS = 2

_COLS = {}


def _col(name, n):
    _COLS[name] = (sum(v[1] for v in _COLS.values()), n)


for _name, _n in (("mix_pre_g", 8), ("ssd_norm_g", 8), ("sb_norm_g", 8), ("mix_post_g", 8), ("ffn_pre_g", 8),
                  ("ffn_post_g", 8), ("norm_w_2", 8), ("final_norm_w_2", 8), ("ssd_conv_w", XBC_B * CONV),
                  ("ssd_conv_b", XBC_B), ("ssd_d", PAIRS), ("ssd_dt_bias", 1), ("ssd_a_log", 1),
                  ("ffn_conv_w", FFB * 3), ("ffn_conv_b", FFB), ("gla_gate_bias_2", 2), ("gla_norm_w_2", 1),
                  ("rwkv_mu_2", 13), ("rwkv_w0_2", 4), ("rwkv_a0_2", 4), ("rwkv_k_k_2", 4), ("rwkv_k_a_2", 4),
                  ("rwkv_r_k_2", 4), ("rwkv_ln_w_2", 4), ("rwkv_ln_b_2", 4)):
    _col(_name, _n)
NCOL = sum(v[1] for v in _COLS.values())


class Names:
    pass


class Phase(ExitStack):

    cleared = []

    def __init__(self, nc):
        super().__init__()
        self.nc, self.used = nc, []
        self.callback(self.clear)

    def semaphore(self, name):
        self.used.append(self.nc.alloc_semaphore(name=name))
        return self.used[-1]

    def clear(self):
        for sem in Phase.cleared:
            self.nc.release_semaphore(sem)
        for sem in self.used:
            self.nc.gpsimd.sem_clear(sem)
        Phase.cleared[:] = self.used


class Chain:

    def __init__(self, eng, sem, base=0, alone=None):
        self.eng, self.sem, self.base, self.n, self.alone = eng, sem, base, 0, alone

    def __call__(self, ins):
        self.n += 1
        ins.then_inc(self.sem, 1)
        if self.alone:
            lone_wait(self.alone, self.eng, self.sem, self.base + self.n)
        else:
            self.eng.wait_ge(self.sem, self.base + self.n)


def lone_wait(S, pool, sem, value):
    pool.wait_ge(sem, value)
    pool.sem_inc(S.waited, 1)


def col(S, name, i=0, n=1):
    at, _ = _COLS[name]
    return S.cols[:, at + i:at + i + n]


def dcol(S, name, b, per=1, j=0):
    at, _ = _COLS[name]
    return S.cols[:, bass.ds(b * per + (at + j), 1)]


def blk(t, b):
    return t[:, bass.ds(b, 1), :].rearrange("p a n -> p (a n)")



def linear_buffers(nc, ctx, w, first, kb, tag, side="left", parts=1):
    L = Names()
    L.parts = parts
    L.w, L.first, L.kb, L.fetched, L.slots_cut = w, first, kb, False, 0
    L.raw = ctx.enter_context(nc.sbuf_tensor(f"wraw_{tag}", [P, SLOTS, kb * P], F32, side=side))
    L.hi = ctx.enter_context(nc.sbuf_tensor(f"whi_{tag}", [P, SLOTS, kb * P], F16, side=side))
    L.lo = ctx.enter_context(nc.sbuf_tensor(f"wlo_{tag}", [P, SLOTS, kb * P], F16, side=side))
    L.landed = [ctx.semaphore(f"w_landed{s}_{tag}") for s in range(SLOTS)]
    L.cut = ctx.semaphore(f"w_cut_{tag}")
    L.step = ctx.semaphore(f"w_cut_step_{tag}")
    L.products = ctx.semaphore(f"products_{tag}")
    L.emptied = ctx.semaphore(f"psum_emptied_{tag}")
    return L


def fetch_first(sp, L):
    for s in range(SLOTS):
        sp.dma_start(L.raw[:, s, :], L.w[L.first + s]).then_inc(L.landed[s], 16)
    L.fetched = True


def stream_weights(sp, L, nb):
    if not L.fetched:
        fetch_first(sp, L)
    with sp.Fori(0, nb // SLOTS - 1) as i:
        for s in range(SLOTS):
            sp.wait_ge(L.cut, i * SLOTS + (s + 1))
            sp.dma_start(L.raw[:, s, :], L.w[bass.ds(i * SLOTS + (L.first + SLOTS + s), 1)]
                         .rearrange("a p n -> p (a n)")).then_inc(L.landed[s], 16)
    if nb % SLOTS:
        sp.wait_ge(L.cut, nb - SLOTS)
        sp.dma_start(L.raw[:, 0, :], L.w[L.first + nb - 1]).then_inc(L.landed[0], 16)


def cut_first(nc, S, pool, L, slots=SLOTS):
    for s in range(L.slots_cut, slots):
        step = Chain(pool, L.step, 2 * s)
        pool.wait_ge(L.landed[s], 16)
        step(nc.gpsimd.tensor_scalar(L.raw[:, s, :], L.raw[:, s, :], WSCALE, 1.0, ALU.mult, ALU.mult))
        step(nc.gpsimd.tensor_scalar(L.hi[:, s, :], L.raw[:, s, :], 1.0, 1.0, ALU.mult, ALU.mult))
        nc.gpsimd.tensor_tensor(L.lo[:, s, :], L.raw[:, s, :], L.hi[:, s, :], ALU.subtract).then_inc(L.cut, 1)
    L.slots_cut = slots


def cut_weights(nc, S, pool, L, nb):
    cut_first(nc, S, pool, L)
    def one(i, s):
        step = Chain(pool, L.step, i * (2 * SLOTS) + 2 * s, alone=S)
        lone_wait(S, pool, L.landed[s], i * 16 + 16)
        step(nc.gpsimd.tensor_scalar(L.raw[:, s, :], L.raw[:, s, :], WSCALE, 1.0, ALU.mult, ALU.mult))
        lone_wait(S, pool, L.products, i * SLOTS + (s + 1))
        step(nc.gpsimd.tensor_scalar(L.hi[:, s, :], L.raw[:, s, :], 1.0, 1.0, ALU.mult, ALU.mult))
        nc.gpsimd.tensor_tensor(L.lo[:, s, :], L.raw[:, s, :], L.hi[:, s, :], ALU.subtract).then_inc(L.cut, 1)

    with pool.Fori(1, nb // SLOTS) as i:
        for s in range(SLOTS):
            one(i, s)
    if nb % SLOTS:
        one(nb // SLOTS, 0)


def products(nc, pe, L, xs, banks, first, nb, nt=NT, tb=TB, t0=0, after=None, ready=None):
    if first == 0:
        nc.tensor.sem_inc(L.products, SLOTS)

    def one(i, s, await_input=False):
        pe.wait_ge(L.emptied, i * SLOTS + (s + 1))
        for part in range(L.parts):
            w = s if L.parts == 1 else part
            pe.wait_ge(L.cut, (i * SLOTS + s) * L.parts + (part + 1))

            def product(n, j):
                k = part * L.kb + j
                hi, lo = (x[:, w, j * P:(j + 1) * P] for x in (L.hi, L.lo))
                xhi, xlo = (x[:, t0 + n * tb:t0 + (n + 1) * tb] for x in xs(k))
                out = banks(s)[:, n, 0:tb]
                nc.tensor.matmul(out, hi, xhi, start=(k == 0), stop=False)
                nc.tensor.matmul(out, hi, xlo, start=False, stop=False)
                return nc.tensor.matmul(out, lo, xhi, start=False, stop=(k == L.parts * L.kb - 1))

            if await_input:
                for j in range(L.kb):
                    ready(pe, part * L.kb + j)
                    for n in range(nt):
                        last = product(n, j)
            else:
                for n in range(nt):
                    for j in range(L.kb):
                        last = product(n, j)
            last.then_inc(L.products, 1)
        if after:
            after(i, s)

    start = first // SLOTS
    if ready:
        for s in range(SLOTS):
            one(start, s, s == 0)
        start += 1
    with pe.Fori(start, nb // SLOTS) as i:
        for s in range(SLOTS):
            one(i, s)
    if nb % SLOTS:
        one(nb // SLOTS, 0)


def done(L, b):
    return b * L.parts + (L.parts + SLOTS)


def normed(S):
    return lambda k: (S.xhi[:, k, :], S.xlo[:, k, :])


def psum_tn(S, s):
    return S.ps[:, NT * s:NT * s + NT, :]


def fm(ap, nt=NT):
    return ap.rearrange("p (n t) -> p n t", n=nt)



def norm_cut(nc, ctx, tag, src, g, kb, width, hi, lo, side="right"):
    N = Names()
    N.src, N.g, N.kb, N.width, N.hi, N.lo = src, g, kb, width, hi, lo
    N.rs = ctx.enter_context(nc.sbuf_tensor(f"rs_{tag}", [P, width], F32, side=side))
    N.ysd, N.used, N.cut, N.cut_v = (ctx.semaphore(f"{n}_{tag}") for n in ("ys", "y_high", "y_cut", "y_cut_v"))
    return N


def by_vector(k):
    return k % 4 == 3


def cut_by_scalar(nc, act, N):
    for k in range(N.kb):
        act.wait_ge(N.ysd, k + 1)
        nc.scalar.activation(N.hi[:, k, 0:N.width], N.y[k % len(N.y)], ACT.Copy).then_inc(N.used, 1)


def slot_used(dve, N, k):
    b = k - len(N.y)
    if b >= 0 and by_vector(b):
        dve.wait_ge(N.cut_v, sum(by_vector(a) for a in range(b + 1)))
    elif b >= 0:
        dve.wait_ge(N.cut, sum(not by_vector(a) for a in range(b + 1)))


def cut_by_vector(nc, S, dve, N):
    def low(k):
        dve.wait_ge(N.used, k + 1)
        nc.vector.tensor_tensor(N.lo[:, k, 0:N.width], N.y[k % len(N.y)], N.hi[:, k, 0:N.width], ALU.subtract).then_inc(N.cut_v, 1)

    for k in range(N.kb):
        slot_used(dve, N, k)
        nc.vector.scalar_tensor_tensor(N.y[k % len(N.y)], N.src[:, k, 0:N.width], col(S, N.g, k), N.rs[:, :],
                                       ALU.mult, ALU.mult).then_inc(N.ysd, 1)
        if k >= 1 and by_vector(k - 1):
            low(k - 1)
    low(N.kb - 1)


def cut_by_pool(nc, pool, N):
    for k in range(N.kb):
        if not by_vector(k):
            pool.wait_ge(N.used, k + 1)
            nc.gpsimd.tensor_tensor(N.lo[:, k, 0:N.width], N.y[k % len(N.y)], N.hi[:, k, 0:N.width], ALU.subtract).then_inc(N.cut, 1)


def cut_ready(N, first=0):
    def ready(pe, k):
        if k >= first and by_vector(k - first):
            pe.wait_ge(N.cut_v, sum(by_vector(a) for a in range(k - first + 1)))
        elif k >= first:
            pe.wait_ge(N.cut, sum(not by_vector(a) for a in range(k - first + 1)))
    return ready


def norm_phase(nc, S, tag, src, g, kb, width, out, nt=NT, tb=TB, ahead=None, sync=None, extra=None, load=None):
    kind = out[0]
    with Phase(nc) as ctx:
        rs = out[1].rs if kind == "rs" else ctx.enter_context(nc.sbuf_tensor(f"rs_{tag}", [P, width], F32))
        YS = 4
        y = ctx.enter_context(nc.sbuf_tensor(f"y_{tag}", [P, YS, width], F32))
        sq = y[:, 2:4, :]
        sem = lambda n: ctx.semaphore(f"{n}_{tag}")
        squared, odd, paired, summed, log, root, ysd, added, added_v = (sem(n) for n in (
            "squared", "odd_squared", "paired", "summed", "log", "root", "ysd", "added", "added_v"))
        landed = [sem(f"x_landed{k}") for k in range(kb)] if load else []
        padded = sem("x_padded")

        def here(eng, k, x):
            if load and load[0] is x:
                eng.wait_ge(padded, 1)
                eng.wait_ge(landed[k], 16)

        ps = S.ps[:, 0:nt, 0:tb]
        with nc.Block() as block:
            @block.scalar
            def _(act):
                nc.scalar.preload_act_table_set("natural_log_exp_and_others")
                for j in range(kb // 2):
                    if j >= 2:
                        act.wait_ge(summed, j - 1)
                    here(act, 2 * j, src)
                    nc.scalar.activation(sq[:, j % 2, :], src[:, 2 * j, 0:width], ACT.Square).then_inc(squared, 1)
                act.wait_ge(summed, kb // 2)
                nc.scalar.activation(fm(rs[:, :], nt), ps, ACT.Ln, scale=1.0 / (kb * P), bias=S.eps[:, 0:1]).then_inc(log, 1)
                act.wait_ge(log, 1)
                nc.scalar.activation(rs[:, :], rs[:, :], ACT.Exp, scale=-0.5).then_inc(root, 1)

            @block.tensor
            def _(pe):
                for j in range(kb // 2):
                    pe.wait_ge(paired, j + 1)
                    for n in range(nt):
                        last = nc.tensor.matmul(S.ps[:, n, 0:tb], S.ones[:, :], sq[:, j % 2, n * tb:(n + 1) * tb],
                                                start=(j == 0), stop=(j == kb // 2 - 1))
                    last.then_inc(summed, 1)

            @block.vector
            def _(dve):
                if load:
                    nc.vector.memset(load[0][:, :, T:TW], 0.0).then_inc(padded, 1)
                for j in range(kb // 2):
                    here(dve, 2 * j + 1, src)
                    nc.vector.tensor_tensor(y[:, j % 2, :], src[:, 2 * j + 1, 0:width], src[:, 2 * j + 1, 0:width], ALU.mult).then_inc(odd, 1)
                    dve.wait_ge(odd, j + 1)
                    dve.wait_ge(squared, j + 1)
                    nc.vector.tensor_tensor(sq[:, j % 2, :], sq[:, j % 2, :], y[:, j % 2, :], ALU.add).then_inc(paired, 1)
                if kind == "rs":
                    return
                dve.wait_ge(root, 1)
                dve.wait_ge(paired, kb // 2)

                def add(k):
                    here(dve, k, out[1])
                    dve.wait_ge(ysd, k + 1)
                    nc.vector.tensor_tensor(out[1][:, k, 0:width], out[1][:, k, 0:width], y[:, k % YS, :], ALU.add).then_inc(added_v, 1)

                for k in range(kb):
                    if kind == "to":
                        nc.vector.scalar_tensor_tensor(out[1][:, k, 0:width], src[:, k, 0:width], col(S, g, k), rs[:, :],
                                                       ALU.mult, ALU.mult).then_inc(ysd, 1)
                        continue
                    if k >= YS and not by_vector(k - YS):
                        dve.wait_ge(added, sum(not by_vector(b) for b in range(k - YS + 1)))
                    if k >= YS and by_vector(k - YS):
                        dve.wait_ge(added_v, sum(by_vector(b) for b in range(k - YS + 1)))
                    nc.vector.scalar_tensor_tensor(y[:, k % YS, :], src[:, k, 0:width], col(S, g, k), rs[:, :],
                                                   ALU.mult, ALU.mult).then_inc(ysd, 1)
                    if kind == "add" and k >= 1 and by_vector(k - 1):
                        add(k - 1)
                if kind == "add":
                    add(kb - 1)

            if ahead or sync or load or kind == "to":
                @block.sync
                def _(sp):
                    if load:
                        for k in range(kb):
                            sp.dma_start(load[0][:, k, 0:T], load[1][:, k, :]).then_inc(landed[k], 16)
                    if ahead:
                        fetch_first(sp, ahead)
                    if kind == "to":
                        for k in range(kb):
                            sp.wait_ge(ysd, k + 1)
                            sp.dma_start(out[2][:, k, :], out[1][:, k, 0:width]).then_inc(out[3], 16)
                        sp.wait_ge(out[3], kb * 16)
                    if sync:
                        sync(sp)

            @block.gpsimd
            def _(pool):
                if extra:
                    extra(pool)
                if ahead:
                    cut_first(nc, S, pool, ahead, 1)
                if kind == "add":
                    for k in range(kb):
                        if not by_vector(k):
                            here(pool, k, out[1])
                            pool.wait_ge(ysd, k + 1)
                            nc.gpsimd.tensor_tensor(out[1][:, k, 0:width], out[1][:, k, 0:width], y[:, k % YS, :], ALU.add).then_inc(added, 1)



def constants_phase(nc, S, A):
    with Phase(nc) as ctx:
        sem = lambda n: ctx.semaphore(n)
        loaded, filled = sem("params_loaded"), sem("masks_filled")
        with nc.Block() as block:
            @block.sync
            def _(sp):
                sp.dma_start(S.cols[:, :], A["cols"]).then_inc(loaded, 16)
                sp.wait_ge(loaded, 16)

            @block.vector
            def _(dve):
                nc.vector.memset(S.ones[:, :], 1.0)
                nc.vector.memset(S.eps[:, :], EPS)
                nc.vector.memset(S.gn_eps[:, :], RWKV_GN_EPS)

            @block.gpsimd
            def _(pool):
                nc.gpsimd.memset(S.ident[:, :], 0.0).then_inc(filled, 1)
                nc.gpsimd.memset(S.upper[:, :], 1.0).then_inc(filled, 1)
                pool.wait_ge(filled, 2)
                nc.gpsimd.memset(S.strict[:, :], 1.0).then_inc(filled, 1)
                nc.gpsimd.memset(S.tri8[:, :], -8.0).then_inc(filled, 1)
                nc.gpsimd.memset(S.ones8[:, :], -8.0)
                pool.wait_ge(filled, 4)
                nc.gpsimd.affine_select(out=S.ident[:, :], in_=S.ident[:, :], compare_op=ALU.not_equal, fill=1.0,
                                        base=0, pattern=[[-1, P]], channel_multiplier=1)
                nc.gpsimd.affine_select(out=S.upper[:, :], in_=S.upper[:, :], compare_op=ALU.is_ge, fill=0.0,
                                        base=0, pattern=[[1, P]], channel_multiplier=-1)
                nc.gpsimd.affine_select(out=S.strict[:, :], in_=S.strict[:, :], compare_op=ALU.is_gt, fill=0.0,
                                        base=0, pattern=[[1, P]], channel_multiplier=-1)
                nc.gpsimd.affine_select(out=S.tri8[:, :], in_=S.tri8[:, :], compare_op=ALU.is_ge, fill=0.0,
                                        base=0, pattern=[[-1, P]], channel_multiplier=1)



def xbc_phase(nc, S, L, N, ahead):
    with Phase(nc) as ctx:
        raw = ctx.enter_context(nc.sbuf_tensor("xbc_raw", [P, SLOTS, CONV - 1 + TW], F32))
        acc = ctx.enter_context(nc.sbuf_tensor("xbc_acc", [P, SLOTS, TW], F32))
        sem = lambda n: ctx.semaphore(n)
        N.y = [raw[:, s, CONV - 1:] for s in range(SLOTS)] + [acc[:, s, :] for s in range(SLOTS)]
        zeroed, copied, conv, conv_step, silu = (sem(n) for n in ("conv_zeroed", "raw_copied", "conv_done", "conv_step", "silu_done"))
        with nc.Block() as block:
            @block.sync
            def _(sp):
                stream_weights(sp, L, XBC_B)
                fetch_first(sp, ahead)

            @block.gpsimd
            def _(pool):
                cut_by_pool(nc, pool, N)
                cut_weights(nc, S, pool, L, XBC_B)
                cut_first(nc, S, pool, ahead)
                nc.gpsimd.memset(S.xbc[:, :, TW:TP], 0.0)

            @block.tensor
            def _(pe):
                products(nc, pe, L, normed(S), lambda s: psum_tn(S, s), 0, XBC_B, ready=cut_ready(N))

            @block.scalar
            def _(act):
                nc.scalar.sem_inc(L.emptied, SLOTS)
                cut_by_scalar(nc, act, N)
                nc.scalar.preload_act_table(ACT.Silu)
                act.wait_ge(zeroed, 1)
                with act.Fori(0, XBC_B // SLOTS) as i:
                    for s in range(SLOTS):
                        act.wait_ge(L.products, done(L, i * SLOTS + s))
                        act.wait_ge(conv, i * SLOTS + (s + 1))
                        nc.scalar.activation(fm(raw[:, s, CONV - 1:]), psum_tn(S, s)[:, :, 0:TB], ACT.Copy,
                                             scale=1.0 / WSCALE).then_inc(copied, 1)
                        act.wait_ge(copied, i * SLOTS + (s + 1))
                        nc.scalar.sem_inc(L.emptied, 1)
                        act.wait_ge(conv, i * SLOTS + (s + 1 + SLOTS))
                        nc.scalar.activation(S.xbc[:, bass.ds(i * SLOTS + s, 1), 0:TW].rearrange("p a n -> p (a n)"), acc[:, s, :],
                                             ACT.Silu).then_inc(silu, 1)

            @block.vector
            def _(dve):
                cut_by_vector(nc, S, dve, N)
                nc.vector.memset(raw[:, :, 0:CONV - 1], 0.0).then_inc(zeroed, 1)
                nc.vector.sem_inc(conv, SLOTS)
                nc.vector.sem_inc(silu, SLOTS)
                with dve.Fori(0, XBC_B // SLOTS) as i:
                    for s in range(SLOTS):
                        b = i * SLOTS + s
                        step = Chain(dve, conv_step, b * (CONV - 1))
                        dve.wait_ge(copied, i * SLOTS + (s + 1))
                        dve.wait_ge(silu, i * SLOTS + (s + 1))
                        step(nc.vector.tensor_scalar(acc[:, s, :], raw[:, s, 0:TW], dcol(S, "ssd_conv_w", b, CONV, 0),
                                                     dcol(S, "ssd_conv_b", b), ALU.mult, ALU.add))
                        for j in range(1, CONV):
                            ins = nc.vector.scalar_tensor_tensor(acc[:, s, :], raw[:, s, j:j + TW], dcol(S, "ssd_conv_w", b, CONV, j),
                                                                 acc[:, s, :], ALU.mult, ALU.add)
                            if j < CONV - 1:
                                step(ins)
                            else:
                                ins.then_inc(conv, 1)


def z_dt_phase(nc, S, L):
    with Phase(nc) as ctx:
        NB = 9
        sem = lambda n: ctx.semaphore(n)
        stored, dts, acts, padded = sem("z_stored"), sem("dt_steps"), sem("dt_acts"), sem("dt_padded")
        raw = ctx.enter_context(nc.sbuf_tensor("dt_raw", [HEADS, TW], F32))
        low = ctx.enter_context(nc.sbuf_tensor("dt_low", [HEADS, TW], F32))
        arate = ctx.enter_context(nc.sbuf_tensor("a_rate", [HEADS, 1], F32))
        with nc.Block() as block:
            @block.sync
            def _(sp):
                stream_weights(sp, L, NB)

            @block.gpsimd
            def _(pool):
                cut_weights(nc, S, pool, L, NB)
                nc.gpsimd.memset(S.z[:, :, TW:TP], 0.0)

            @block.tensor
            def _(pe):
                products(nc, pe, L, normed(S), lambda s: psum_tn(S, s), 0, NB)

            @block.scalar
            def _(act):
                nc.scalar.sem_inc(L.emptied, SLOTS)
                nc.scalar.preload_act_table(ACT.Silu)
                with act.Fori(0, 4) as i:
                    for s in range(SLOTS):
                        act.wait_ge(L.products, done(L, i * SLOTS + s))
                        nc.scalar.activation(fm(blk(S.z[:, :, 0:TW], i * SLOTS + s)), psum_tn(S, s)[:, :, 0:TB], ACT.Silu,
                                             scale=1.0 / WSCALE).then_inc(L.emptied, 1)
                act.wait_ge(dts, 2)
                nc.scalar.activation(low[:, :], low[:, :], ACT.Exp).then_inc(acts, 1)
                act.wait_ge(acts, 1)
                nc.scalar.activation(low[:, :], low[:, :], ACT.Ln, bias=1.0).then_inc(acts, 1)
                nc.scalar.activation(arate[:, :], col(S, "ssd_a_log")[0:HEADS], ACT.Exp).then_inc(acts, 1)

            @block.vector
            def _(dve):
                step = Chain(dve, dts)
                nc.vector.memset(S.dt[:, :, T:TP], 0.0).then_inc(padded, 1)
                dve.wait_ge(L.products, done(L, 8))
                step(nc.vector.tensor_scalar(fm(raw[:, :]), psum_tn(S, 0)[0:HEADS, :, 0:TB], 1.0 / WSCALE,
                                             col(S, "ssd_dt_bias")[0:HEADS], ALU.mult, ALU.add))
                step(nc.vector.scalar_tensor_tensor(low[:, :], raw[:, :], -1.0, raw[:, :], ALU.mult, ALU.min))
                dve.wait_ge(acts, 3)
                step(nc.vector.scalar_tensor_tensor(S.dt[:, 0, 0:T], raw[:, 0:T], 0.0, low[:, 0:T], ALU.max, ALU.add))
                step(nc.vector.tensor_scalar(S.dt[:, 1, 0:T], S.dt[:, 0, 0:T], arate[:, 0:1], -1.0, ALU.mult, ALU.mult))



def ssd_phase(nc, S):
    QUADS, QH = 4, 4
    with Phase(nc) as ctx:
        sb = lambda n, shape: ctx.enter_context(nc.sbuf_tensor(n, shape, F32))
        sem = lambda n: ctx.semaphore(n)
        ch = sb("chunk", [P, 2, XBC_B, P])
        dtc = sb("chunk_dt", [HEADS, 2, 2, P])
        bt = sb("b_tokens", [P, 2, P])
        da2 = sb("dt_tokens", [P, 2, 2 * HEADS])
        sums2 = sb("dt_a_sums", [P, 2, 2 * HEADS])
        gap = sb("to_end", [P, HEADS])
        decs = sb("decay_to_end", [P, HEADS])
        ctot = sb("chunk_decay", [P, HEADS])
        xdt = sb("x_dt", [P, HEADS, HD])
        xdec = sb("x_decayed", [P, HEADS, HD])
        cbm = sb("cb_masked", [P, 2, P])
        seg2 = sb("seg", [P, 2, HEADS, P])
        ea2 = sb("decay_in", [P, 2, PAIRS, P])
        xd = sb("x_skip", [P, PAIRS, P])
        yt = sb("y_terms", [P, PAIRS, P])
        state = sb("state", [P, HEADS, HD])
        (s_copied, s_dtc, s_xt, s_dat, s_da, s_bt, s_cum, s_gap, s_dec, s_xdt, s_xdec, s_cb, s_cbm, s_row, s_ea, s_seg, s_m,
         s_off, s_diag, s_t, s_yd, s_step, s_y, s_st, s_decd, s_state, s_skip, s_exp) = (sem("ssd_" + n) for n in (
            "copied", "dtc", "xt", "dat", "da", "bt", "cum", "gap", "dec", "xdt", "xdec", "cb", "cbm", "row", "ea", "seg", "m",
            "off", "diag", "t", "yd", "step", "y", "st", "decd", "state", "skip", "exp"))
        ps = S.ps
        xt_ps = ps[:, 0:2, :]
        st_ps = [ps[:, 0, :], ps[:, 1, :]]
        b_ps, cb_ps = ps[:, 2, 0:2 * P], ps[:, 2, 2 * P:4 * P]
        da_ps, sum_ps = ps[:, 3, 0:2 * HEADS], ps[:, 3, 2 * HEADS:4 * HEADS]
        row_ps = [ps[:, 4, :], ps[:, 5, :]]
        off_ps, diag_ps = ps[:, 6, :], ps[:, 7, :]

        def chunks(eng, step):
            with eng.Fori(0, NCH // 2) as i:
                for s in range(2):
                    step(i * 2 + s, s, False)
            step(NCH - 1, 0, True)

        with nc.Block() as block:
            @block.gpsimd
            def _(pool):
                nc.gpsimd.memset(state[:, :, :], 0.0).then_inc(s_state, 2)

                def fixed(c, s):
                    lone_wait(S, pool, s_diag, c * 2)
                    nc.gpsimd.tensor_copy(ch[:, s, :, :], S.xbc[:, :, bass.ds(c * P, P)]).then_inc(s_copied, 1)

                def fixed_dt(c, s):
                    lone_wait(S, pool, s_da, c)
                    nc.gpsimd.tensor_copy(dtc[:, s, :, :], S.dt[:, :, bass.ds(c * P, P)]).then_inc(s_dtc, 1)

                def step(c, s, last_chunk):
                    if not last_chunk:
                        fixed_dt(c + 1, 1 - s)
                    lone_wait(S, pool, s_copied, c + 1)
                    lone_wait(S, pool, s_yd, c * 2 + 1)
                    for p in range(PAIRS):
                        last = nc.gpsimd.tensor_scalar(xd[:, p, :], ch[:, s, p, :], col(S, "ssd_d", p), 1.0, ALU.mult, ALU.mult)
                    last.then_inc(s_skip, 1)
                    lone_wait(S, pool, s_xdt, c + 1)
                    lone_wait(S, pool, s_dec, c * 2 + 1)
                    nc.gpsimd.tensor_tensor(xdec[:, :, :], xdt[:, :, :], decs[:, :].unsqueeze(2).to_broadcast([P, HEADS, HD]),
                                            ALU.mult).then_inc(s_xdec, 1)
                    if not last_chunk:
                        fixed(c + 1, 1 - s)

                fixed_dt(0, 0)
                fixed(0, 0)
                chunks(pool, step)

            @block.tensor
            def _(pe):
                nc.tensor.sem_inc(s_st, 1)
                nc.tensor.sem_inc(s_diag, 2)

                def turn_dt(c, s):
                    pe.wait_ge(s_dtc, c + 1)
                    lone_wait(S, pe, s_step, c)
                    for j in range(2):
                        last = nc.tensor.transpose(da_ps[:, j * HEADS:(j + 1) * HEADS], dtc[:, s, j, :], S.ident[0:HEADS, 0:HEADS])
                    last.then_inc(s_dat, 1)

                def cumulate(c, s):
                    pe.wait_ge(s_da, c + 1)
                    nc.tensor.matmul(sum_ps[:, 0:HEADS], S.upper[:, :], da2[:, s, HEADS:], start=True, stop=True)
                    nc.tensor.matmul(sum_ps[:, HEADS:], S.ones[:, :], da2[:, s, HEADS:], start=True, stop=True).then_inc(s_cum, 1)

                def rows(c, s, q):
                    pe.wait_ge(s_seg, c * 4 + (q + 1))
                    for j in range(QH):
                        a = HEADS + q * QH + j
                        last = nc.tensor.matmul(row_ps[q % 2][:, j * P:(j + 1) * P], da2[:, s, a:a + 1].to_broadcast([P, P]),
                                                S.upper[:, :], start=True, stop=True)
                    last.then_inc(s_row, 1)

                turn_dt(0, 0)
                cumulate(0, 0)
                for q in range(QUADS):
                    rows(0, 0, q)

                def step(c, s, last_chunk):
                    seg = seg2[:, s, :, :]
                    pe.wait_ge(s_copied, c + 1)
                    if not last_chunk:
                        turn_dt(c + 1, 1 - s)
                    pe.wait_ge(s_cbm, c + 1)
                    for g in range(2):
                        nc.tensor.transpose(b_ps[:, g * P:(g + 1) * P], ch[:, s, DB + g, :], S.ident[:, :])
                    for g in range(2):
                        last = nc.tensor.matmul(cb_ps[:, g * P:(g + 1) * P], ch[:, s, DB + g, :], ch[:, s, DB + 2 + g, :], start=True, stop=True)
                    last.then_inc(s_cb, 1)
                    pe.wait_ge(s_state, c * 2 + 2)
                    for j in range(DB):
                        last = nc.tensor.transpose(xt_ps.rearrange("p a n -> p (a n)")[:, j * P:(j + 1) * P], ch[:, s, j, :], S.ident[:, :])
                    last.then_inc(s_xt, 1)
                    if not last_chunk:
                        cumulate(c + 1, 1 - s)
                        rows(c + 1, 1 - s, 0)
                        rows(c + 1, 1 - s, 1)
                    for g in range(2):
                        pe.wait_ge(s_t, c * 2 + (g + 1))
                        for p in range(4):
                            last = nc.tensor.matmul(off_ps[:, p * P:(p + 1) * P],
                                                    state[:, g * 8 + 2 * p:g * 8 + 2 * p + 2, :].rearrange("p a n -> p (a n)"),
                                                    ch[:, s, DB + 2 + g, :], start=True, stop=True)
                        last.then_inc(s_off, 1)
                        pe.wait_ge(s_m, c * 4 + 2 * g + 2)
                        pe.wait_ge(s_xdt, c + 1)
                        pe.wait_ge(s_yd, c * 2 + (g + 1))
                        for p in range(4):
                            for a in range(2):
                                h = g * 8 + 2 * p + a
                                last = nc.tensor.matmul(diag_ps[a * HD:(a + 1) * HD, p * P:(p + 1) * P], xdt[:, h, :], seg[:, h, :],
                                                        start=True, stop=True)
                        last.then_inc(s_diag, 1)
                        if not last_chunk:
                            rows(c + 1, 1 - s, 2 + g)
                    pe.wait_ge(s_xdec, c + 1)
                    pe.wait_ge(s_bt, c + 1)
                    for g in range(2):
                        nc.tensor.matmul(st_ps[g], bt[:, g, :], xdec[:, g * 8:g * 8 + 8, :].rearrange("p a n -> p (a n)"),
                                         start=True, stop=True).then_inc(s_st, 1)

                chunks(pe, step)

            @block.scalar
            def _(act):
                nc.scalar.sem_inc(s_seg, 2)
                nc.scalar.preload_act_table(ACT.Exp)

                def decays(c, s):
                    seg, ea = seg2[:, s, :, :], ea2[:, s, :, :]
                    for q in range(QUADS):
                        act.wait_ge(s_row, c * 4 + (q + 1))
                        rows = row_ps[q % 2].rearrange("p (a b n) -> p a b n", a=2, b=2)
                        for a in range(2):
                            nc.scalar.activation(ea[a * HD:(a + 1) * HD, 2 * q:2 * q + 2, :], rows[a * HD:(a + 1) * HD, :, a, :],
                                                 ACT.Exp).then_inc(s_ea, 1)
                        if q == 0:
                            act.wait_ge(s_gap, c + 1)
                        for j in range(QH):
                            h = q * QH + j
                            last = nc.scalar.activation(seg[:, h, :], row_ps[q % 2][:, j * P:(j + 1) * P], ACT.Relu, scale=-1.0,
                                                        bias=sums2[:, s, h:h + 1])
                        last.then_inc(s_seg, 1)
                        act.wait_ge(s_seg, c * 4 + (q + 3))
                        four = seg[:, q * QH:(q + 1) * QH, :]
                        nc.scalar.activation(four, four, ACT.Exp, scale=-1.0).then_inc(s_exp, 1)

                decays(0, 0)

                def step(c, s, last_chunk):
                    act.wait_ge(s_gap, c + 1)
                    act.wait_ge(s_xdec, c)
                    nc.scalar.activation(decs[:, :], gap[:, :], ACT.Exp).then_inc(s_dec, 1)
                    act.wait_ge(s_decd, c * 2)
                    nc.scalar.activation(ctot[:, :], sums2[:, s, HEADS:], ACT.Exp).then_inc(s_dec, 1)
                    if not last_chunk:
                        act.wait_ge(s_t, c * 2 + 1)
                        act.wait_ge(s_diag, c * 2 + 2)
                        decays(c + 1, 1 - s)

                chunks(act, step)

            @block.vector
            def _(dve):
                nc.vector.sem_inc(s_cbm, 1)
                nc.vector.sem_inc(s_t, 1)
                nc.vector.sem_inc(s_yd, 1)

                def dt_out(c, s):
                    dve.wait_ge(s_dat, c + 1)
                    nc.vector.tensor_copy(da2[:, s, :], da_ps).then_inc(s_da, 1)

                def sums_out(c, s):
                    sums = sums2[:, s, :]
                    dve.wait_ge(s_cum, c + 1)
                    nc.vector.tensor_copy(sums, sum_ps).then_inc(s_step, 1)
                    dve.wait_ge(s_step, c + 1)
                    nc.vector.tensor_tensor(gap[:, :], sums[:, HEADS:], sums[:, 0:HEADS], ALU.subtract).then_inc(s_gap, 1)

                dt_out(0, 0)
                sums_out(0, 0)

                def step(c, s, last_chunk):
                    seg, ea = seg2[:, s, :, :], ea2[:, s, :, :]
                    if not last_chunk:
                        dt_out(c + 1, 1 - s)
                    dve.wait_ge(s_cb, c + 1)
                    nc.vector.tensor_copy(bt[:, :, :].rearrange("p a n -> p (a n)"), b_ps).then_inc(s_bt, 1)
                    nc.vector.tensor_tensor(cbm[:, :, :], cb_ps.rearrange("p (a n) -> p a n", a=2),
                                            S.upper[:, :].unsqueeze(1).to_broadcast([P, 2, P]), ALU.mult).then_inc(s_cbm, 1)
                    dve.wait_ge(s_cbm, c + 2)
                    for q in range(QUADS):
                        dve.wait_ge(s_exp, c * 4 + (q + 1))
                        four = seg[:, q * QH:(q + 1) * QH, :]
                        nc.vector.tensor_tensor(four, four, cbm[:, q // 2, :].unsqueeze(1).to_broadcast([P, QH, P]),
                                                ALU.mult).then_inc(s_m, 1)
                        if q == 1:
                            dve.wait_ge(s_xt, c + 1)
                            dve.wait_ge(s_da, c + 1)
                            nc.vector.tensor_tensor(xdt[:, :, :], xt_ps.rearrange("p a (b n) -> p (a b) n", n=HD),
                                                    da2[:, s, 0:HEADS].unsqueeze(2).to_broadcast([P, HEADS, HD]), ALU.mult).then_inc(s_xdt, 1)
                    if not last_chunk:
                        dve.wait_ge(s_dec, c * 2 + 1)
                        sums_out(c + 1, 1 - s)
                    dve.wait_ge(s_skip, c + 1)
                    for g in range(2):
                        mine = slice(4 * g, 4 * g + 4)
                        dve.wait_ge(s_off, c * 2 + (g + 1))
                        dve.wait_ge(s_ea, c * 8 + 4 * g + 4)
                        nc.vector.tensor_tensor(yt[:, mine, :], off_ps.rearrange("p (a n) -> p a n", a=4), ea[:, mine, :], ALU.mult).then_inc(s_t, 1)
                        dve.wait_ge(s_t, c * 2 + (g + 2))
                        nc.vector.tensor_tensor(yt[:, mine, :], yt[:, mine, :], xd[:, mine, :], ALU.add).then_inc(s_y, 1)
                        dve.wait_ge(s_y, c * 4 + 2 * g + 1)
                        dve.wait_ge(s_diag, c * 2 + (g + 3))
                        nc.vector.tensor_tensor(yt[:, mine, :], yt[:, mine, :], diag_ps.rearrange("p (a n) -> p a n", a=4), ALU.add).then_inc(s_yd, 1)
                        dve.wait_ge(s_yd, c * 2 + (g + 2))
                        zs = S.z[:, mine, bass.ds(c * P, P)]
                        nc.vector.tensor_tensor(zs, yt[:, mine, :], zs, ALU.mult).then_inc(s_y, 1)
                    for g in range(2):
                        mine = slice(8 * g, 8 * g + 8)
                        if g == 0:
                            dve.wait_ge(s_dec, c * 2 + 2)
                        nc.vector.tensor_tensor(state[:, mine, :], state[:, mine, :], ctot[:, mine].unsqueeze(2).to_broadcast([P, 8, HD]),
                                                ALU.mult).then_inc(s_decd, 1)
                        dve.wait_ge(s_decd, c * 2 + (g + 1))
                        dve.wait_ge(s_st, c * 2 + (g + 2))
                        nc.vector.tensor_tensor(state[:, mine, :], state[:, mine, :], st_ps[g].rearrange("p (a n) -> p a n", n=HD),
                                                ALU.add).then_inc(s_state, 1)

                chunks(dve, step)



HALF = HEADS // 2
QKV_B = 12


def qkv_phase(nc, S, L, half, N=None):
    tag = f"qkv{half}"
    with Phase(nc) as ctx:
        sem = lambda n: ctx.semaphore(f"{n}_{tag}")
        sb = lambda n, shape, dt: ctx.enter_context(nc.sbuf_tensor(f"{n}_{tag}", shape, dt))
        full = sb("full", [P, SLOTS, TP], F32)
        if N:
            y = sb("y", [P, 2, TW], F32)
            N.y = [y[:, j, :] for j in range(2)]
        hi, lo = sb("hi", [P, SLOTS, TW], F16), sb("lo", [P, SLOTS, TW], F16)
        s_full, s_hi, s_lo, s_placed, s_zero, s_turned, s_vhi, s_vlo = (
            sem(n) for n in ("full", "hi", "lo", "placed", "zero", "turned", "vhi", "vlo"))
        QK_B = 8
        tiles = lambda s, n: psum_tn(S, s)[:, n, 0:3 * P].rearrange("p (t h d) -> p t h d", t=3, d=HD)
        def v2(b, n, part):
            return S.v2[:, 3 * n:3 * n + 3, bass.ds((b - QK_B) * 2, 2), part * HD:(part + 1) * HD]
        with nc.Block() as block:
            @block.sync
            def _(sp):
                stream_weights(sp, L, QKV_B)

            @block.gpsimd
            def _(pool):
                if N:
                    cut_by_pool(nc, pool, N)
                cut_weights(nc, S, pool, L, QKV_B)

            @block.tensor
            def _(pe):
                banks = lambda s: psum_tn(S, s)

                def turn(i, s):
                    pe.wait_ge(s_full, i * SLOTS + (s + 1))
                    for t in range(NCH):
                        last = nc.tensor.transpose(psum_tn(S, s)[:, t // 3, (t % 3) * P:(t % 3 + 1) * P],
                                                   full[:, s, t * P:(t + 1) * P], S.ident[:, :])
                    last.then_inc(s_turned, 1)

                products(nc, pe, L, normed(S), banks, 0, QK_B)
                products(nc, pe, L, normed(S), banks, QK_B, QKV_B, after=turn)

            @block.scalar
            def _(act):
                nc.scalar.sem_inc(L.emptied, SLOTS)
                if N:
                    cut_by_scalar(nc, act, N)
                act.wait_ge(s_zero, 1)
                with act.Fori(0, QK_B // SLOTS) as i:
                    for s in range(SLOTS):
                        act.wait_ge(L.products, done(L, i * SLOTS + s))
                        act.wait_ge(s_placed, i * SLOTS + (s + 1))
                        nc.scalar.activation(fm(hi[:, s, :]), psum_tn(S, s)[:, :, 0:TB], ACT.Copy, scale=1.0 / WSCALE).then_inc(s_hi, 1)
                        nc.scalar.activation(fm(full[:, s, 0:TW]), psum_tn(S, s)[:, :, 0:TB], ACT.Copy, scale=1.0 / WSCALE).then_inc(s_full, 1)
                        act.wait_ge(s_full, i * SLOTS + (s + 1))
                        nc.scalar.sem_inc(L.emptied, 1)
                with act.Fori(QK_B // SLOTS, QKV_B // SLOTS) as i:
                    for s in range(SLOTS):
                        b = i * SLOTS + s
                        act.wait_ge(L.products, done(L, b))
                        act.wait_ge(s_placed, QK_B + SLOTS)
                        nc.scalar.activation(fm(full[:, s, 0:TW]), psum_tn(S, s)[:, :, 0:TB], ACT.Copy, scale=1.0 / WSCALE).then_inc(s_full, 1)
                        act.wait_ge(s_turned, b - (QK_B - 1))
                        for n in range(NT):
                            last = nc.scalar.activation(v2(b, n, 0), tiles(s, n), ACT.Copy)
                        last.then_inc(s_vhi, 1)
                        act.wait_ge(s_vlo, b - (QK_B - 1))
                        nc.scalar.sem_inc(L.emptied, 1)

            @block.vector
            def _(dve):
                nc.vector.memset(full[:, :, TW:TP], 0.0).then_inc(s_zero, 1)
                if N:
                    cut_by_vector(nc, S, dve, N)
                nc.vector.sem_inc(s_placed, SLOTS)
                with dve.Fori(0, QK_B // SLOTS) as i:
                    for s in range(SLOTS):
                        b = i * SLOTS + s
                        dve.wait_ge(s_full, i * SLOTS + (s + 1))
                        nc.vector.tensor_tensor(lo[:, s, :], full[:, s, 0:TW], hi[:, s, :], ALU.subtract).then_inc(s_lo, 1)
                        dve.wait_ge(s_lo, i * SLOTS + (s + 1))
                        for a in range(2):
                            mine = slice(a * HD, (a + 1) * HD)
                            dst = S.qk[:, bass.ds(b * 2 + a, 1), :].rearrange("p a n -> p (a n)")
                            nc.vector.tensor_copy(dst[0:HD], hi[mine, s, :])
                            last = nc.vector.tensor_copy(dst[HD:P], lo[mine, s, :])
                        last.then_inc(s_placed, 1)
                with dve.Fori(QK_B // SLOTS, QKV_B // SLOTS) as i:
                    for s in range(SLOTS):
                        b = i * SLOTS + s
                        dve.wait_ge(s_vhi, b - (QK_B - 1))
                        for n in range(NT):
                            last = nc.vector.tensor_tensor(v2(b, n, 1), tiles(s, n), v2(b, n, 0), ALU.subtract)
                        last.then_inc(s_vlo, 1)


class Tile:

    def __init__(self, i):
        self.i = i
        self.first_queries = i == NCH
        self.sb = 0 if self.first_queries else NCH - 1 - i
        self.s0 = self.sb * P
        self.rows = META if self.first_queries or self.sb == NCH - 1 else P
        self.t0 = 0 if self.first_queries else max(self.s0, META)
        self.w = (META if self.first_queries else T) - self.t0
        self.slot = i % 3
        self.dw = min(self.s0 + P, self.t0 + self.w) - self.t0
        self.d0 = self.t0 - self.s0

    def cuts(self, at=0):
        out = []
        while at < self.w:
            end = min(self.w, (at // BANK + 1) * BANK)
            out.append((at, end))
            at = end
        return out


TILES = [Tile(i) for i in range(NCH + 1)]
NTILE = len(TILES)
NLATER = NCH - 1


HGROUP = 4
NSTREAM = HGROUP * NTILE


def attention_phase(nc, S, half):
    tag = f"att{half}"
    CAP = 40.0
    with Phase(nc) as ctx:
        sem = lambda n: ctx.semaphore(f"{n}_{tag}")
        sb = lambda n, shape, dt=F32: ctx.enter_context(nc.sbuf_tensor(f"{n}_{tag}", shape, dt))
        kf, ks = sb("k_head", [P, 2, TW], F16), sb("k_swapped", [P, 2, TW], F16)
        vf = sb("v_head", [P, NCH, P], F16)
        e = sb("e", [P, 2, SEQ])
        sp_ = sb("softplus", [P, 2, SEQ])
        later = sb("later", [P, 2, T])
        w = sb("w", [P, 2, SEQ])
        whi, wlo = sb("w_hi", [P, 2, SEQ], F16), sb("w_lo", [P, 2, SEQ], F16)
        (s_head, s_z, s_zm, s_e, s_l, s_raw, s_sp, s_lat, s_b, s_w, s_wm, s_whi, s_cut, s_c, s_v, s_fe, s_oe, s_clear) = (sem(n) for n in (
            "head", "z", "zm", "e", "l", "raw", "sp", "lat", "b", "w", "wm", "whi", "cut", "c", "v", "fe", "oe", "clear"))
        flat = S.ps[:, :, :].rearrange("p a n -> p (a n)")
        zps = lambda n: flat[:, 2 * (n % 3) * BANK:2 * (n % 3) * BANK + 2 * BANK]
        rows_of = lambda a: slice((a % 2) * HD, (a % 2 + 1) * HD)
        ops = lambda a: flat[rows_of(a), 6 * BANK:8 * BANK]
        first_o = lambda a: zps(a * NTILE + NCH)[rows_of(a), BANK:BANK + META]
        tile = lambda n: TILES[n % NTILE]

        def index(it, n):
            return it * NSTREAM + n

        def o_of(it, a):
            return S.z[(a % 2) * HD:(a % 2 + 1) * HD, bass.ds(it * (HGROUP // 2) + (half * (HALF // 2) + a // 2), 1), 0:T].rearrange("p a n -> p (a n)")

        with nc.Block() as block:
            @block.tensor
            def _(pe):
                nc.tensor.sem_inc(s_b, 2)
                nc.tensor.sem_inc(s_c, 2)

                def scores(it, n):
                    t, a = tile(n), n // NTILE
                    if t.i == 0:
                        pe.wait_ge(s_head, it * HGROUP + (a + 1))
                    if n < 3:
                        pe.wait_ge(s_w, index(it, 0))
                    else:
                        pe.wait_ge(s_w, index(it, n - 2))
                    if n == 0:
                        pe.wait_ge(s_oe, it * HGROUP)
                    if n == 0 or (a > 0 and t.i == 4):
                        pe.wait_ge(s_fe, it * HGROUP + a)
                    q = S.qk[:, bass.ds(it * HGROUP + a, 1), :].rearrange("p a n -> p (a n)")
                    for lo_, hi_ in t.cuts():
                        for k in (kf, ks):
                            last = nc.tensor.matmul(zps(n)[0:t.rows, lo_:hi_], k[:, a % 2, t.s0:t.s0 + t.rows], q[:, t.t0 + lo_:t.t0 + hi_],
                                                    start=(k is kf), stop=(k is ks), skip_group_check=True)
                    last.then_inc(s_z, 1)

                def sums(it, n):
                    t, a = tile(n), n // NTILE
                    lone_wait(S, pe, s_sp, index(it, n + 1))
                    for lo_, hi_ in t.cuts():
                        last = nc.tensor.matmul(zps(n)[0:t.rows, lo_:hi_], S.tri8[0:t.rows, 0:t.rows], sp_[0:t.rows, n % 2, lo_:hi_],
                                                start=False, stop=True, skip_group_check=True)
                    if 1 <= t.i < NCH:
                        pe.wait_ge(s_lat, it * (HGROUP * NLATER) + (a * NLATER + t.i))
                        for lo_, hi_ in t.cuts(TILES[t.i - 1].t0 - t.t0):
                            last = nc.tensor.matmul(zps(n)[:, lo_:hi_], S.ones8[:, :], later[:, n % 2, t.t0 + lo_:t.t0 + hi_],
                                                    start=False, stop=True, skip_group_check=True)
                    last.then_inc(s_b, 1)

                def values(it, n):
                    t, a = tile(n), n // NTILE
                    if t.i == 0:
                        lone_wait(S, pe, s_v, it * (2 * HGROUP) + (2 * a + 1))
                        if a >= 2:
                            lone_wait(S, pe, s_oe, it * HGROUP + (a - 1))
                    if t.sb == 0 and not t.first_queries:
                        lone_wait(S, pe, s_v, it * (2 * HGROUP) + (2 * a + 2))
                    lone_wait(S, pe, s_cut, index(it, n + 3))
                    vhi, vlo = (vf[0:t.rows, t.sb, j * HD:(j + 1) * HD] for j in range(2))
                    parts = ((vhi, whi), (vhi, wlo), (vlo, whi))
                    if t.first_queries:
                        for j, (v, x) in enumerate(parts):
                            last = nc.tensor.matmul(first_o(a), v, x[0:t.rows, n % 2, 0:t.w], start=(j == 0), stop=(j == 2), skip_group_check=True)
                    else:
                        c0 = t.t0 - META
                        for bank in range(2):
                            lo_, hi_ = max(c0, bank * BANK), (bank + 1) * BANK
                            if lo_ >= hi_:
                                continue
                            opens = t.i == 0 or (bank == 0 and TILES[t.i - 1].t0 - META >= BANK)
                            for j, (v, x) in enumerate(parts):
                                last = nc.tensor.matmul(ops(a)[:, lo_:hi_], v, x[0:t.rows, n % 2, lo_ - c0:hi_ - c0],
                                                        start=(opens and j == 0), stop=True, skip_group_check=True)
                    last.then_inc(s_c, 1)

                with pe.Fori(0, HALF // HGROUP) as it:
                    scores(it, 0)
                    scores(it, 1)
                    for n in range(NSTREAM):
                        if n + 2 < NSTREAM:
                            scores(it, n + 2)
                        sums(it, n)
                        if n >= 2:
                            values(it, n - 2)
                    values(it, NSTREAM - 2)
                    values(it, NSTREAM - 1)

            @block.scalar
            def _(act):
                nc.scalar.sem_inc(s_l, 2)
                nc.scalar.preload_act_table_set("natural_log_exp_and_others")

                def log1p(it, n):
                    t = tile(n)
                    x = e[0:t.rows, n % 2, 0:t.w]
                    act.wait_ge(s_zm, index(it, n + 1))
                    nc.scalar.activation(x, x, ACT.Exp).then_inc(s_e, 1)
                    act.wait_ge(s_e, index(it, n + 1))
                    nc.scalar.activation(x, x, ACT.Ln, bias=1.0).then_inc(s_l, 1)

                def weights(it, n):
                    t = tile(n)
                    act.wait_ge(s_b, index(it, n + 3))
                    act.wait_ge(s_cut, index(it, n + 1))
                    nc.scalar.activation(w[0:t.rows, n % 2, 0:t.w], zps(n)[0:t.rows, 0:t.w], ACT.Exp, scale=0.125).then_inc(s_w, 1)

                def store_first(it, a):
                    act.wait_ge(s_c, index(it, (a + 1) * NTILE + 2))
                    nc.scalar.activation(o_of(it, a)[:, 0:META], first_o(a), ACT.Copy).then_inc(s_fe, 1)

                def store_o(it, a):
                    nc.scalar.activation(o_of(it, a)[:, META:T], ops(a), ACT.Copy).then_inc(s_oe, 1)

                with act.Fori(0, HALF // HGROUP) as it:
                    log1p(it, 0)
                    log1p(it, 1)
                    for n in range(NSTREAM):
                        weights(it, n)
                        if n + 2 < NSTREAM:
                            log1p(it, n + 2)
                        if n >= NTILE and tile(n).i == 1:
                            store_first(it, n // NTILE - 1)
                        if n >= NTILE and tile(n).i == 4:
                            store_o(it, n // NTILE - 1)
                    store_first(it, HGROUP - 1)
                    store_o(it, HGROUP - 1)

            @block.vector
            def _(dve):
                def load_k(it, a):
                    k = S.qk[:, bass.ds(it * HGROUP + (a + HALF), 1), :].rearrange("p a n -> p (a n)")
                    if a < 2:
                        dve.wait_ge(s_c, index(it, 2))
                    else:
                        dve.wait_ge(s_z, index(it, (a - 1) * NTILE))
                    nc.vector.tensor_copy(kf[:, a % 2, :], k)
                    nc.vector.tensor_copy(ks[0:HD, a % 2, :], k[HD:P])
                    nc.vector.tensor_copy(ks[HD:P, a % 2, :], k[0:HD]).then_inc(s_head, 1)

                def load_v(it, a, first):
                    dve.wait_ge(s_c, index(it, a * NTILE + (2 if first else 0)))
                    these = slice(0, 1) if first else slice(1, NCH)
                    nc.vector.tensor_copy(vf[:, these, :], S.v2[:, these, bass.ds(it * HGROUP + a, 1), :].rearrange("p t a n -> p t (a n)")).then_inc(s_v, 1)

                def capped(it, n):
                    t = tile(n)
                    dve.wait_ge(s_z, index(it, n + 1))
                    dve.wait_ge(s_l, index(it, n + 1))
                    nc.vector.tensor_scalar(e[0:t.rows, n % 2, 0:t.w], zps(n)[0:t.rows, 0:t.w], 0.125, CAP, ALU.mult, ALU.min).then_inc(s_zm, 1)

                def softplus(it, n):
                    t = tile(n)
                    dve.wait_ge(s_l, index(it, n + 3))
                    dve.wait_ge(s_b, index(it, n + 1))
                    x = sp_[0:t.rows, n % 2, 0:t.w]
                    nc.vector.scalar_tensor_tensor(x, zps(n)[0:t.rows, 0:t.w], 0.125, e[0:t.rows, n % 2, 0:t.w],
                                                   ALU.mult, ALU.max).then_inc(s_raw, 1)
                    dve.wait_ge(s_raw, index(it, n + 1))
                    d = sp_[0:t.rows, n % 2, 0:t.dw]
                    nc.vector.tensor_tensor(d, d, S.strict[0:t.rows, t.d0:t.d0 + t.dw], ALU.mult).then_inc(s_sp, 1)

                def add_later(it, n):
                    t, a = tile(n), n // NTILE
                    if t.i >= NLATER:
                        return
                    dve.wait_ge(s_sp, index(it, n + 1))
                    new, old = later[:, (n + 1) % 2, :], later[:, n % 2, :]
                    dve.wait_ge(s_b, index(it, n + 2))
                    if t.i == 0:
                        nc.vector.memset(new[:, t.t0:T], 0.0).then_inc(s_clear, 1)
                        dve.wait_ge(s_clear, it * HGROUP + (a + 1))
                        nc.vector.tensor_copy(new[0:t.rows, t.t0:T], sp_[0:t.rows, n % 2, 0:t.w]).then_inc(s_lat, 1)
                        return
                    seam = TILES[t.i - 1].t0
                    nc.vector.tensor_copy(new[:, t.t0:seam], sp_[:, n % 2, 0:seam - t.t0])
                    nc.vector.tensor_tensor(new[:, seam:T], old[:, seam:T], sp_[:, n % 2, seam - t.t0:t.w], ALU.add).then_inc(s_lat, 1)

                def mask_weights(it, n):
                    t = tile(n)
                    dve.wait_ge(s_w, index(it, n + 1))
                    d = w[0:t.rows, n % 2, 0:t.dw]
                    nc.vector.scalar_tensor_tensor(d, d, 1.0, S.strict[0:t.rows, t.d0:t.d0 + t.dw], ALU.min, ALU.mult).then_inc(s_wm, 1)

                with dve.Fori(0, HALF // HGROUP) as it:
                    load_k(it, 0)
                    load_v(it, 0, False)
                    load_v(it, 0, True)
                    capped(it, 0)
                    capped(it, 1)
                    softplus(it, 0)
                    add_later(it, 0)
                    for n in range(NSTREAM):
                        if n + 2 < NSTREAM:
                            capped(it, n + 2)
                        if n + 1 < NSTREAM:
                            softplus(it, n + 1)
                            add_later(it, n + 1)
                        mask_weights(it, n)
                        if n >= NTILE and tile(n).i in (0, 3):
                            load_v(it, n // NTILE, tile(n).i == 3)
                        if tile(n).i == 5 and n // NTILE + 1 < HGROUP:
                            load_k(it, n // NTILE + 1)

            @block.gpsimd
            def _(pool):
                nc.gpsimd.sem_inc(s_cut, 2)
                with pool.Fori(0, HALF // HGROUP) as it:
                    for n in range(NSTREAM):
                        t = tile(n)
                        x = w[0:t.rows, n % 2, 0:t.w]
                        hi, lo = whi[0:t.rows, n % 2, 0:t.w], wlo[0:t.rows, n % 2, 0:t.w]
                        lone_wait(S, pool, s_wm, index(it, n + 1))
                        lone_wait(S, pool, s_c, index(it, n + 1))
                        nc.gpsimd.tensor_scalar(hi, x, 1.0, 1.0, ALU.mult, ALU.mult).then_inc(s_whi, 1)
                        lone_wait(S, pool, s_whi, index(it, n + 1))
                        nc.gpsimd.tensor_tensor(lo, x, hi, ALU.subtract).then_inc(s_cut, 1)



def linear_phase(nc, S, L, xs, nb, out, nt=NT, tb=TB, t0=0, plus=None, after=None, silu=None, norm=None, norm_from=0):
    banks = lambda s: S.ps[:, nt * s:nt * s + nt, :]
    with nc.Block() as block:
        @block.sync
        def _(sp):
            stream_weights(sp, L, nb * L.parts)

        @block.gpsimd
        def _(pool):
            if norm:
                cut_by_pool(nc, pool, norm)
            cut_weights(nc, S, pool, L, nb * L.parts)

        @block.tensor
        def _(pe):
            products(nc, pe, L, xs, banks, 0, nb, nt, tb, t0, ready=cut_ready(norm, norm_from) if norm else None)

        if plus is None:
            @block.scalar
            def _(act):
                nc.scalar.sem_inc(L.emptied, SLOTS)
                if norm:
                    cut_by_scalar(nc, act, norm)
                for first, end, func in ((0, nb if silu is None else silu, ACT.Copy), (silu, nb, ACT.Silu)):
                    if first is None:
                        continue
                    nc.scalar.preload_act_table(func)
                    with act.Fori(first // SLOTS, end // SLOTS) as i:
                        for s in range(SLOTS):
                            act.wait_ge(L.products, done(L, i * SLOTS + s))
                            nc.scalar.activation(fm(blk(out, i * SLOTS + s), nt), banks(s)[:, :, 0:tb], func,
                                                 scale=1.0 / WSCALE).then_inc(L.emptied, 1)
            if norm or after:
                @block.vector
                def _(dve):
                    if norm:
                        cut_by_vector(nc, S, dve, norm)
                    if after:
                        after(dve, L)
        else:
            @block.vector
            def _(dve):
                nc.vector.sem_inc(L.emptied, SLOTS)
                with dve.Fori(0, nb // SLOTS) as i:
                    for s in range(SLOTS):
                        dve.wait_ge(L.products, done(L, i * SLOTS + s))
                        nc.vector.scalar_tensor_tensor(fm(blk(out, i * SLOTS + s), nt), banks(s)[:, :, 0:tb], 1.0 / WSCALE,
                                                       fm(blk(plus, i * SLOTS + s), nt), ALU.mult, ALU.add).then_inc(L.emptied, 1)


FTAPS = 3


def ffn_up_phase(nc, S, L, N):
    with Phase(nc) as ctx:
        sb = lambda n: ctx.enter_context(nc.sbuf_tensor(n, [P, TW], F32))
        sem = lambda n: ctx.semaphore("ffn_" + n)
        raw = ctx.enter_context(nc.sbuf_tensor("gate_raw", [P, FTAPS - 1 + TW], F32))
        acc, f = sb("gate_conv"), sb("f_full")
        N.y = [raw[:, FTAPS - 1:], acc[:, :], f[:, :]]
        s_zero, s_raw, s_step, s_conv, s_gelu, s_f, s_hi, s_lo = (sem(n) for n in ("zero", "raw", "step", "conv", "gelu", "f", "hi", "lo"))
        with nc.Block() as block:
            @block.sync
            def _(sp):
                stream_weights(sp, L, 2 * FFB)

            @block.gpsimd
            def _(pool):
                cut_by_pool(nc, pool, N)
                cut_weights(nc, S, pool, L, 2 * FFB)

            @block.tensor
            def _(pe):
                products(nc, pe, L, normed(S), lambda s: psum_tn(S, s), 0, 2 * FFB, ready=cut_ready(N))

            @block.scalar
            def _(act):
                nc.scalar.sem_inc(L.emptied, SLOTS)
                cut_by_scalar(nc, act, N)
                nc.scalar.preload_act_table(ACT.Gelu_apprx_tanh)
                act.wait_ge(s_zero, 1)
                with act.Fori(0, FFB) as i:
                    act.wait_ge(L.products, done(L, i * 2))
                    act.wait_ge(s_conv, i)
                    nc.scalar.activation(fm(raw[:, FTAPS - 1:]), psum_tn(S, 0)[:, :, 0:TB], ACT.Copy, scale=1.0 / WSCALE).then_inc(s_raw, 1)
                    act.wait_ge(s_raw, i + 1)
                    nc.scalar.sem_inc(L.emptied, 1)
                    act.wait_ge(s_conv, i + 1)
                    nc.scalar.activation(acc[:, :], acc[:, :], ACT.Gelu_apprx_tanh).then_inc(s_gelu, 1)
                    act.wait_ge(s_f, i + 1)
                    nc.scalar.activation(blk(S.fhi, i), f[:, :], ACT.Copy).then_inc(s_hi, 1)
                    nc.scalar.sem_inc(L.emptied, 1)

            @block.vector
            def _(dve):
                cut_by_vector(nc, S, dve, N)
                nc.vector.memset(raw[:, 0:FTAPS - 1], 0.0).then_inc(s_zero, 1)
                with dve.Fori(0, FFB) as i:
                    step = Chain(dve, s_step, i * (FTAPS - 1))
                    dve.wait_ge(s_raw, i + 1)
                    step(nc.vector.tensor_scalar(acc[:, :], raw[:, 0:TW], dcol(S, "ffn_conv_w", i, FTAPS, 0),
                                                 dcol(S, "ffn_conv_b", i), ALU.mult, ALU.add))
                    step(nc.vector.scalar_tensor_tensor(acc[:, :], raw[:, 1:1 + TW], dcol(S, "ffn_conv_w", i, FTAPS, 1), acc[:, :], ALU.mult, ALU.add))
                    nc.vector.scalar_tensor_tensor(acc[:, :], raw[:, 2:2 + TW], dcol(S, "ffn_conv_w", i, FTAPS, 2), acc[:, :],
                                                   ALU.mult, ALU.add).then_inc(s_conv, 1)
                    dve.wait_ge(L.products, done(L, i * 2 + 1))
                    dve.wait_ge(s_gelu, i + 1)
                    nc.vector.scalar_tensor_tensor(fm(f[:, :]), psum_tn(S, 1)[:, :, 0:TB], 1.0 / WSCALE, fm(acc[:, :]),
                                                   ALU.mult, ALU.mult).then_inc(s_f, 1)
                    dve.wait_ge(s_hi, i + 1)
                    nc.vector.tensor_tensor(blk(S.flo, i), f[:, :], blk(S.fhi, i), ALU.subtract).then_inc(s_lo, 1)
                    dve.wait_ge(s_lo, i + 1)


def ffn(nc, S, A):
    with ExitStack() as ctx:
        sb = lambda n, shape, dt: ctx.enter_context(nc.sbuf_tensor(n, shape, dt))
        S.fhi, S.flo = sb("f_hi", [P, FFB, TW], F16), sb("f_lo", [P, FFB, TW], F16)
        with ExitStack() as inp:
            S.xhi, S.xlo = (inp.enter_context(nc.sbuf_tensor(n, [P, DB, TW], F16)) for n in ("ffn_x_hi", "ffn_x_lo"))
            with Phase(nc) as layer:
                L = linear_buffers(nc, layer, A["w_up"], 0, DB, "up", "right")
                N = norm_cut(nc, layer, "ffn_pre_y", S.h, "ffn_pre_g", DB, TW, S.xhi, S.xlo)
                norm_phase(nc, S, "ffn_pre", S.h, "ffn_pre_g", DB, TW, ("rs", N), ahead=L)
                ffn_up_phase(nc, S, L, N)
        with nc.sbuf_tensor("ffn_out", [P, DB, SEQ], F32) as down:
            with Phase(nc) as layer:
                L = linear_buffers(nc, layer, A["w_down"], 0, FFB // 2, "down", parts=2)
                linear_phase(nc, S, L, lambda k: (S.fhi[:, k, :], S.flo[:, k, :]), DB, down, 2, BANK, META)
            norm_phase(nc, S, "ffn_post", down, "ffn_post_g", DB, SEQ, ("add", S.h[:, :, META:T]), 2, BANK)



SUB = 64
NSUB = SEQ // SUB
NUNIT = SEQ // P
NLEVEL = 6
GLR, GWA, GQ, GK, GV, GG, GLA_B = 0, 1, 2, 4, 6, 10, 14
GLA_HEADS = 4
GLA_TAU = 16.0


def second_masks(nc, S, pool, s_set):
    step = Chain(pool, s_set)
    nc.gpsimd.memset(S.levels[:, :, :], 1.0)
    step(nc.gpsimd.memset(S.same[:, :], 0.0))
    for a in range(2):
        last = nc.gpsimd.memset(S.same[a * SUB:(a + 1) * SUB, a * SUB:(a + 1) * SUB], 1.0)
    step(last)
    nc.gpsimd.tensor_tensor(S.incl[:, :], S.same[:, :], S.upper[:, :], ALU.mult)
    nc.gpsimd.tensor_tensor(S.excl[:, :], S.same[:, :], S.strict[:, :], ALU.mult)
    for l in range(NLEVEL):
        m = 1 << l
        v = S.levels[:, l, :].rearrange("p (b c t) -> p b c t", c=2, t=m)
        step(nc.gpsimd.affine_select(out=v, in_=v, compare_op=ALU.is_ge, fill=0.0, base=0,
                                     pattern=[[-2 * m, P // (2 * m)], [0, 2], [0, m]], channel_multiplier=1))
        step(nc.gpsimd.affine_select(out=v, in_=v, compare_op=ALU.is_ge, fill=0.0, base=m - 1,
                                     pattern=[[2 * m, P // (2 * m)], [0, 2], [0, m]], channel_multiplier=-1))
        step(nc.gpsimd.memset(v[:, :, 0, :], 0.0))


def scan_starts(nc, S, pool, s_scan):
    Chain(pool, s_scan)(nc.gpsimd.memset(S.scan[:, :], 1.0))
    nc.gpsimd.memset(S.scan[:, :].rearrange("p (c t) -> p c t", t=SUB)[:, :, 0:1], 0.0)


def gla_in_phase(nc, S, A, L, N, u, kst, dec, s_set):
    EARLY = GV
    with Phase(nc) as ctx:
        sb = lambda n, shape: ctx.enter_context(nc.sbuf_tensor("gla_" + n, shape, F32))
        sem = lambda n: ctx.semaphore("gla_" + n)
        up = sb("gate_up", [16, 2 * P])
        x, low, b = sb("gate", [P, 2, SEQ]), sb("low", [P, 2, SEQ]), sb("cum", [P, 2, SEQ])
        N.y = [t[:, c, :] for t in (x, low) for c in range(2)]
        s_up, s_g, s_v, s_a, s_p = (sem(n) for n in ("up", "g", "v", "a", "p"))
        q, k = u[:, GQ:GQ + 2, :], u[:, GK:GK + 2, :]
        banks = lambda s: S.ps[:, 2 * s:2 * s + 2, :]
        gate_ps = lambda c: S.ps[:, 4 + 2 * c:6 + 2 * c, :]
        with nc.Block() as block:
            @block.sync
            def _(sp):
                sp.dma_start(up[:, :], A["gate_up"]).then_inc(s_up, 16)
                stream_weights(sp, L, GLA_B)

            @block.gpsimd
            def _(pool):
                cut_by_pool(nc, pool, N)
                cut_weights(nc, S, pool, L, GLA_B)
                second_masks(nc, S, pool, s_set)

            @block.tensor
            def _(pe):
                products(nc, pe, L, normed(S), banks, 0, EARLY, 2, BANK, ready=cut_ready(N))
                pe.wait_ge(s_up, 16)
                pe.wait_ge(L.emptied, SLOTS + GLR + 1)
                for c in range(2):
                    for n in range(2):
                        last = nc.tensor.matmul(gate_ps(c)[:, n, :], up[:, c * P:(c + 1) * P], u[0:16, GLR, n * BANK:(n + 1) * BANK],
                                                start=True, stop=True)
                last.then_inc(s_g, 1)
                products(nc, pe, L, normed(S), banks, EARLY, GLA_B, 2, BANK)

            @block.scalar
            def _(act):
                nc.scalar.sem_inc(L.emptied, SLOTS)
                cut_by_scalar(nc, act, N)
                nc.scalar.preload_act_table_set("natural_log_exp_and_others")

                def empty(b, s, out, func=ACT.Copy):
                    act.wait_ge(L.products, done(L, b))
                    nc.scalar.activation(fm(out, 2), banks(s), func, scale=1.0 / WSCALE).then_inc(L.emptied, 1)

                with act.Fori(0, EARLY // SLOTS) as i:
                    for s in range(SLOTS):
                        empty(i * SLOTS + s, s, blk(u, i * SLOTS + s))
                act.wait_ge(s_v, 2)
                nc.scalar.activation(low[:, :, :], low[:, :, :], ACT.Exp).then_inc(s_p, 1)
                act.wait_ge(s_p, 1)
                nc.scalar.activation(low[:, :, :], low[:, :, :], ACT.Ln, bias=1.0).then_inc(s_a, 1)
                empty(GV, 0, u[:, GV, :])
                act.wait_ge(s_v, 5)
                nc.scalar.activation(low[:, :, :], b[:, :, :], ACT.Exp).then_inc(s_a, 1)
                nc.scalar.activation(x[:, :, :], b[:, :, :], ACT.Exp, scale=-1.0).then_inc(s_a, 1)
                empty(GV + 1, 1, u[:, GV + 1, :])
                act.wait_ge(s_v, 7)
                nc.scalar.activation(low[:, :, :], low[:, :, :], ACT.Exp).then_inc(s_a, 1)
                for j in range(2, GLA_HEADS):
                    empty(GV + j, j % 2, u[:, GV + j, :])
                nc.scalar.preload_act_table(ACT.Silu)
                for j in range(GLA_HEADS):
                    empty(GG + j, j % 2, u[:, GG + j, :], ACT.Silu)

            @block.vector
            def _(dve):
                cut_by_vector(nc, S, dve, N)
                step = Chain(dve, s_v)
                dve.wait_ge(s_g, 1)
                for c in range(2):
                    last = nc.vector.tensor_scalar(fm(x[:, c, :], 2), gate_ps(c), col(S, "gla_gate_bias_2", c), None, ALU.add)
                step(last)
                step(nc.vector.scalar_tensor_tensor(low[:, :, :], x[:, :, :], -1.0, x[:, :, :], ALU.mult, ALU.min))
                dve.wait_ge(s_a, 1)
                step(nc.vector.scalar_tensor_tensor(x[:, :, :], x[:, :, :], 0.0, low[:, :, :], ALU.min, ALU.subtract))
                step(nc.vector.tensor_scalar(x[:, :, :], x[:, :, :], 1.0 / GLA_TAU, None, ALU.mult))
                for c in range(2):
                    last = nc.vector.tensor_tensor_scan(b[:, c, :], S.scan[:, :], x[:, c, :], 0.0, ALU.mult, ALU.add)
                step(last)
                dve.wait_ge(s_a, 2)
                nc.vector.scalar_tensor_tensor(q, q, GLA_DK_SCALE, low[:, :, :], ALU.mult, ALU.mult)
                step(nc.vector.tensor_copy(dec[:, :, :], low[:, :, SUB - 1::SUB]))
                for c in range(2):
                    bc = b[:, c, :].rearrange("p (n t) -> p n t", t=SUB)
                    last = nc.vector.tensor_tensor(low[:, c, :].rearrange("p (n t) -> p n t", t=SUB),
                                                   bc[:, :, SUB - 1:SUB].to_broadcast([P, NSUB, SUB]), bc, ALU.subtract)
                step(last)
                dve.wait_ge(s_a, 4)
                step(nc.vector.tensor_tensor(kst[:, :, :], k, low[:, :, :], ALU.mult))
                step(nc.vector.tensor_tensor(k, k, x[:, :, :], ALU.mult))


GLA_DK_SCALE = 64 ** -0.5


def gla_units_phase(nc, S, u, qi, ki, kst, dec):
    H = GLA_HEADS
    with Phase(nc) as ctx:
        sb = lambda n, shape: ctx.enter_context(nc.sbuf_tensor("gu_" + n, shape, F32))
        sem = lambda n: ctx.semaphore("gu_" + n)
        fmaj = sb("fm", [P, 2, 6 + H, P])
        tok = sb("tok", [P, 2, 2 + H, P])
        am = sb("scores", [P, 2, H, P])
        st = sb("state", [P, 2, P])
        s_zero, s_in, s_tp, s_tok, s_a, s_am, s_ds, s_used, s_st, s_out = (sem(n) for n in (
            "zero", "in", "tp", "tok", "a", "am", "ds", "used", "st", "out"))
        tp = S.ps[:, 0:2, :].rearrange("p a n -> p (a n)")
        aps, ops, dps = ([S.ps[:, b, 0:2 * P] for b in pair] for pair in ((2, 7), (3, 4), (5, 6)))
        half = lambda h: slice((h % 2) * HD, (h % 2 + 1) * HD)
        two = lambda ap: ap.rearrange("p (a n) -> p a n", a=2)

        def units(eng, step):
            with eng.Fori(0, NUNIT // 2 - 1) as i:
                for s in range(2):
                    step(i * 2 + s, s, False)
            for s in range(2):
                step(NUNIT - 2 + s, s, s == 1)

        with nc.Block() as block:
            @block.gpsimd
            def _(pool):
                nc.gpsimd.memset(st[:, :, :], 0.0).then_inc(s_zero, 1)

                def fixed(c, s, last):
                    lone_wait(S, pool, s_used, c * 2)
                    at = c * P if isinstance(c, int) else None
                    at = bass.ds(c * P, P) if at is None else slice(at, at + P)
                    for j, src in enumerate((qi, ki, kst)):
                        nc.gpsimd.tensor_copy(fmaj[:, s, 2 * j:2 * j + 2, :], src[:, :, at])
                    nc.gpsimd.tensor_copy(fmaj[:, s, 6:6 + H, :], u[:, GV:GV + H, at]).then_inc(s_in, 1)

                units(pool, fixed)

            @block.tensor
            def _(pe):
                nc.tensor.sem_inc(s_used, 2)

                def front(c, s):
                    pe.wait_ge(s_in, c + 1)
                    pe.wait_ge(s_tok, c)
                    for j in range(2 + H):
                        last = nc.tensor.transpose(tp[:, j * P:(j + 1) * P], fmaj[:, s, 4 + j, :], S.ident[:, :])
                    last.then_inc(s_tp, 1)
                    lone_wait(S, pe, s_am, c)
                    for h in range(H):
                        last = nc.tensor.matmul(aps[h % 2][:, (h // 2) * P:(h // 2 + 1) * P], fmaj[half(h), s, 2 + h // 2, :],
                                                fmaj[half(h), s, h // 2, :], start=True, stop=True)
                    last.then_inc(s_a, 1)

                def step(c, s, last_unit):
                    pe.wait_ge(s_tok, c + 1)
                    pe.wait_ge(s_am, c + 1)
                    pe.wait_ge(s_out, c)
                    for h in range(H):
                        nc.tensor.matmul(ops[h % 2][:, (h // 2) * P:(h // 2 + 1) * P], tok[:, s, 2 + h, :], am[:, s, h, :],
                                         start=(h < 2), stop=False)
                    lone_wait(S, pe, s_st, c * 2)
                    for k in range(2):
                        t = slice(k * SUB, (k + 1) * SUB)
                        for h in range(H):
                            last = nc.tensor.matmul(dps[k][half(h), (h // 2) * P:(h // 2 + 1) * P], tok[t, s, h // 2, half(h)],
                                                    tok[t, s, 2 + h, :], start=True, stop=True)
                        last.then_inc(s_ds, 1)
                    if not last_unit:
                        front(c + 1, 1 - s)
                    for k in range(2):
                        lone_wait(S, pe, s_st, c * 2 + k)
                        t = slice(k * SUB, (k + 1) * SUB)
                        for h in range(H):
                            last = nc.tensor.matmul(ops[h % 2][:, (h // 2) * P + k * SUB:(h // 2) * P + (k + 1) * SUB],
                                                    st[half(h), h // 2, :], fmaj[half(h), s, h // 2, t],
                                                    start=False, stop=(k == 1 and h >= 2))
                        last.then_inc(s_used, 1)

                pe.wait_ge(s_zero, 1)
                front(0, 0)
                units(pe, step)

            @block.vector
            def _(dve):
                def turned(c, s):
                    dve.wait_ge(s_tp, c + 1)
                    nc.vector.tensor_copy(tok[:, s, :, :].rearrange("p a n -> p (a n)"), tp[:, 0:(2 + H) * P]).then_inc(s_tok, 1)

                def masked(c, s):
                    dve.wait_ge(s_a, c + 1)
                    for a in range(2):
                        last = nc.vector.tensor_tensor(am[:, s, a::2, :], two(aps[a]), S.incl[:, :].unsqueeze(1).to_broadcast([P, 2, P]), ALU.mult)
                    last.then_inc(s_am, 1)

                def state(c, k):
                    dve.wait_ge(s_ds, c * 2 + (k + 1))
                    dve.wait_ge(s_used, c * 2 + (k + 3))
                    for j in range(2):
                        n = bass.ds(c * 2 + k, 1) if not isinstance(c, int) else slice(c * 2 + k, c * 2 + k + 1)
                        last = nc.vector.scalar_tensor_tensor(st[:, j, :], st[:, j, :], dec[:, j, n], dps[k][:, j * P:(j + 1) * P],
                                                              ALU.mult, ALU.add)
                    last.then_inc(s_st, 1)

                def step(c, s, last_unit):
                    if not last_unit:
                        turned(c + 1, 1 - s)
                    state(c, 0)
                    if not last_unit:
                        masked(c + 1, 1 - s)
                    state(c, 1)

                turned(0, 0)
                masked(0, 0)
                units(dve, step)

            @block.scalar
            def _(act):
                def step(c, s, last_unit):
                    act.wait_ge(s_used, c * 2 + 4)
                    at = bass.ds(c * P, P) if not isinstance(c, int) else slice(c * P, (c + 1) * P)
                    for a in range(2):
                        last = nc.scalar.activation(u[:, GV + a:GV + H:2, at], two(ops[a]), ACT.Copy)
                    last.then_inc(s_out, 1)

                units(act, step)


def gla_finish_phase(nc, S, u, mhi, mlo, wa, ahead, parked):
    H = GLA_HEADS
    with Phase(nc) as ctx:
        sb = lambda n: ctx.enter_context(nc.sbuf_tensor("gf_" + n, [P, 2, SEQ], F32))
        sem = lambda n: ctx.semaphore("gf_" + n)
        sq, rs = sb("sq"), sb("rs")
        s_sq, s_sum, s_ln, s_rt, s_y, s_hi, s_lo, s_parked = (sem(n) for n in ("sq", "sum", "ln", "rt", "y", "hi", "lo", "parked"))
        with nc.Block() as block:
            @block.scalar
            def _(act):
                nc.scalar.preload_act_table_set("natural_log_exp_and_others")
                for h in range(H):
                    if h >= 2:
                        act.wait_ge(s_sum, h - 1)
                    nc.scalar.activation(sq[:, h % 2, :], u[:, GV + h, :], ACT.Square).then_inc(s_sq, 1)
                for h in range(H):
                    act.wait_ge(s_sum, h + 1)
                    if h >= 2:
                        act.wait_ge(s_y, 2 * (h - 1))
                    nc.scalar.activation(fm(rs[:, h % 2, :], 2), S.ps[:, 2 * h:2 * h + 2, :], ACT.Ln, scale=1.0 / P,
                                         bias=S.eps[:, 0:1]).then_inc(s_ln, 1)
                    act.wait_ge(s_ln, h + 1)
                    nc.scalar.activation(rs[:, h % 2, :], rs[:, h % 2, :], ACT.Exp, scale=-0.5).then_inc(s_rt, 1)
                for h in range(H):
                    act.wait_ge(s_y, 2 * h + 2)
                    nc.scalar.activation(mhi[:, h, :], u[:, GV + h, :], ACT.Copy).then_inc(s_hi, 1)

            @block.tensor
            def _(pe):
                for h in range(H):
                    pe.wait_ge(s_sq, h + 1)
                    for n in range(2):
                        last = nc.tensor.matmul(S.ps[:, 2 * h + n, :], S.ones[:, :], sq[:, h % 2, n * BANK:(n + 1) * BANK], start=True, stop=True)
                    last.then_inc(s_sum, 1)

            @block.vector
            def _(dve):
                nc.vector.tensor_copy(wa[:, :], u[:, GWA, :])
                for h in range(H):
                    dve.wait_ge(s_rt, h + 1)
                    o = u[:, GV + h, :]
                    nc.vector.scalar_tensor_tensor(o, o, col(S, "gla_norm_w_2"), rs[:, h % 2, :], ALU.mult, ALU.mult).then_inc(s_y, 1)
                    dve.wait_ge(s_y, 2 * h + 1)
                    nc.vector.tensor_tensor(o, o, u[:, GG + h, :], ALU.mult).then_inc(s_y, 1)

            @block.sync
            def _(sp):
                fetch_first(sp, ahead)
                for h in range(H):
                    for m, done_, at in ((mhi, s_hi, parked[0]), (mlo, s_lo, parked[1])):
                        sp.wait_ge(done_, h + 1)
                        sp.dma_start(at[:, h, :], m[:, h, :]).then_inc(s_parked, 16)
                sp.wait_ge(s_parked, 2 * H * 16)

            @block.gpsimd
            def _(pool):
                cut_first(nc, S, pool, ahead)
                for h in range(H):
                    pool.wait_ge(s_hi, h + 1)
                    nc.gpsimd.tensor_tensor(mlo[:, h, :], u[:, GV + h, :], mhi[:, h, :], ALU.subtract).then_inc(s_lo, 1)



RR, RK, RV, RG, RWKV_B = 0, 4, 8, 12, 16
RWKV_P = 4
RWKV_H = 2 * RWKV_P
MIXED = 12
DECAY = math.exp(-0.5)
LEVELS = range(1, NLEVEL)
VSTEPS = 11


def rwkv_in_phase(nc, S, L, u, wa):
    with Phase(nc) as ctx:
        d = ctx.enter_context(nc.sbuf_tensor("rwkv_shift", [P, SEQ], F32))
        s_mix = ctx.semaphore("rwkv_mix")

        def mix(step, ub, mu):
            nc.vector.tensor_scalar(d[:, 0:1], ub[:, 0:1], -1.0, None, ALU.mult)
            step(nc.vector.tensor_tensor(d[:, 1:SEQ], ub[:, 0:SEQ - 1], ub[:, 1:SEQ], ALU.subtract))
            step(nc.vector.scalar_tensor_tensor(ub, d[:, :], mu, ub, ALU.mult, ALU.add))

        def shift(dve, L):
            mix(Chain(dve, s_mix), wa[:, :], col(S, "rwkv_mu_2", MIXED))
            with dve.Fori(0, MIXED) as i:
                dve.wait_ge(L.emptied, i + (SLOTS + 1))
                mix(Chain(dve, s_mix, i * 2 + 2), blk(u, i), dcol(S, "rwkv_mu_2", i))

        linear_phase(nc, S, L, normed(S), RWKV_B, u, 2, BANK, after=shift, silu=RG)


def rwkv_prepare_phase(nc, S, A, u, wa, kap, bt, bonus, plast):
    with Phase(nc) as ctx:
        sb = lambda n, shape=(P, SEQ): ctx.enter_context(nc.sbuf_tensor("rp_" + n, list(shape), F32))
        sem = lambda n: ctx.semaphore("rp_" + n)
        up, upb = sb("up", [P, RWKV_P * P]), sb("up_block", [P, P])
        sg, a, cum, ep, en, em, kk, sq, t, rkr = (sb(n) for n in ("sg", "a", "cum", "ep", "en", "em", "kk", "sq", "t", "rkr"))
        (s_up, s_tanh, s_upb, s_x, s_sg, s_v, s_sq, s_sum, s_exp, s_fin, s_pool, s_bon, s_norm, s_ln) = (
            sem(n) for n in ("up_landed", "tanh", "upb", "x", "sg", "v", "sq", "sum", "exp", "fin", "pool", "bon", "norm", "ln"))
        xw, xa, sums, bsum = (S.ps[:, 2 * j:2 * j + 2, :] for j in range(4))
        with nc.Block() as block:
            @block.sync
            def _(sp):
                sp.dma_start(up[:, :], A["decay_a_up"]).then_inc(s_up, 16)
                sp.wait_ge(s_up, 16)

            @block.vector
            def _(dve):
                with dve.Fori(0, RWKV_P) as b:
                    step = Chain(dve, s_v, b * VSTEPS)
                    r, rk = blk(u, b + RR), blk(u, b + RK)
                    dve.wait_ge(s_fin, b)
                    step(nc.vector.tensor_scalar(kk[:, :], rk, dcol(S, "rwkv_k_k_2", b), None, ALU.mult))
                    dve.wait_ge(s_sg, b * 2 + 1)
                    step(nc.vector.tensor_tensor_scan(cum[:, :], S.scan[:, :], sg[:, :], 0.0, ALU.mult, ALU.add))
                    step(nc.vector.tensor_tensor(em[:, :], cum[:, :], sg[:, :], ALU.subtract))
                    dve.wait_ge(s_sg, b * 2 + 2)
                    step(nc.vector.tensor_scalar(t[:, :], a[:, :], -1.0, dcol(S, "rwkv_k_a_2", b), ALU.add, ALU.mult))
                    step(nc.vector.scalar_tensor_tensor(t[:, :], t[:, :], 1.0, rk, ALU.add, ALU.mult))
                    step(nc.vector.scalar_tensor_tensor(rkr[:, :], r, dcol(S, "rwkv_r_k_2", b), t[:, :], ALU.mult, ALU.mult))
                    dve.wait_ge(s_sum, b + 1)
                    step(nc.vector.tensor_scalar(fm(sq[:, :], 2), sums, 1e-24, None, ALU.max))
                    dve.wait_ge(s_exp, b * 3 + 3)
                    nc.vector.tensor_copy(blk(plast, b), ep[:, SUB - 1::SUB])
                    step(nc.vector.tensor_tensor(r, r, ep[:, :], ALU.mult))
                    step(nc.vector.tensor_tensor(rk, t[:, :], en[:, :], ALU.mult))
                    dve.wait_ge(s_norm, b + 1)
                    step(nc.vector.tensor_tensor(kk[:, :], kk[:, :], sq[:, :], ALU.mult))
                    dve.wait_ge(s_bon, b + 1)
                    step(nc.vector.tensor_tensor(fm(blk(bonus, b), 2), bsum, fm(blk(u, b + RV), 2), ALU.mult))

            @block.gpsimd
            def _(pool):
                with pool.Fori(0, RWKV_P) as b:
                    lone_wait(S, pool, s_v, b * VSTEPS + 10)
                    lone_wait(S, pool, s_exp, b * 3 + 3)
                    nc.gpsimd.tensor_tensor(blk(kap, b), kk[:, :], em[:, :], ALU.mult)
                    nc.gpsimd.tensor_tensor(kk[:, :], kk[:, :], a[:, :], ALU.mult).then_inc(s_pool, 1)
                    lone_wait(S, pool, s_pool, b + 1)
                    nc.gpsimd.tensor_tensor(blk(bt, b), kk[:, :], en[:, :], ALU.mult).then_inc(s_fin, 1)

            @block.tensor
            def _(pe):
                with pe.Fori(0, RWKV_P) as b:
                    pe.wait_ge(s_upb, b + 1)
                    for n in range(2):
                        cols = slice(n * BANK, (n + 1) * BANK)
                        nc.tensor.matmul(xw[:, n, :], upb[0:HD, :], wa[0:HD, cols], start=True, stop=True)
                        last = nc.tensor.matmul(xa[:, n, :], upb[HD:P, :], wa[HD:P, cols], start=True, stop=True)
                    last.then_inc(s_x, 1)
                    pe.wait_ge(s_sq, b + 1)
                    for n in range(2):
                        last = nc.tensor.matmul(sums[:, n, :], S.same[:, :], sq[:, n * BANK:(n + 1) * BANK], start=True, stop=True)
                    last.then_inc(s_sum, 1)
                    pe.wait_ge(s_v, b * VSTEPS + 6)
                    for n in range(2):
                        last = nc.tensor.matmul(bsum[:, n, :], S.same[:, :], rkr[:, n * BANK:(n + 1) * BANK], start=True, stop=True)
                    last.then_inc(s_bon, 1)

            @block.scalar
            def _(act):
                act.wait_ge(s_up, 16)
                nc.scalar.activation(wa[0:HD, :], wa[0:HD, :], ACT.Tanh).then_inc(s_tanh, 1)
                act.wait_ge(s_tanh, 1)
                with act.Fori(0, RWKV_P) as b:
                    act.wait_ge(s_x, b)
                    nc.scalar.activation(upb[:, :], up[:, bass.ds(b * P, P)], ACT.Copy).then_inc(s_upb, 1)
                    act.wait_ge(s_v, b * VSTEPS + 1)
                    nc.scalar.activation(sq[:, :], kk[:, :], ACT.Square).then_inc(s_sq, 1)
                    act.wait_ge(s_x, b + 1)
                    act.wait_ge(s_fin, b)
                    nc.scalar.activation(fm(sg[:, :], 2), xw, ACT.Sigmoid, bias=dcol(S, "rwkv_w0_2", b)).then_inc(s_sg, 1)
                    nc.scalar.activation(fm(a[:, :], 2), xa, ACT.Sigmoid, bias=dcol(S, "rwkv_a0_2", b)).then_inc(s_sg, 1)
                    nc.scalar.preload_act_table_set("natural_log_exp_and_others")
                    act.wait_ge(s_v, b * VSTEPS + 3)
                    nc.scalar.activation(ep[:, :], cum[:, :], ACT.Exp, scale=-DECAY).then_inc(s_exp, 1)
                    nc.scalar.activation(en[:, :], cum[:, :], ACT.Exp, scale=DECAY).then_inc(s_exp, 1)
                    nc.scalar.activation(em[:, :], em[:, :], ACT.Exp, scale=-DECAY).then_inc(s_exp, 1)
                    act.wait_ge(s_v, b * VSTEPS + 7)
                    nc.scalar.activation(sq[:, :], sq[:, :], ACT.Ln).then_inc(s_ln, 1)
                    act.wait_ge(s_ln, b + 1)
                    nc.scalar.activation(sq[:, :], sq[:, :], ACT.Exp, scale=-0.5).then_inc(s_norm, 1)


def rwkv_units_phase(nc, S, u, kap, bt, plast):
    H = RWKV_H
    KAP, RT, BT, KT, VV = range(5)
    with Phase(nc) as ctx:
        sb = lambda n, shape: ctx.enter_context(nc.sbuf_tensor("ru_" + n, shape, F32))
        sem = lambda n: ctx.semaphore("ru_" + n)
        fx = sb("fm", [P, 5, RWKV_P, P])
        tok = sb("tok", [P, 3, RWKV_P, 2, HD])
        z = sb("kk_akv", [P, H, 2, HD])
        ab, rb, ak, rkm = (sb(n, [P, H, P]) for n in ("ab", "rb", "ak", "rk"))
        am = sb("a_level", [P, 2, H, P])
        x, xt, t1, first = (sb(n, [P, H, P]) for n in ("x", "xt", "t1", "a_first"))
        nw = sb("removed", [P, H, 2, HD])
        g = sb("g", [P, 2, RWKV_P, HD])
        rr = sb("rr", [P, RWKV_P, P])
        st = sb("state", [P, 2, RWKV_P, HD])
        eye2 = sb("eye2", [P, HD])
        (s_in, s_am, s_tr, s_ab, s_ak, s_l0, s_akv, s_t1, s_dx, s_w, s_g, s_rr, s_gs, s_zero,
         s_tokb, s_abm, s_first, s_rbm, s_akm, s_rkm, s_x, s_z, s_gc, s_rrc, s_state, s_tokv, s_t1c, s_nw, s_y, s_yd, s_h) = (sem(n) for n in (
            "in", "am", "tr", "ab", "ak", "l0", "akv", "t1", "dx", "w", "g", "rr", "gs", "zero",
            "tokb", "abm", "first", "rbm", "akm", "rkm", "x", "z", "gc", "rrc", "state", "tokv", "t1c", "nw", "y", "yd", "h"))
        two = [S.ps[:, 2 * j:2 * j + 2, :].rearrange("p a n -> p (a n)") for j in range(4)]
        heads = lambda ap: ap.rearrange("p (h n) -> p h n", h=H)
        mask = lambda m: m.unsqueeze(1).to_broadcast([P, H, P])
        akv_ps, rr_ps, y_ps = (S.ps[:, b, :] for b in (6, 4, 5))
        g_ps, h_ps = [S.ps[:, k, 0:4 * HD] for k in range(2)], [S.ps[:, 2 + k, 0:4 * HD] for k in range(2)]
        HEADS_BY_BLOCK = [a * RWKV_P + q for q in range(RWKV_P) for a in range(2)]
        half = lambda h: slice((h // RWKV_P) * HD, (h // RWKV_P + 1) * HD)
        first_in_bank, last_in_bank = (lambda h: h % RWKV_P == 0), (lambda h: h % RWKV_P == RWKV_P - 1)
        by_half = lambda ap: ap.rearrange("p (q a n) -> p a q n", q=RWKV_P, a=2)
        NL = len(LEVELS)
        group = lambda a: range(a * RWKV_P, (a + 1) * RWKV_P)
        level = lambda c, l, a: c * (2 * NL) + ((l - 1) * 2 + a + 1)
        inverse = lambda c, l, a: c * (2 * NL + 2) + (l * 2 + a + 1)
        dx_ps, dxt_ps = ([S.ps[:, 4 + a, o * 4 * HD:(o + 1) * 4 * HD] for a in range(2)] for o in range(2))

        def side(buf, h0, h1, l, right):
            return buf[:, h0:h1, :].rearrange("p h (b c t) -> p (h b) c t", c=2, t=1 << l)[:, :, right, :]

        with nc.Block() as block:
            @block.gpsimd
            def _(pool):
                nc.gpsimd.memset(st[:, :, :, :], 0.0).then_inc(s_zero, 1)
                nc.gpsimd.tensor_tensor(eye2[:, :], S.ident[:, 0:HD], S.ident[:, HD:P], ALU.add).then_inc(s_zero, 1)
                with pool.Fori(0, NUNIT) as c:
                    lone_wait(S, pool, s_ak, c * 2)
                    at = bass.ds(c * P, P)
                    for j, src in ((KAP, kap[:, :, at]), (RT, u[:, RR:RR + RWKV_P, at]), (BT, bt[:, :, at]),
                                   (KT, u[:, RK:RK + RWKV_P, at]), (VV, u[:, RV:RV + RWKV_P, at])):
                        last = nc.gpsimd.tensor_copy(fx[:, j, :, :], src)
                    last.then_inc(s_in, 1)
                    lone_wait(S, pool, s_abm, c + 1)
                    for l in LEVELS:
                        if l > 2:
                            lone_wait(S, pool, s_t1, level(c, l - 2, 1))
                        else:
                            lone_wait(S, pool, s_w, c)
                        nc.gpsimd.tensor_tensor(am[:, l % 2, :, :], ab[:, :, :], mask(S.levels[:, l, :]), ALU.mult).then_inc(s_am, 1)

            @block.tensor
            def _(pe):
                with pe.Fori(0, NUNIT) as c:
                    pe.wait_ge(s_in, c + 1)
                    pe.wait_ge(s_state, c * 2)
                    for j, (kind, out) in enumerate(((KAP, two[0][:, 0:BANK]), (BT, two[0][:, BANK:]), (KT, two[1][:, 0:BANK]), (VV, two[1][:, BANK:]))):
                        for p in range(RWKV_P):
                            last = nc.tensor.transpose(out[:, p * P:(p + 1) * P], fx[:, kind, p, :], S.ident[:, :])
                    last.then_inc(s_tr, 1)
                    lone_wait(S, pe, s_y, c)

                    def products_with(key, kind, out):
                        for h in HEADS_BY_BLOCK:
                            last = nc.tensor.matmul(out[:, h * P:(h + 1) * P], fx[half(h), key, h % RWKV_P, :], fx[half(h), kind, h % RWKV_P, :],
                                                    start=True, stop=True)
                        return last

                    products_with(BT, KAP, two[2]).then_inc(s_ab, 1)
                    products_with(BT, RT, two[3]).then_inc(s_ab, 1)
                    lone_wait(S, pe, s_tokb, c + 1)
                    lone_wait(S, pe, s_tokv, c + 1)
                    products_with(KT, KAP, two[0]).then_inc(s_ak, 1)
                    pe.wait_ge(s_first, c + 1)
                    for h in HEADS_BY_BLOCK:
                        last = nc.tensor.transpose(two[2][:, h * P:(h + 1) * P], first[:, h, :], S.ident[:, :])
                    last.then_inc(s_l0, 1)
                    products_with(KT, RT, two[1]).then_inc(s_ak, 1)
                    lone_wait(S, pe, s_akm, c + 1)
                    lone_wait(S, pe, s_rbm, c + 1)
                    for h in HEADS_BY_BLOCK:
                        last = nc.tensor.matmul(akv_ps[:, h * HD:(h + 1) * HD], ak[:, h, :], tok[:, 2, h % RWKV_P, h // RWKV_P, :], start=True, stop=True)
                    last.then_inc(s_akv, 1)
                    for l in LEVELS:
                        pe.wait_ge(s_am, c * NL + l)
                        for a in range(2):
                            pe.wait_ge(s_x, inverse(c, l - 1, a))
                            for h in group(a):
                                last = nc.tensor.matmul(two[0][:, h * P:(h + 1) * P], am[:, l % 2, h, :], x[:, h, :], start=True, stop=True)
                            last.then_inc(s_t1, 1)
                        for a in range(2):
                            pe.wait_ge(s_t1c, level(c, l, a))
                            if l != LEVELS[-1]:
                                for q, h in enumerate(group(a)):
                                    nc.tensor.matmul(dx_ps[a][:, q * HD:(q + 1) * HD], xt[:, h, :], side(t1, h, h + 1, l, 0), start=True, stop=True)
                            for q, h in enumerate(group(a)):
                                last = nc.tensor.matmul(dxt_ps[a][:, q * HD:(q + 1) * HD], t1[:, h, :], side(xt, h, h + 1, l, 1), start=True, stop=True)
                            last.then_inc(s_dx, 1)
                    pe.wait_ge(s_x, inverse(c, NL, 1))
                    pe.wait_ge(s_z, c + 1)
                    for h in HEADS_BY_BLOCK:
                        last = nc.tensor.matmul(two[0][:, h * P:(h + 1) * P], xt[:, h, :], z[:, h, :, :].rearrange("p a n -> p (a n)"),
                                                start=True, stop=True)
                    last.then_inc(s_w, 1)
                    lone_wait(S, pe, s_rkm, c + 1)
                    state_cols = lambda h: slice((h % RWKV_P) * HD, (h % RWKV_P + 1) * HD)
                    for k in range(2):
                        i = slice(k * SUB, (k + 1) * SUB)
                        for h in HEADS_BY_BLOCK:
                            nc.tensor.matmul(h_ps[k][half(h), state_cols(h)], tok[i, 1, h % RWKV_P, h // RWKV_P, :],
                                             tok[i, 2, h % RWKV_P, h // RWKV_P, :], start=first_in_bank(h), stop=False)
                    y_cols = lambda h: slice((h % RWKV_P) * P, (h % RWKV_P + 1) * P)
                    for h in HEADS_BY_BLOCK:
                        nc.tensor.matmul(y_ps[half(h), y_cols(h)], tok[:, 2, h % RWKV_P, h // RWKV_P, :], rkm[:, h, :], start=first_in_bank(h), stop=False)
                    lone_wait(S, pe, s_nw, c + 1)
                    for k in range(2):
                        i = slice(k * SUB, (k + 1) * SUB)
                        for h in HEADS_BY_BLOCK:
                            last = nc.tensor.matmul(g_ps[k][half(h), state_cols(h)], nw[i, h, 0, :], tok[i, 0, h % RWKV_P, h // RWKV_P, :], start=True, stop=True)
                    last.then_inc(s_g, 1)
                    for h in HEADS_BY_BLOCK:
                        last = nc.tensor.matmul(rr_ps[half(h), y_cols(h)], nw[:, h, 0, :], rb[:, h, :], start=True, stop=True)
                    last.then_inc(s_rr, 1)
                    for k in range(2):
                        i = slice(k * SUB, (k + 1) * SUB)
                        for h in HEADS_BY_BLOCK:
                            last = nc.tensor.matmul(h_ps[k][half(h), state_cols(h)], tok[i, 0, h % RWKV_P, h // RWKV_P, :], nw[i, h, 1, :], start=False, stop=False)
                    last.then_inc(s_h, 1)
                    for h in HEADS_BY_BLOCK:
                        nc.tensor.matmul(y_ps[half(h), y_cols(h)], nw[:, h, 1, :], rb[:, h, :], start=False, stop=False)
                    lone_wait(S, pe, s_gc, c + 1)
                    lone_wait(S, pe, s_rrc, c + 1)
                    lone_wait(S, pe, s_h, c + 1)
                    for k in range(2):
                        lone_wait(S, pe, s_state, c * 2 + k)
                        for h in HEADS_BY_BLOCK:
                            last = nc.tensor.matmul(h_ps[k][half(h), state_cols(h)], g[half(h), k, h % RWKV_P, :], st[half(h), k, h % RWKV_P, :],
                                                    start=False, stop=last_in_bank(h))
                        last.then_inc(s_gs, 1)
                        for h in HEADS_BY_BLOCK:
                            o = slice((h % RWKV_P) * P + k * SUB, (h % RWKV_P) * P + (k + 1) * SUB)
                            last = nc.tensor.matmul(y_ps[half(h), o], st[half(h), k, h % RWKV_P, :], rr[half(h), h % RWKV_P, k * SUB:(k + 1) * SUB],
                                                    start=False, stop=(k == 1 and last_in_bank(h)))
                    last.then_inc(s_yd, 1)

            @block.vector
            def _(dve):
                dve.wait_ge(s_zero, 2)
                with dve.Fori(0, NUNIT) as c:
                    dve.wait_ge(s_tr, c + 1)
                    nc.vector.tensor_copy(z[:, :, 0, :].rearrange("p (a q) n -> p a q n", a=2), by_half(two[0][:, 0:BANK]))
                    nc.vector.tensor_copy(tok[:, 0, :, :, :].rearrange("p q a n -> p (q a n)"), two[0][:, BANK:]).then_inc(s_tokb, 1)
                    dve.wait_ge(s_ab, c * 2 + 1)
                    nc.vector.tensor_tensor(ab[:, :, :], heads(two[2]), mask(S.excl[:, :]), ALU.mult).then_inc(s_abm, 1)
                    dve.wait_ge(s_abm, c + 1)
                    nc.vector.tensor_tensor(first[:, :, :], ab[:, :, :], mask(S.levels[:, 0, :]), ALU.mult).then_inc(s_first, 1)
                    dve.wait_ge(s_first, c + 1)
                    nc.vector.scalar_tensor_tensor(xt[:, :, :], first[:, :, :], -1.0, mask(S.ident[:, :]), ALU.mult, ALU.add)
                    dve.wait_ge(s_ab, c * 2 + 2)
                    nc.vector.tensor_tensor(rb[:, :, :], heads(two[3]), mask(S.incl[:, :]), ALU.mult).then_inc(s_rbm, 1)
                    dve.wait_ge(s_ak, c * 2 + 1)
                    nc.vector.tensor_tensor(ak[:, :, :], heads(two[0]), mask(S.excl[:, :]), ALU.mult).then_inc(s_akm, 1)
                    dve.wait_ge(s_l0, c + 1)
                    for a in range(2):
                        mine = slice(a * RWKV_P, (a + 1) * RWKV_P)
                        nc.vector.scalar_tensor_tensor(x[:, mine, :], heads(two[2])[:, mine, :], -1.0,
                                                       S.ident[:, :].unsqueeze(1).to_broadcast([P, RWKV_P, P]), ALU.mult, ALU.add).then_inc(s_x, 1)
                    dve.wait_ge(s_ak, c * 2 + 2)
                    nc.vector.tensor_tensor(rkm[:, :, :], heads(two[1]), mask(S.incl[:, :]), ALU.mult).then_inc(s_rkm, 1)
                    dve.wait_ge(s_akv, c + 1)
                    nc.vector.tensor_copy(z[:, :, 1, :], akv_ps.rearrange("p (h n) -> p h n", h=H)).then_inc(s_z, 1)
                    for l in LEVELS:
                        for a in range(2):
                            dve.wait_ge(s_x, inverse(c, l - 1, a))
                            dve.wait_ge(s_dx, level(c, l, a))
                            for buf, ps, right in ((x, dx_ps[a], 0), (xt, dxt_ps[a], 1)):
                                if buf is x and l == LEVELS[-1]:
                                    continue
                                cols = side(buf, a * RWKV_P, (a + 1) * RWKV_P, l, right)
                                last = nc.vector.tensor_tensor(cols, cols, ps.rearrange("p (b t) -> p b t", t=1 << l), ALU.subtract)
                            last.then_inc(s_x, 1)
                    dve.wait_ge(s_g, c + 1)
                    for k in range(2):
                        last = nc.vector.tensor_tensor(g[:, k, :, :], g_ps[k].rearrange("p (q n) -> p q n", q=RWKV_P),
                                                       eye2[:, :].unsqueeze(1).to_broadcast([P, RWKV_P, HD]), ALU.add)
                    last.then_inc(s_gc, 1)
                    dve.wait_ge(s_rr, c + 1)
                    nc.vector.tensor_tensor(rr[:, :, :], rr_ps.rearrange("p (q n) -> p q n", q=RWKV_P),
                                            u[:, RR:RR + RWKV_P, bass.ds(c * P, P)], ALU.add).then_inc(s_rrc, 1)
                    for k in range(2):
                        dve.wait_ge(s_gs, c * 2 + (k + 1))
                        nc.vector.tensor_tensor(st[:, 1 - k, :, :], h_ps[k].rearrange("p (q n) -> p q n", q=RWKV_P),
                                                plast[:, :, bass.ds(c * 2 + k, 1)].to_broadcast([P, RWKV_P, HD]), ALU.mult).then_inc(s_state, 1)

            @block.scalar
            def _(act):
                with act.Fori(0, NUNIT) as c:
                    act.wait_ge(s_tr, c + 1)
                    act.wait_ge(s_state, c * 2)
                    nc.scalar.activation(tok[:, 1:3, :, :, :].rearrange("p j q a n -> p (j q a n)"), two[1], ACT.Copy).then_inc(s_tokv, 1)
                    for l in LEVELS:
                        for a in range(2):
                            mine = slice(a * RWKV_P, (a + 1) * RWKV_P)
                            act.wait_ge(s_t1, level(c, l, a))
                            nc.scalar.activation(t1[:, mine, :], heads(two[0])[:, mine, :], ACT.Copy).then_inc(s_t1c, 1)
                    act.wait_ge(s_w, c + 1)
                    nc.scalar.activation(nw[:, :, :, :].rearrange("p h a n -> p (h a n)"), two[0], ACT.Copy, scale=-1.0).then_inc(s_nw, 1)
                    act.wait_ge(s_yd, c + 1)
                    nc.scalar.activation(u[:, RR:RR + RWKV_P, bass.ds(c * P, P)], y_ps.rearrange("p (q n) -> p q n", q=RWKV_P),
                                         ACT.Copy).then_inc(s_y, 1)


def rwkv_finish_phase(nc, S, u, bonus, mhi, mlo, ahead, fetch_back):
    with Phase(nc) as ctx:
        sb = lambda n: ctx.enter_context(nc.sbuf_tensor("rf_" + n, [P, SEQ], F32))
        sem = lambda n: ctx.semaphore("rf_" + n)
        dev, sq, rs = sb("dev"), sb("sq"), sb("rs")
        s_mean, s_v, s_sq, s_var, s_ln, s_rt, s_hi, s_lo = (sem(n) for n in ("mean", "v", "sq", "var", "ln", "rt", "hi", "lo"))
        mean, var = S.ps[:, 0:2, :], S.ps[:, 2:4, :]
        V = 4
        with nc.Block() as block:
            @block.scalar
            def _(act):
                nc.scalar.preload_act_table_set("natural_log_exp_and_others")
                with act.Fori(0, RWKV_P) as b:
                    act.wait_ge(s_v, b * V + 1)
                    nc.scalar.activation(sq[:, :], dev[:, :], ACT.Square).then_inc(s_sq, 1)
                    act.wait_ge(s_var, b + 1)
                    nc.scalar.activation(fm(rs[:, :], 2), var, ACT.Ln, scale=1.0 / HD, bias=S.gn_eps[:, 0:1]).then_inc(s_ln, 1)
                    act.wait_ge(s_ln, b + 1)
                    nc.scalar.activation(rs[:, :], rs[:, :], ACT.Exp, scale=-0.5).then_inc(s_rt, 1)
                    act.wait_ge(s_v, b * V + 4)
                    nc.scalar.activation(blk(mhi, b + RWKV_P), dev[:, :], ACT.Copy).then_inc(s_hi, 1)

            @block.tensor
            def _(pe):
                with pe.Fori(0, RWKV_P) as b:
                    pe.wait_ge(s_v, b * V)
                    for n in range(2):
                        last = nc.tensor.matmul(mean[:, n, :], S.same[:, :], blk(u, b + RR)[:, n * BANK:(n + 1) * BANK], start=True, stop=True)
                    last.then_inc(s_mean, 1)
                    pe.wait_ge(s_sq, b + 1)
                    for n in range(2):
                        last = nc.tensor.matmul(var[:, n, :], S.same[:, :], sq[:, n * BANK:(n + 1) * BANK], start=True, stop=True)
                    last.then_inc(s_var, 1)

            @block.vector
            def _(dve):
                with dve.Fori(0, RWKV_P) as b:
                    step = Chain(dve, s_v, b * V)
                    dve.wait_ge(s_mean, b + 1)
                    dve.wait_ge(s_lo, b)
                    step(nc.vector.scalar_tensor_tensor(fm(dev[:, :], 2), mean, -1.0 / HD, fm(blk(u, b + RR), 2), ALU.mult, ALU.add))
                    dve.wait_ge(s_rt, b + 1)
                    step(nc.vector.scalar_tensor_tensor(dev[:, :], dev[:, :], dcol(S, "rwkv_ln_w_2", b), rs[:, :], ALU.mult, ALU.mult))
                    step(nc.vector.scalar_tensor_tensor(dev[:, :], dev[:, :], dcol(S, "rwkv_ln_b_2", b), blk(bonus, b), ALU.add, ALU.add))
                    step(nc.vector.tensor_tensor(dev[:, :], dev[:, :], blk(u, b + RG), ALU.mult))

            @block.sync
            def _(sp):
                fetch_first(sp, ahead)
                fetch_back(sp)

            @block.gpsimd
            def _(pool):
                cut_first(nc, S, pool, ahead)
                with pool.Fori(0, RWKV_P) as b:
                    lone_wait(S, pool, s_hi, b + 1)
                    nc.gpsimd.tensor_tensor(blk(mlo, b + RWKV_P), dev[:, :], blk(mhi, b + RWKV_P), ALU.subtract).then_inc(s_lo, 1)



def scratch(nc, name, shape, dt=F32):
    return nc.dram_tensor(name, shape, dt, kind="Internal").ap()


def second_layer(nc, S, A, out):
    h = S.h[:, :, META:T]
    parked_h = scratch(nc, "parked_h", (P, DB, SEQ))
    parked_gla = [scratch(nc, n, (P, GLA_HEADS, SEQ), F16) for n in ("parked_gla_hi", "parked_gla_lo")]
    with Phase(nc) as ctx:
        sb = lambda e, n, shape, dt=F32, **kw: e.enter_context(nc.sbuf_tensor(n, shape, dt, **kw))
        S.same, S.incl, S.excl = (sb(ctx, n, [P, P]) for n in ("same_chunk", "incl", "excl"))
        S.scan, S.levels = sb(ctx, "scan_starts", [P, SEQ]), sb(ctx, "levels", [P, NLEVEL, P])
        s_set, s_scan, s_parked, s_back, s_result = (ctx.semaphore(n) for n in ("masks_set", "scan_set", "h_parked", "parked_back", "result_out"))
        wa = sb(ctx, "rwkv_low_ranks", [P, SEQ])
        inp = ExitStack()
        S.xhi, S.xlo = (sb(inp, n, [P, DB, SEQ], F16, side="right") for n in ("second_x_hi", "second_x_lo"))

        def park_h(sp):
            sp.dma_start(parked_h, h).then_inc(s_parked, 16)
            sp.wait_ge(s_parked, 16)

        with ExitStack() as gla:
            m1 = [sb(gla, n, [P, GLA_HEADS, SEQ], F16) for n in ("gla_hi", "gla_lo")]
            with Phase(nc) as layer:
                L = linear_buffers(nc, layer, A["w_gla"], 0, DB, "gla", "right")
                N = norm_cut(nc, layer, "second_y", h, "norm_w_2", DB, SEQ, S.xhi, S.xlo)
                norm_phase(nc, S, "second", h, "norm_w_2", DB, SEQ, ("rs", N), 2, BANK, ahead=L, sync=park_h,
                           extra=lambda pool: scan_starts(nc, S, pool, s_scan))
                u = sb(gla, "gla_u", [P, GLA_B, SEQ])
                kst, dec = sb(gla, "gla_kst", [P, 2, SEQ]), sb(gla, "gla_dec", [P, 2, NSUB])
                gla_in_phase(nc, S, A, L, N, u, kst, dec, s_set)
            gla_units_phase(nc, S, u, u[:, GQ:GQ + 2, :], u[:, GK:GK + 2, :], kst, dec)
            layer = Phase(nc)
            L = linear_buffers(nc, layer, A["w_rwkv"], 0, DB, "rwkv", "right")
            gla_finish_phase(nc, S, u, *m1, wa, L, parked_gla)
        with ExitStack() as rwkv:
            u = sb(rwkv, "rwkv_u", [P, RWKV_B, SEQ])
            rwkv_in_phase(nc, S, L, u, wa[:, :])
            layer.close()
            inp.close()
            S.free_h()
            plast = sb(rwkv, "rwkv_last", [P, RWKV_P, NSUB])
            bonus = sb(rwkv, "rwkv_bonus", [P, RWKV_P, SEQ])
            with ExitStack() as e:
                kap, bt = (sb(e, n, [P, RWKV_P, SEQ]) for n in ("rwkv_kap", "rwkv_bt"))
                rwkv_prepare_phase(nc, S, A, u, wa, kap, bt, bonus, plast)
                rwkv_units_phase(nc, S, u, kap, bt, plast)
            back = sb(ctx, "h_back", [P, DB, SEQ], side="right")
            m = [sb(ctx, n, [P, 2 * RWKV_P, SEQ], F16, side="right") for n in ("merged_hi", "merged_lo")]
            layer = Phase(nc)
            L = linear_buffers(nc, layer, A["w_out_2"], 0, DB, "out2", "right")

            def fetch_back(sp):
                for n in range(2):
                    sp.dma_start(m[n][:, 0:GLA_HEADS, :], parked_gla[n]).then_inc(s_back, 16)
                sp.dma_start(back[:, :, :], parked_h).then_inc(s_back, 16)
                sp.wait_ge(s_back, 3 * 16)

            rwkv_finish_phase(nc, S, u, bonus, *m, L, fetch_back)
        linear_phase(nc, S, L, lambda k: (m[0][:, k, :], m[1][:, k, :]), DB, back, 2, BANK, plus=back)
        layer.close()
        res = sb(ctx, "result_fm", [P, DB, SEQ])
        norm_phase(nc, S, "final", back, "final_norm_w_2", DB, SEQ, ("to", res, out, s_result), 2, BANK)



def persistent(nc, ctx, S):
    sb = lambda n, shape, dt=F32: ctx.enter_context(nc.sbuf_tensor(n, shape, dt))
    S.cols = sb("params", [P, NCOL])
    S.ones = sb("ones", [P, P])
    S.ident = sb("ident", [P, P])
    S.upper = sb("upper", [P, P])
    S.strict = sb("strict", [P, P])
    S.tri8 = sb("tri8", [P, P])
    S.ones8 = sb("ones8", [P, P])
    S.eps = sb("eps", [P, 1])
    S.gn_eps = sb("gn_eps", [P, 1])
    S.waited = ctx.enter_context(nc.semaphore("waited"))
    S.ps = ctx.enter_context(nc.psum_tensor("ps", [P, 8, BANK], F32))


def program(nc, A, out):
    with ExitStack() as ctx:
        S = Names()
        Phase.cleared.clear()
        persistent(nc, ctx, S)
        constants_phase(nc, S, A)
        with ExitStack() as mix:
            sb = lambda n, shape, dt=F32: mix.enter_context(nc.sbuf_tensor(n, shape, dt))
            S.z = sb("z", [P, DB, TP])
            with ExitStack() as inp:
                S.xhi, S.xlo = (inp.enter_context(nc.sbuf_tensor(n, [P, DB, TW], F16)) for n in ("x_hi", "x_lo"))
                layer_z, layer_xbc = Phase(nc), Phase(nc)
                Lz = linear_buffers(nc, layer_z, A["w_z"], 0, DB, "z", "right")
                Lx = linear_buffers(nc, layer_xbc, A["w_in"], DB, DB, "xbc", "right")
                h = S.z[:, :, 0:TW]
                Nx = norm_cut(nc, layer_xbc, "mix_pre_y", h, "mix_pre_g", DB, TW, S.xhi, S.xlo)
                norm_phase(nc, S, "mix_pre", h, "mix_pre_g", DB, TW, ("rs", Nx), ahead=Lx, load=(h, A["hT"]))
                with ExitStack() as ssd:
                    S.xbc = ssd.enter_context(nc.sbuf_tensor("xbc", [P, XBC_B, TP], F32))
                    S.dt = ssd.enter_context(nc.sbuf_tensor("dt", [HEADS, 2, TP], F32))
                    xbc_phase(nc, S, Lx, Nx, Lz)
                    layer_xbc.close()
                    z_dt_phase(nc, S, Lz)
                    layer_z.close()
                    ssd_phase(nc, S)
                y1_scope = ExitStack()
                y1 = [y1_scope.enter_context(nc.sbuf_tensor(n, [P, DB, TW], F16, side="right")) for n in ("y_ssd_hi", "y_ssd_lo")]
                layer = Phase(nc)
                L = linear_buffers(nc, layer, A["w_qkv"], 0, DB, "qkv0", "right")
                N = norm_cut(nc, layer, "ssd_y", S.z, "ssd_norm_g", DB, TW, *y1)
                norm_phase(nc, S, "ssd", S.z, "ssd_norm_g", DB, TW, ("rs", N), ahead=L)
                with ExitStack() as att:
                    S.qk = att.enter_context(nc.sbuf_tensor("qk", [P, 2 * HALF, TW], F16))
                    S.v2 = att.enter_context(nc.sbuf_tensor("v2", [P, NCH, HALF, P], F16))
                    for half in range(2):
                        if half:
                            layer = Phase(nc)
                            L = linear_buffers(nc, layer, A["w_qkv"], QKV_B, DB, "qkv1", "right")
                        qkv_phase(nc, S, L, half, None if half else N)
                        layer.close()
                        attention_phase(nc, S, half)
            y2 = [sb(n, [P, DB, TW], F16) for n in ("y_sb_hi", "y_sb_lo")]
            mixed = S.z[:, :, 0:TW]
            with Phase(nc) as layer:
                L = linear_buffers(nc, layer, A["w_out"], 0, DB, "out", "right", parts=2)
                N = norm_cut(nc, layer, "sb_y", S.z, "sb_norm_g", DB, TW, *y2)
                norm_phase(nc, S, "sb", S.z, "sb_norm_g", DB, TW, ("rs", N), ahead=L)
                y = layer.enter_context(nc.sbuf_tensor("y_sb_slots", [P, 4, TW], F32))
                N.y = [y[:, j, :] for j in range(4)]
                linear_phase(nc, S, L, lambda k: tuple(y[:, k % DB, :] for y in ((y1, y2)[k // DB])), DB, mixed, norm=N, norm_from=DB)
            y1_scope.close()
            h_scope = ExitStack()
            S.h = h_scope.enter_context(nc.sbuf_tensor("h", [P, DB, TW], F32, side="right"))
            S.free_h = h_scope.close
            norm_phase(nc, S, "mix_post", mixed, "mix_post_g", DB, TW, ("add", S.h), load=(S.h, A["hT"]))
        ffn(nc, S, A)
        second_layer(nc, S, A, out)



def lay_out(inputs):
    import numpy as np
    get = lambda n: np.ascontiguousarray(np.asarray(inputs[n]))
    cols = np.zeros((P, NCOL), np.float32)

    def put(name, a, per=1):
        at, n = _COLS[name]
        cols[:a.shape[0], at:at + n] = a

    feature = lambda a: np.ascontiguousarray(a.reshape(-1, P).T)
    taps = lambda a: np.ascontiguousarray(a.reshape(a.shape[0], -1, P).transpose(2, 1, 0).reshape(P, -1))
    for name in _COLS:
        a = get(name)
        if name in ("ssd_conv_w", "ffn_conv_w"):
            put(name, taps(a[0]))
        elif name == "ssd_d":
            put(name, np.repeat(a[0].reshape(PAIRS, 2).T, HD, axis=0))
        elif name in ("ssd_dt_bias", "ssd_a_log"):
            put(name, a.reshape(-1, 1))
        else:
            put(name, feature(a.reshape(-1)))

    def blocks(w, parts=1):
        k, n = w.shape
        v = w.reshape(parts, k // P // parts, P, n // P, P).transpose(3, 0, 2, 1, 4)
        return np.ascontiguousarray(v).reshape(n // P * parts, P, k // parts)

    w_in = get("w_in")[0]
    z0, x0, d0, q0, k0, v0, end = 0, 1024, 2560, 2576, 3600, 4624, 5648
    zw = np.concatenate([w_in[:, z0:x0], w_in[:, d0:d0 + P]], axis=1)
    halves = [w_in[:, o + 512 * g:o + 512 * (g + 1)] for g in range(2) for o in (q0, k0, v0)]
    w_up = get("w_up")[0].reshape(D, 2, FFB, P)
    w2 = get("w_in_2")[0]
    h = np.concatenate([get("meta_tokens"), get("x")[0]], axis=0)
    return {
        "hT": np.ascontiguousarray(h.T.reshape(DB, P, T).transpose(1, 0, 2)),
        "cols": cols,
        "w_in": blocks(w_in[:, 0:d0]),
        "w_z": blocks(zw),
        "w_qkv": blocks(np.concatenate(halves, axis=1)),
        "w_out": blocks(get("w_out")[0], 2),
        "w_up": blocks(np.ascontiguousarray(w_up.transpose(0, 2, 1, 3)).reshape(D, -1)),
        "w_down": blocks(get("w_down")[0], 2),
        "w_gla": blocks(np.concatenate([w2[:, 1024:1152], w2[:, 3088:3216], w2[:, 0:1024], w2[:, 1040:1552]], axis=1)),
        "w_rwkv": blocks(np.concatenate([w2[:, 1552:3088], w2[:, 3216:3728]], axis=1)),
        "w_out_2": blocks(get("w_out_2")[0]),
        "gate_up": get("gla_gate_up_2")[0],
        "decay_a_up": np.concatenate([get("rwkv_w_up_2")[0], get("rwkv_a_up_2")[0]], axis=0),
    }


def kernel(**inputs):
    import numpy as np
    import concourse.bacc as bacc
    from concourse.bass_utils import run_bass_kernel_spmd

    arrays = lay_out(inputs)
    nc = bacc.Bacc("TRN2", target_bir_lowering=False, num_devices=1)
    A = {n: nc.dram_tensor("in_" + n, a.shape, F32, kind="ExternalInput").ap() for n, a in arrays.items()}
    out = nc.dram_tensor("result", (P, DB, SEQ), F32, kind="ExternalOutput").ap()
    program(nc, A, out)
    r = run_bass_kernel_spmd(nc, [{"in_" + n: a for n, a in arrays.items()}], core_ids=[0])
    got = r.results[0]["result"]
    return np.ascontiguousarray(got.transpose(2, 1, 0)).reshape(1, SEQ, D)
```
